# Optimizing a Trainium2 kernel written in Bass

```python
import jax, jax.numpy as jnp
from jax import lax
import numpy as np
import math

D_MODEL = 1024
BATCH = 1
SEQ = 256
DEPTH = 2

CHUNK = 64
N_META = 16
EPS = 1e-6
GLA_HEADS = 4
GLA_DV = D_MODEL // 2 // GLA_HEADS
GLA_DK = GLA_DV // 2
GLA_LOWRANK = 16
GLA_TAU = 16.0
FOX_DH = 64
FOX_HEADS = D_MODEL // 2 // FOX_DH
Q_BLOCK = 128
FORGET_BIAS_INIT = 4.0
D_FF = 128 * (-(-8 * D_MODEL // (3 * 128)))
CONV_W = 3
GLA_WIDTH = GLA_HEADS * GLA_DV
FOX_WIDTH = FOX_HEADS * FOX_DH
MIX_WIDTH = GLA_WIDTH + FOX_WIDTH
IN_SIZES = (GLA_HEADS * GLA_DK, GLA_HEADS * GLA_DK, GLA_WIDTH, GLA_WIDTH, GLA_LOWRANK,
            FOX_WIDTH, FOX_WIDTH, FOX_WIDTH, FOX_HEADS)
N_IN = sum(IN_SIZES)


def rms_norm(x, g):
    xf = x.astype(jnp.float32)
    y = xf * lax.rsqrt(jnp.mean(xf * xf, axis=-1, keepdims=True) + EPS)
    return (y * g.astype(jnp.float32)).astype(x.dtype)

def chunk_kv_summary(k, v, log_a):
    log_b = jnp.cumsum(log_a, axis=3)
    log_end = log_b[:, :, :, -1:, :]
    u = jnp.einsum('bhntk,bhntv->bhnkv', k * jnp.exp(log_end - log_b), v)
    return u, jnp.exp(log_end[:, :, :, 0, :])

def gla_chunk_causal(q, k, v, log_a):
    B, L, H, _ = q.shape
    dv = v.shape[-1]
    n_chunks = (L - N_META) // CHUNK

    def split(t):
        t = jnp.transpose(t.astype(jnp.float32), (0, 2, 1, 3))
        d = t.shape[-1]
        return (t[:, :, :N_META].reshape(B, H, 1, N_META, d),
                t[:, :, N_META:].reshape(B, H, n_chunks, CHUNK, d))

    q_m, q_r = split(q)
    k_m, k_r = split(k)
    v_m, v_r = split(v)
    a_m, a_r = split(log_a)
    u_m, _ = chunk_kv_summary(k_m, v_m, a_m)
    s_meta = u_m[:, :, 0]
    u_r, decay_r = chunk_kv_summary(k_r, v_r, a_r)

    def step(s, inp):
        u_c, d_c = inp
        s = d_c[..., None] * s + u_c
        return s, s

    _, states = lax.scan(step, s_meta, (jnp.moveaxis(u_r, 2, 0), jnp.moveaxis(decay_r, 2, 0)))
    states = jnp.moveaxis(states, 0, 2)
    o_m = jnp.einsum('bhtk,bhkv->bhtv', q_m[:, :, 0], s_meta)
    o_r = jnp.einsum('bhntk,bhnkv->bhntv', q_r, states).reshape(B, H, n_chunks * CHUNK, dv)
    o = jnp.concatenate([o_m, o_r], axis=2)
    return jnp.transpose(o, (0, 2, 1, 3))

def forgetting_attention(q, k, v, log_f):
    B, L, H, dh = q.shape
    n_blk = -(-L // Q_BLOCK)
    pad = n_blk * Q_BLOCK - L
    c = jnp.cumsum(log_f.astype(jnp.float32), axis=1)
    c_k = jnp.transpose(c, (0, 2, 1))
    c_q = jnp.pad(c, ((0, 0), (0, pad), (0, 0)), mode='edge')
    q_pad = jnp.pad(q.astype(jnp.float32) * dh ** -0.5, ((0, 0), (0, pad), (0, 0), (0, 0)))
    q_blocks = jnp.moveaxis(q_pad.reshape(B, n_blk, Q_BLOCK, H, dh), 1, 0)
    c_blocks = jnp.moveaxis(jnp.transpose(c_q.reshape(B, n_blk, Q_BLOCK, H), (0, 1, 3, 2)), 1, 0)
    kf = k.astype(jnp.float32)
    vf = v.astype(jnp.float32)
    key_pos = jnp.arange(L)

    def block(inp):
        q_b, c_b, start = inp
        logits = (jnp.einsum('bqhd,bkhd->bhqk', q_b, kf)
                  + c_b[..., None] - c_k[:, :, None, :])
        q_pos = start + jnp.arange(Q_BLOCK)
        logits = jnp.where(key_pos[None, :] <= q_pos[:, None], logits, -jnp.inf)
        return jnp.einsum('bhqk,bkhd->bqhd', jax.nn.softmax(logits, axis=-1), vf)

    out = lax.map(block, (q_blocks, c_blocks, jnp.arange(n_blk) * Q_BLOCK))
    out = jnp.moveaxis(out, 0, 1).reshape(B, n_blk * Q_BLOCK, H, dh)
    return out[:, :L]

def conv_ffn(x, w_up, conv_w, conv_b, w_down):
    h = x @ w_up
    L = h.shape[1]
    hp = jnp.pad(h, ((0, 0), (CONV_W - 1, 0), (0, 0)))
    hc = conv_b
    for j in range(CONV_W):
        hc = hc + hp[:, j:j + L] * conv_w[j]
    u, g = jnp.split(hc, 2, axis=-1)
    return (jax.nn.silu(g) * u) @ w_down

def first_inputs(seed: int = 0) -> dict:
    key = jax.random.key(seed)
    ks = jax.random.split(key, 16)

    def nrm(k, shape, scale):
        return jax.random.normal(k, shape, jnp.float32) * scale

    return {
        'x': nrm(ks[0], (BATCH, SEQ, D_MODEL), 1.0),
        'meta_tokens': nrm(ks[1], (N_META, D_MODEL), 1.0),
        'attn_norm': 1.0 + nrm(ks[2], (DEPTH, D_MODEL), 0.02),
        'w_in': nrm(ks[3], (DEPTH, D_MODEL, N_IN), D_MODEL ** -0.5),
        'w_alpha_up': nrm(ks[4], (DEPTH, GLA_LOWRANK, GLA_HEADS * GLA_DK), GLA_LOWRANK ** -0.5),
        'b_alpha': nrm(ks[5], (DEPTH, GLA_HEADS * GLA_DK), 0.1),
        'b_forget': FORGET_BIAS_INIT + nrm(ks[6], (DEPTH, FOX_HEADS), 0.5),
        'gla_norm': 1.0 + nrm(ks[7], (DEPTH, GLA_WIDTH), 0.02),
        'fox_norm': 1.0 + nrm(ks[8], (DEPTH, FOX_WIDTH), 0.02),
        'w_out': nrm(ks[9], (DEPTH, MIX_WIDTH, D_MODEL), MIX_WIDTH ** -0.5),
        'ffn_norm': 1.0 + nrm(ks[10], (DEPTH, D_MODEL), 0.02),
        'w_up': nrm(ks[11], (DEPTH, D_MODEL, 2 * D_FF), D_MODEL ** -0.5),
        'conv_w': nrm(ks[12], (DEPTH, CONV_W, 2 * D_FF), CONV_W ** -0.5),
        'conv_b': nrm(ks[13], (DEPTH, 2 * D_FF), 0.02),
        'w_down': nrm(ks[14], (DEPTH, D_FF, D_MODEL), D_FF ** -0.5),
        'final_norm': 1.0 + nrm(ks[15], (D_MODEL,), 0.02),
    }

def first_block(x, meta_tokens, attn_norm, w_in, w_alpha_up, b_alpha, b_forget, gla_norm,
              fox_norm, w_out, ffn_norm, w_up, conv_w, conv_b, w_down, final_norm):
    B = x.shape[0]
    meta = jnp.broadcast_to(meta_tokens[None].astype(x.dtype), (B, N_META, D_MODEL))
    h = jnp.concatenate([meta, x], axis=1)
    L = h.shape[1]
    cuts = np.cumsum(IN_SIZES)[:-1].tolist()
    for i in range(DEPTH):
        xn = rms_norm(h, attn_norm[i])
        gq, gk, gv, gr, glr, fq, fk, fv, ff = jnp.split(xn @ w_in[i], cuts, axis=-1)
        log_a = jax.nn.log_sigmoid((glr @ w_alpha_up[i] + b_alpha[i]).astype(jnp.float32)) / GLA_TAU
        o_gla = gla_chunk_causal(gq.reshape(B, L, GLA_HEADS, GLA_DK) * GLA_DK ** -0.5,
                                 gk.reshape(B, L, GLA_HEADS, GLA_DK),
                                 gv.reshape(B, L, GLA_HEADS, GLA_DV),
                                 log_a.reshape(B, L, GLA_HEADS, GLA_DK)).astype(h.dtype)
        o_gla = rms_norm(o_gla, gla_norm[i].reshape(GLA_HEADS, GLA_DV)).reshape(B, L, GLA_WIDTH)
        o_gla = o_gla * jax.nn.silu(gr)
        log_f = jax.nn.log_sigmoid((ff + b_forget[i]).astype(jnp.float32))
        o_fox = forgetting_attention(fq.reshape(B, L, FOX_HEADS, FOX_DH),
                                     fk.reshape(B, L, FOX_HEADS, FOX_DH),
                                     fv.reshape(B, L, FOX_HEADS, FOX_DH), log_f).astype(h.dtype)
        o_fox = rms_norm(o_fox, fox_norm[i].reshape(FOX_HEADS, FOX_DH)).reshape(B, L, FOX_WIDTH)
        h = h + jnp.concatenate([o_gla, o_fox], axis=-1) @ w_out[i]
        h = h + conv_ffn(rms_norm(h, ffn_norm[i]), w_up[i], conv_w[i], conv_b[i], w_down[i])
    return rms_norm(h, final_norm)[:, N_META:]


DEPTH_2 = 1

ATTN_HEADS = 8
ATTN_KV_HEADS = 2
ATTN_HEAD_DIM = 64
Q_PER_KV = ATTN_HEADS // ATTN_KV_HEADS
WINDOW = 128
ATTN_BLOCK = WINDOW
ATTN_WIDTH = ATTN_HEADS * ATTN_HEAD_DIM
KV_WIDTH = ATTN_KV_HEADS * ATTN_HEAD_DIM
HGRN_HEADS = 4
HGRN_KEY_DIM = 128
HGRN_VAL_DIM = 128
HGRN_WIDTH = HGRN_HEADS * HGRN_VAL_DIM
HGRN_KEY_WIDTH = HGRN_HEADS * HGRN_KEY_DIM
HGRN_CHUNK = 32
MIX_WIDTH_2 = ATTN_WIDTH + HGRN_WIDTH
IN_SPLITS = [ATTN_WIDTH, KV_WIDTH, KV_WIDTH, HGRN_KEY_WIDTH, HGRN_KEY_WIDTH, HGRN_WIDTH, HGRN_WIDTH]
IN_WIDTH = sum(IN_SPLITS)
N_GROUPS = 4
EXPERTS_PER_GROUP = 8
N_EXPERTS = N_GROUPS * EXPERTS_PER_GROUP
TOP_K = 2
EXPERT_FF = D_MODEL // 4

NORM_EPS = 1e-6
NEG_INF = -1e30


def rmsnorm(x, g):
    xf = x.astype(jnp.float32)
    y = xf * lax.rsqrt(jnp.mean(xf * xf, axis=-1, keepdims=True) + NORM_EPS)
    return (y * g.astype(jnp.float32)).astype(x.dtype)

def swa_sink_alibi(q, k, v, sinks):
    B, T, _ = q.shape
    NB = T // ATTN_BLOCK
    qb = q.reshape(B, NB, ATTN_BLOCK, ATTN_KV_HEADS, Q_PER_KV, ATTN_HEAD_DIM)
    pad = ((0, 0), (ATTN_BLOCK, 0), (0, 0))
    kp = jnp.pad(k, pad).reshape(B, NB + 1, ATTN_BLOCK, ATTN_KV_HEADS, ATTN_HEAD_DIM)
    vp = jnp.pad(v, pad).reshape(B, NB + 1, ATTN_BLOCK, ATTN_KV_HEADS, ATTN_HEAD_DIM)
    kb = jnp.concatenate([kp[:, :-1], kp[:, 1:]], axis=2)
    vb = jnp.concatenate([vp[:, :-1], vp[:, 1:]], axis=2)
    scale = 1.0 / math.sqrt(ATTN_HEAD_DIM)
    s = jnp.einsum('bnqgrd,bnkgd->bngrqk', qb, kb, preferred_element_type=jnp.float32) * scale
    qi = jnp.arange(ATTN_BLOCK)[:, None]
    kj = jnp.arange(2 * ATTN_BLOCK)[None, :]
    dist = qi + ATTN_BLOCK - kj
    in_win = (dist >= 0) & (dist < WINDOW)
    not_pad = (jnp.arange(NB)[:, None, None] > 0) | (kj >= ATTN_BLOCK)[None]
    valid = in_win[None] & not_pad
    slopes = jnp.exp2(-8.0 * (jnp.arange(ATTN_HEADS, dtype=jnp.float32) + 1.0) / ATTN_HEADS)
    slopes = slopes.reshape(ATTN_KV_HEADS, Q_PER_KV)[:, :, None, None]
    s = s - slopes * dist.astype(jnp.float32)
    s = jnp.where(valid[None, :, None, None], s, NEG_INF)
    sink = sinks.astype(jnp.float32).reshape(ATTN_KV_HEADS, Q_PER_KV)[:, :, None, None]
    m = jnp.maximum(jnp.max(s, axis=-1, keepdims=True), sink)
    p = jnp.exp(s - m)
    p = p / (jnp.sum(p, axis=-1, keepdims=True) + jnp.exp(sink - m))
    o = jnp.einsum('bngrqk,bnkgd->bnqgrd', p.astype(v.dtype), vb)
    return o.reshape(B, T, ATTN_WIDTH)

def hgrn2(q_raw, f_raw, i_raw, lb):
    B, T, _ = q_raw.shape
    NC = T // HGRN_CHUNK
    shp_k = (B, NC, HGRN_CHUNK, HGRN_HEADS, HGRN_KEY_DIM)
    q = jax.nn.silu(q_raw.astype(jnp.float32)).reshape(shp_k)
    lbf = lb.astype(jnp.float32)
    f = lbf + (1.0 - lbf) * jax.nn.sigmoid(f_raw.astype(jnp.float32))
    k = (1.0 - f).reshape(shp_k)
    logf = jnp.log(f).reshape(shp_k)
    v = i_raw.astype(jnp.float32).reshape(B, NC, HGRN_CHUNK, HGRN_HEADS, HGRN_VAL_DIM)
    b = jnp.cumsum(logf, axis=2)
    b_last = b[:, :, -1:]
    q_dec = q * jnp.exp(b)
    k_dec = k * jnp.exp(-b)
    k_end = k * jnp.exp(b_last - b)
    causal = jnp.tril(jnp.ones((HGRN_CHUNK, HGRN_CHUNK), dtype=bool))
    a = jnp.einsum('bnchk,bnshk->bnhcs', q_dec, k_dec)
    a = jnp.where(causal, a, 0.0)
    o_intra = jnp.einsum('bnhcs,bnshv->bnchv', a, v)

    def step(S, inp):
        qd, ke, vv, decay = inp
        o = jnp.einsum('bchk,bhkv->bchv', qd, S)
        S = S * decay[..., None] + jnp.einsum('bchk,bchv->bhkv', ke, vv)
        return S, o

    S0 = jnp.zeros((B, HGRN_HEADS, HGRN_KEY_DIM, HGRN_VAL_DIM), jnp.float32)
    xs = (jnp.moveaxis(q_dec, 1, 0), jnp.moveaxis(k_end, 1, 0), jnp.moveaxis(v, 1, 0),
          jnp.moveaxis(jnp.exp(b_last[:, :, 0]), 1, 0))
    _, o_inter = lax.scan(step, S0, xs)
    o = o_intra + jnp.moveaxis(o_inter, 0, 1)
    return o.reshape(B, T, HGRN_HEADS, HGRN_VAL_DIM).astype(q_raw.dtype)

def hierarchical_moe(h, w_rg, b_rg, w_re, b_re, w_gate, w_up, w_down):
    B, T, D = h.shape
    tok = h.reshape(-1, D)
    N = tok.shape[0]
    g_prob = jax.nn.softmax((tok @ w_rg + b_rg).astype(jnp.float32), axis=-1)
    g_w, g_idx = lax.top_k(g_prob, 1)
    e_logits = (tok @ w_re + b_re).astype(jnp.float32).reshape(N, N_GROUPS, EXPERTS_PER_GROUP)
    e_sel = e_logits[jnp.arange(N), g_idx[:, 0]]
    e_w, e_idx = lax.top_k(jax.nn.softmax(e_sel, axis=-1), TOP_K)
    e_w = e_w / jnp.sum(e_w, axis=-1, keepdims=True)
    weights = (g_w * e_w).astype(h.dtype)
    expert = (g_idx * EXPERTS_PER_GROUP + e_idx).reshape(-1)
    order = jnp.argsort(expert)
    inv = jnp.argsort(order)
    xs = tok[order // TOP_K]
    sizes = jnp.bincount(expert, length=N_EXPERTS).astype(jnp.int32)
    hg = lax.ragged_dot(xs, w_gate, sizes)
    hu = lax.ragged_dot(xs, w_up, sizes)
    ys = lax.ragged_dot(jax.nn.silu(hg) * hu, w_down, sizes)
    ys = ys[inv].reshape(N, TOP_K, D)
    out = jnp.einsum('nkd,nk->nd', ys, weights)
    return out.reshape(B, T, D)

def second_inputs(seed: int = 0) -> dict:
    key = jax.random.key(seed)
    ks = jax.random.split(key, 24)
    f32 = jnp.float32
    L, D = DEPTH_2, D_MODEL

    def nrm(k, shape, scale):
        return jax.random.normal(k, shape, f32) * scale

    return {
        "x": nrm(ks[0], (BATCH, SEQ, D), 1.0),
        "c": nrm(ks[1], (BATCH, D), 1.0),
        "ln1_pre": 1.0 + nrm(ks[2], (L, D), 0.02),
        "ln1_post": 1.0 + nrm(ks[3], (L, D), 0.02),
        "ln2_pre": 1.0 + nrm(ks[4], (L, D), 0.02),
        "ln2_post": 1.0 + nrm(ks[5], (L, D), 0.02),
        "w_ada": nrm(ks[6], (L, D, 6 * D), 0.25 * D ** -0.5),
        "b_ada": nrm(ks[7], (L, 6 * D), 0.01),
        "w_in": nrm(ks[8], (L, D, IN_WIDTH), D ** -0.5),
        "attn_sinks": nrm(ks[9], (L, ATTN_HEADS), 0.5),
        "attn_out_norm": 1.0 + nrm(ks[10], (L, ATTN_WIDTH), 0.02),
        "hgrn_lb": nrm(ks[11], (L + 1, HGRN_KEY_WIDTH), 0.1),
        "hgrn_out_norm": 1.0 + nrm(ks[12], (L, HGRN_WIDTH), 0.02),
        "w_out": nrm(ks[13], (L, MIX_WIDTH_2, D), MIX_WIDTH_2 ** -0.5),
        "w_router_group": nrm(ks[14], (L, D, N_GROUPS), D ** -0.5),
        "b_router_group": nrm(ks[15], (L, N_GROUPS), 0.01),
        "w_router_expert": nrm(ks[16], (L, D, N_EXPERTS), D ** -0.5),
        "b_router_expert": nrm(ks[17], (L, N_EXPERTS), 0.01),
        "w_exp_gate": nrm(ks[18], (L, N_EXPERTS, D, EXPERT_FF), D ** -0.5),
        "w_exp_up": nrm(ks[19], (L, N_EXPERTS, D, EXPERT_FF), D ** -0.5),
        "w_exp_down": nrm(ks[20], (L, N_EXPERTS, EXPERT_FF, D), EXPERT_FF ** -0.5),
    }

def second_block(x, c, ln1_pre, ln1_post, ln2_pre, ln2_post, w_ada, b_ada, w_in, attn_sinks,
              attn_out_norm, hgrn_lb, hgrn_out_norm, w_out, w_router_group, b_router_group,
              w_router_expert, b_router_expert, w_exp_gate, w_exp_up, w_exp_down):
    B, T, D = x.shape
    lb_all = jnp.cumsum(jax.nn.softmax(hgrn_lb.astype(jnp.float32), axis=0), axis=0)
    offsets = list(np.cumsum(IN_SPLITS)[:-1])
    c_act = jax.nn.silu(c)
    for l in range(DEPTH_2):
        mod = (c_act @ w_ada[l] + b_ada[l])[:, None, :]
        sh1, sc1, ga1, sh2, sc2, ga2 = jnp.split(mod, 6, axis=-1)
        h = rmsnorm(x, ln1_pre[l]) * (1.0 + sc1) + sh1
        proj = h @ w_in[l]
        q_a, k_a, v_a, q_h, f_h, i_h, g_h = jnp.split(proj, offsets, axis=-1)
        attn = rmsnorm(swa_sink_alibi(q_a, k_a, v_a, attn_sinks[l]), attn_out_norm[l])
        hg = hgrn2(q_h, f_h, i_h, lb_all[l])
        hg = rmsnorm(hg, hgrn_out_norm[l].reshape(HGRN_HEADS, HGRN_VAL_DIM)).reshape(B, T, HGRN_WIDTH)
        hg = hg * jax.nn.silu(g_h)
        mix = jnp.concatenate([attn, hg], axis=-1) @ w_out[l]
        x = x + ga1 * rmsnorm(mix, ln1_post[l])
        h = rmsnorm(x, ln2_pre[l]) * (1.0 + sc2) + sh2
        y = hierarchical_moe(h, w_router_group[l], b_router_group[l], w_router_expert[l],
                             b_router_expert[l], w_exp_gate[l], w_exp_up[l], w_exp_down[l])
        x = x + ga2 * rmsnorm(y, ln2_post[l])
    return x


def setup_inputs(seed=0):
    out = dict(first_inputs(seed))
    for name, value in second_inputs(seed + 1).items():
        if name != "x":
            out[name + "_2"] = value
    return out


def reference(
    x, meta_tokens, attn_norm, w_in, w_alpha_up, b_alpha, b_forget, gla_norm, fox_norm, w_out,
    ffn_norm, w_up, conv_w, conv_b, w_down, final_norm, c_2, ln1_pre_2, ln1_post_2, ln2_pre_2,
    ln2_post_2, w_ada_2, b_ada_2, w_in_2, attn_sinks_2, attn_out_norm_2, hgrn_lb_2,
    hgrn_out_norm_2, w_out_2, w_router_group_2, b_router_group_2, w_router_expert_2,
    b_router_expert_2, w_exp_gate_2, w_exp_up_2, w_exp_down_2,
):
    x = first_block(
        x, meta_tokens, attn_norm, w_in, w_alpha_up, b_alpha, b_forget, gla_norm, fox_norm,
        w_out, ffn_norm, w_up, conv_w, conv_b, w_down, final_norm,
    )
    return second_block(
        x, c_2, ln1_pre_2, ln1_post_2, ln2_pre_2, ln2_post_2, w_ada_2, b_ada_2, w_in_2,
        attn_sinks_2, attn_out_norm_2, hgrn_lb_2, hgrn_out_norm_2, w_out_2, w_router_group_2,
        b_router_group_2, w_router_expert_2, b_router_expert_2, w_exp_gate_2, w_exp_up_2,
        w_exp_down_2,
    )


_drawn_inputs = setup_inputs


def setup_inputs(seed=0):
    import zlib

    import numpy as np

    out = dict(_drawn_inputs(seed))
    spreads = {}
    factors = {'gla_norm': 2.797,
     'ln1_pre_2': 4.45,
     'ln1_post_2': 8.0,
     'ln2_post_2': 36.013,
     'attn_sinks_2': 21.648,
     'attn_out_norm_2': 5.398,
     'hgrn_lb_2': 8.0,
     'hgrn_out_norm_2': 8.0,
     'b_router_group_2': 3.673,
     'b_router_expert_2': 6.757}
    for name, (base, spread) in spreads.items():
        noise = np.random.default_rng([zlib.crc32(name.encode()), seed]).standard_normal(out[name].shape)
        drawn = base * np.exp(spread * noise) if base else spread * noise
        out[name] = __import__('jax').numpy.asarray(drawn.astype(out[name].dtype))
    for name, factor in factors.items():
        out[name] = (out[name] * factor).astype(out[name].dtype)
    return out
```

```python
from contextlib import ExitStack

import concourse.bass as bass
from concourse import mybir

F32 = mybir.dt.float32
F32R = mybir.dt.float32r
BF16 = mybir.dt.bfloat16
I32 = mybir.dt.int32
U32 = mybir.dt.uint32
ALU = mybir.AluOpType
ACT = mybir.ActivationFunctionType
AX_X = mybir.AxisListType.X

P = 128
DEPTH = 2
META = 16
T = 272
T2 = 256
D = 1024
KT = D // P
EPS = 1e-6
DFF = 2816
FT = DFF // P
FOX_H = 8
TOK = [(0, META), (META, P), (META + P, P)]
GLA_CHUNKS = [(0, 0, META), (1, 0, 64), (1, 64, 64), (2, 0, 64), (2, 64, 64)]
ATT_H = 8
HG_H = 4
HG_C = 32
NEXP = 32
GLA_BANK = [2, 3, 5, 6]
FOX_BANK = [0, 1, 4]
HG_BANK = [4, 5, 6, 3]
HEADS = [0, 4, 1, 5, 2, 6, 3, 7]
CW = 256
RAW = 4
SPLIT = 2
BIG = 1.0e30
IN_AT = {"gq": 0, "gk": 256, "gv": 512, "gr": 1024, "glr": 1536, "fq": 1552, "fk": 2064, "fv": 2576, "ff": 3088}
IN_ORDER = [("gk", 0), ("gv", 0), ("gv", 1), ("gq", 0), ("gr", 0), ("gr", 1),
            ("fv", 0), ("fv", 1), ("fk", 0), ("fk", 1), ("fq", 0), ("fq", 1)]
IN2_AT = {"qa": 0, "ka": 512, "qh": 768, "fh": 1280, "ih": 1792, "gh": 2304}
IN2_ORDER = [("fh", 0), ("fh", 1), ("ih", 0), ("ih", 1), ("qh", 0), ("qh", 1), ("gh", 0), ("gh", 1),
             ("ka", 0), ("qa", 0), ("qa", 1)]
DOWN_K = [(0, 8), (8, 7), (15, 7)]

ROWS = {}


def _rows():
    at = 0
    for name, n in (("conv_w", 3 * DEPTH * 2 * FT), ("conv_b", DEPTH * 2 * FT), ("attn_norm", 16), ("ffn_norm", 16),
                    ("gla_norm", 8), ("fox_norm", 8), ("final_norm", 8), ("c", 8), ("ln1_pre", 8), ("ln1_post", 8),
                    ("ln2_pre", 8), ("ln2_post", 8), ("b_ada", 48), ("attn_out_norm", 4), ("hgrn_lb", 8),
                    ("hgrn_out_norm", 4)):
        ROWS[name] = (at, n)
        at += n
    return at


NROWS = _rows()
RBLK = -(-NROWS // P)


def gemm_groups():
    out = []
    for l in range(DEPTH):
        out += [("in", l, i) for i in range(len(IN_ORDER))]
        out += [("out", l, i) for i in range(4)]
        out += [("up", l, i) for i in range(FT)]
        out += [("down", l, i) for i in range(4)]
    out += [("in2", 0, i) for i in range(len(IN2_ORDER))]
    out += [("out2", 0, i) for i in range(4)]
    return out


GROUPS = gemm_groups()


def chunk_list():
    out = []
    for g in GROUPS:
        out += [(g, j) for j in range(3 if g[0] == "down" else 1)]
    for e in range(NEXP):
        out += [(("gate", 0, e), 0), (("upx", 0, e), 0), (("dn", 0, e), 0)]
    return out


CHUNKS = chunk_list()
CHUNK_NO = {c: n for n, c in enumerate(CHUNKS)}


class Signal:

    def __init__(self, sem, order, known):
        self.sem, self.order, self.known = sem, order, known

    @staticmethod
    def flat(key):
        return sum((Signal.flat(k) if isinstance(k, tuple) else (k,) for k in key), ())

    def event(self, *key):
        self.order.append(self.flat(key))
        return 1

    def after(self, *key):
        return 1 if self.known is None else self.known[self.flat(key)] + 1


def build(nc, A, out, known):
    orders = {}
    with ExitStack() as ctx:
        def sem(name):
            return ctx.enter_context(nc.semaphore(name))

        def signal(name):
            orders[name] = []
            numbers = None if known is None else {k: n for n, k in enumerate(known[name])}
            return Signal(sem("s_" + name), orders[name], numbers)

        top = [-(-nc.sbuf_base // 64) * 64]

        def sb(name, shape, dt=F32, at=None):
            n = 2 if dt == BF16 else 4
            for s in shape[1:]:
                n *= s
            if at is None:
                off, top[0] = top[0], top[0] + -(-n // 32) * 32
            else:
                off, at[0] = at[0], at[0] + -(-n // 32) * 32
                assert at[0] <= at[1], name
            return nc.alloc_sbuf_tensor_at(name, list(shape), dt, offset=off)

        raw = [sb(f"raw{i}", [P, 8, CW]) for i in range(RAW)]
        whi = [sb(f"whi{i}", [P, 8, CW], F32R) for i in range(SPLIT)]
        wlo = [sb(f"wlo{i}", [P, 8, CW], F32R) for i in range(SPLIT)]
        ada_at = top[0]
        ada = [sb(f"ada{i}", [P, 8, CW]) for i in range(2)]
        XT, XN = sb("XT", [P, KT, T]), sb("XN", [P, KT, T])
        xhi, xlo = sb("xhi", [P, KT, T], F32R), sb("xlo", [P, KT, T], F32R)
        mix_at = top[0]
        hhi, hlo = sb("hhi", [P, FT, T], F32R), sb("hlo", [P, FT, T], F32R)
        mix_end = top[0]
        sq = sb("sq", [P, 4, T])
        rs = sb("rs", [P, 2, T])
        ident, ones_1 = sb("ident", [P, P]), sb("ones_1", [P, P])
        ones_d, ones_v, ones_a, ones_f = (sb(n, [P, P]) for n in ("ones_d", "ones_v", "ones_a", "ones_f"))
        after = sb("after", [P, P])
        half = sb("half", [P, 2])
        identb, causal = sb("identb", [P, P], BF16), sb("causal", [P, P], BF16)
        same_c = sb("same_c", [P, P])
        restart = sb("restart", [P, T2])
        onesrow = sb("onesrow", [8, T])
        slope_i = sb("slope_i", [P, ATT_H, P], BF16)
        dist = sb("dist", [P, 2 * P], BF16)
        iota8 = sb("iota8", [P, 8])
        PC = sb("PC", [P, RBLK * P])
        wsm = sb("wsm", [P, DEPTH, KT, 24])
        wa1 = sb("wa1", [17, DEPTH, 256])
        bfo = sb("bfo", [8, DEPTH])
        wr = sb("wr", [P, KT, 36])
        rows44 = sb("rows44", [1, 44])
        bc44 = sb("bc44", [P, 44])
        epst = sb("epst", [P, 1])
        mod = sb("mod", [P, 48])
        gsc = sb("gsc", [P, 4, KT])
        cact = sb("cact", [P, KT])
        lbt = sb("lbt", [P, 5, 8])
        adr = sb("adr", [P, 2, CW])
        cv = sb("cv", [P, 2, 2, T])
        hf = sb("hf", [P, 2, T])
        glr1 = sb("glr1", [17, T])
        fz, fl, negc = sb("fz", [8, T]), sb("fl", [8, T]), sb("negc", [8, T])
        nmx, psm, pri = sb("nmx", [P, 24]), sb("psm", [P, 24]), sb("pri", [P, 24])
        keT, kdT = sb("keT", [P, HG_H, T2]), sb("kdT", [P, HG_H, T2])
        assert top[0] <= nc.sbuf_usable_end

        m = [mix_at, mix_end]
        gkt, gvt, fvt = sb("gkt", [P, 3, 256], at=m), sb("gvt", [P, 3, 512], at=m), sb("fvt", [P, 3, 512], at=m)
        gqT, grT = sb("gqT", [P, 2, T], at=m), sb("grT", [P, 4, T], at=m)
        fqT, fkT = sb("fqT", [P, 4, T], at=m), sb("fkT", [P, 4, T], at=m)
        rest = m[0]
        Pq, PTs, PTm = sb("Pq", [P, 2, 3, T], at=m), sb("PTs", [P, 2, 384], at=m), sb("PTm", [META, 2, T], at=m)
        m = [rest, mix_end]
        la, kd, ST = sb("la", [P, 3, 256], at=m), sb("kd", [P, 3, 256], at=m), sb("ST", [P, 2, 5, P], at=m)
        dec = sb("dec", [P, 8], at=m)
        m = [mix_at, mix_end]
        xs, prm = sb("xs", [P, 3, D], at=m), sb("prm", [P, RBLK, P], at=m)
        m = [mix_at, mix_end]
        qh, fh, gh, kh = (sb(n, [P, HG_H, T2], at=m) for n in ("qh", "fh", "gh", "kh"))
        bb, ih = sb("bb", [P, HG_H, T2], at=m), sb("ih", [P, 2, 512], at=m)
        qaT, kaT, vaT = sb("qaT", [P, 4, T2], at=m), sb("kaT", [P, T2], at=m), sb("vaT", [P, T2], at=m)
        ke, At, va = sb("ke", [P, 2, HG_H, P], at=m), sb("At", [P, 2, HG_H, P], at=m), sb("va", [P, 2, P], at=m)
        P2, PT2 = sb("P2", [P, 2, 384], at=m), sb("PT2", [P, 2, 384], at=m)
        m = [ada_at, ada_at + 2 * 8 * CW * 4]
        SS = sb("SS", [P, 7, HG_H, P], at=m)
        m = [mix_at, mix_end]
        rt = sb("rt", [P, 2, 160], at=m)
        wt = sb("wt", [P, 2, NEXP], at=m)
        WT = sb("WT", [NEXP, T2], at=m)
        sg, hu = sb("sg", [P, 2, 512], at=m), sb("hu", [P, 2, 512], at=m)
        huh, hul = sb("huh", [P, 2, 512], F32R, at=m), sb("hul", [P, 2, 512], F32R, at=m)
        OB = sb("OB", [P, 2, D], at=m)

        ps = [ctx.enter_context(nc.psum_tensor(f"ps{i}", [P, 512], F32)) for i in range(8)]
        SUM = ps[7][:, 64:64 + T]

        s_raw = [sem(f"s_raw{i}") for i in range(RAW)]
        s_ada = [sem(f"s_ada{i}") for i in range(2)]
        s_x = sem("s_x")
        s_prm = sem("s_prm")
        s_small = sem("s_small")
        s_out = sem("s_out")

        s_xt = signal("xt")
        s_convolved = signal("convolved")
        s_mixout = signal("mixout")
        s_normed = signal("normed")
        s_scaled = signal("scaled")
        s_mixed = signal("mixed")
        s_scaled_n = signal("scaled_n")
        s_scaled2 = signal("scaled2")
        s_mixed2 = signal("mixed2")
        s_post = signal("post")
        s_averaged = signal("averaged")
        s_logged = signal("logged")
        s_squared = signal("squared")
        s_w_used = signal("w_used")
        s_w_hi = signal("w_hi")
        s_x_hi = signal("x_hi")
        s_w_lo = signal("w_lo")
        s_x_lo = signal("x_lo")
        s_h_lo = signal("h_lo")
        s_ada_sum = signal("ada_sum")
        s_turned_back = signal("turned_back")
        s_filled = signal("filled")
        s_consts = signal("consts")
        s_ada_mul = signal("ada_mul")
        s_ada_four = signal("ada_four")
        s_ada_two = signal("ada_two")
        s_ada_used = signal("ada_used")
        s_cact = signal("cact")
        s_gated = signal("gated")
        s_params = signal("params")
        s_fz = signal("fz")
        s_fl1 = signal("fl1")
        s_fl2 = signal("fl2")
        s_z = signal("z")
        s_gla_d = signal("gla_d")
        s_gla_o = signal("gla_o")
        s_nmax = signal("nmax")
        s_turned = signal("turned")
        s_pv = signal("pv")
        s_fox_o = signal("fox_o")
        s_hidden = signal("hidden")
        s_lb_sub = signal("lb_sub")
        s_forget = signal("forget")
        s_cum = signal("cum")
        s_end_sub = signal("end_sub")
        s_hg_o = signal("hg_o")
        s_nmax2 = signal("nmax2")
        s_turned2 = signal("turned2")
        s_pv2 = signal("pv2")
        s_att_o = signal("att_o")
        s_r_sub = signal("r_sub")
        s_hu = signal("hu")
        s_y = signal("y")
        s_rooted = signal("rooted")
        s_prm_turned = signal("prm_turned")
        s_x_turned = signal("x_turned")
        s_bc = signal("bc")
        s_small_ff = signal("small_ff")
        s_small_glr = signal("small_glr")
        s_fl3 = signal("fl3")
        s_lf = signal("lf")
        s_zc = signal("zc")
        s_gla_e = signal("gla_e")
        s_gla_u = signal("gla_u")
        s_state = signal("state")
        s_scores = signal("scores")
        s_pexp = signal("pexp")
        s_recip = signal("recip")
        s_tap2 = signal("tap2")
        s_tap1 = signal("tap1")
        s_h_hi = signal("h_hi")
        s_mod = signal("mod")
        s_lb_max = signal("lb_max")
        s_gsc = signal("gsc")
        s_lb_exp = signal("lb_exp")
        s_lb_sum = signal("lb_sum")
        s_lb_rec = signal("lb_rec")
        s_lb = signal("lb")
        s_lb1 = signal("lb1")
        s_lb2 = signal("lb2")
        s_drained_act = signal("drained_act")
        s_kh = signal("kh")
        s_logf = signal("logf")
        s_exp_b = signal("exp_b")
        s_exp_nb = signal("exp_nb")
        s_exp_end = signal("exp_end")
        s_ke_turned = signal("ke_turned")
        s_intra = signal("intra")
        s_va_turned = signal("va_turned")
        s_hg_u = signal("hg_u")
        s_hg_s = signal("hg_s")
        s_bc44 = signal("bc44")
        s_scores2 = signal("scores2")
        s_nmaxa = signal("nmaxa")
        s_pexp2 = signal("pexp2")
        s_den2 = signal("den2")
        s_rec2 = signal("rec2")
        s_routed = signal("routed")
        s_r = signal("r")
        s_r_exp = signal("r_exp")
        s_wt_turned = signal("wt_turned")
        s_e_gate = signal("e_gate")
        s_weighed = signal("weighed")
        s_sgw = signal("sgw")
        s_hu_lo = signal("hu_lo")
        s_hu_hi = signal("hu_hi")
        s_out_turned = signal("out_turned")
        s_glr = signal("glr")
        s_la = signal("la")
        s_kd = signal("kd")
        s_negc = signal("negc")
        s_pt_copied = signal("pt_copied")
        s_ptm_copied = signal("ptm_copied")
        s_prob = signal("prob")
        s_ke = signal("ke")
        s_ke_copied = signal("ke_copied")
        s_va = signal("va")
        s_a_copied = signal("a_copied")
        s_pt2 = signal("pt2")
        s_prob2 = signal("prob2")
        s_wt = signal("wt")
        s_WT = signal("WT")
        s_drained_dve = signal("drained_dve")
        s_qd = signal("qd")
        s_kd2 = signal("kd2")
        s_za = signal("za")
        s_zb = signal("zb")

        def col(name, i, n=1):
            a = ROWS[name][0] + i
            return PC[:, a:a + n]

        def pair(g):
            return 2 * (GROUPS.index(g) % 3)

        ACT_DRAINS = {"gv", "gr", "fv", "fq", "fh", "qh", "gh", "ka"}

        def drained(eng, g):
            kind, l, i = g
            if kind in ("out", "down"):
                eng.wait_ge(s_xt.sem, s_xt.after("o" if kind == "out" else "d", l, 2 * i + 1))
            elif kind == "up":
                eng.wait_ge(s_convolved.sem, s_convolved.after(l, i))
            elif kind == "out2":
                eng.wait_ge(s_mixout.sem, s_mixout.after(2 * i + 1))
            else:
                name = (IN_ORDER if kind == "in" else IN2_ORDER)[i][0]
                if name in ACT_DRAINS:
                    eng.wait_ge(s_drained_act.sem, s_drained_act.after(g))
                else:
                    eng.wait_ge(s_drained_dve.sem, s_drained_dve.after(g))

        def root_read(eng, key):
            kind = key[0]
            if kind in ("n1", "n2"):
                eng.wait_ge(s_normed.sem, s_normed.after(key, KT - 1))
            elif kind == "g":
                eng.wait_ge(s_scaled.sem, s_scaled.after(key[1:]))
            elif kind == "f":
                eng.wait_ge(s_mixed.sem, s_mixed.after(key[1], 4 + key[2]))
            elif kind == "nf":
                eng.wait_ge(s_xt.sem, s_xt.after("f", KT - 1))
            elif kind in ("n3", "n5"):
                eng.wait_ge(s_scaled_n.sem, s_scaled_n.after(key, KT - 1))
            elif kind == "h":
                eng.wait_ge(s_scaled2.sem, s_scaled2.after(key[1]))
            elif kind == "att":
                eng.wait_ge(s_mixed2.sem, s_mixed2.after(3))
            else:
                eng.wait_ge(s_post.sem, s_post.after(key, KT - 1))

        def kp(w):
            return w.rearrange("(k p) n -> p k n", p=P)

        def pieces(n):
            (kind, l, i), j = CHUNKS[n]
            dst = raw[n % RAW]
            if kind == "in":
                name, h = IN_ORDER[i]
                c0 = IN_AT[name] + CW * h
                return [(dst[:, :, :], kp(A["w_in"][l])[:, :, c0:c0 + CW])]
            if kind == "out":
                return [(dst[:, :, :], kp(A["w_out"][l])[:, :, CW * i:CW * (i + 1)])]
            if kind == "up":
                w = kp(A["w_up"][l])
                return [(dst[:, :, P * h:P * (h + 1)], w[:, :, DFF * h + P * i:DFF * h + P * (i + 1)]) for h in range(2)]
            if kind == "down":
                k0, nk = DOWN_K[j]
                return [(dst[:, 0:nk, :], kp(A["w_down"][l])[:, k0:k0 + nk, CW * i:CW * (i + 1)])]
            if kind == "in2":
                name, h = IN2_ORDER[i]
                w = A["w_in_2"][0]
                if name == "qa":
                    v = w[:, 0:512].rearrange("(k p) (g t d) -> p k g t d", p=P, g=2, d=64)
                    return [(dst[:, :, P * t + 64 * g:P * t + 64 * g + 64], v[:, :, g, 2 * h + t, :])
                            for t in range(2) for g in range(2)]
                c0 = IN2_AT[name] + CW * h
                return [(dst[:, :, :], kp(w)[:, :, c0:c0 + CW])]
            if kind == "out2":
                cs = slice(CW * i, CW * (i + 1))
                w = A["w_out_2"][0]
                v = w[0:512, cs].rearrange("(g t d) n -> g d t n", g=2, d=64)
                return [(dst[64 * g:64 * g + 64, 0:4, :], v[g]) for g in range(2)] + \
                       [(dst[:, 4:8, :], kp(w)[:, 4:8, cs])]
            if kind == "dn":
                flat = dst[:, :, :].rearrange("p a b -> p (a b)").rearrange("p (k n) -> p k n", k=2)
                return [(flat, kp(A["w_exp_down_2"][0, i]))]
            w = A["w_exp_gate_2" if kind == "gate" else "w_exp_up_2"]
            return [(dst[:, :, :], kp(w[0, i]))]

        landed_at, total = [], [0] * RAW
        for n in range(len(CHUNKS)):
            total[n % RAW] += 16 * len(pieces(n))
            landed_at.append(total[n % RAW])

        def k_tiles(n):
            (kind, _, _), j = CHUNKS[n]
            return DOWN_K[j][1] if kind == "down" else 8


        def v2(name):
            return A[name].rearrange("l (a p) -> (l a) p", p=P)

        row_srcs = [("conv_w", A["conv_w"].rearrange("l j (a p) -> (l j a) p", p=P)), ("conv_b", v2("conv_b")),
                    ("attn_norm", v2("attn_norm")), ("ffn_norm", v2("ffn_norm")), ("gla_norm", v2("gla_norm")),
                    ("fox_norm", v2("fox_norm")), ("final_norm", A["final_norm"].rearrange("(a p) -> a p", p=P)),
                    ("c", v2("c_2"))] + [(nm, v2(nm + "_2")) for nm in
                    ("ln1_pre", "ln1_post", "ln2_pre", "ln2_post", "b_ada", "hgrn_lb", "hgrn_out_norm")]
        row_dmas = []
        for name, src in row_srcs:
            at, cnt = ROWS[name]
            done = 0
            while done < cnt:
                b, r = divmod(at + done, P)
                k = min(cnt - done, P - r)
                row_dmas.append((prm[r:r + k, b, :], src[done:done + k, :]))
                done += k
        b0, r0 = divmod(ROWS["attn_out_norm"][0], P)
        aon = A["attn_out_norm_2"].rearrange("l (g j d) -> (l g) j d", g=2, d=64)
        row_dmas += [(prm[r0:r0 + 4, b0, 64 * g:64 * g + 64], aon[g]) for g in range(2)]
        PRM_ALL = 16 * len(row_dmas)
        small_dmas = []
        for l in range(DEPTH):
            wv = kp(A["w_in"][l])
            small_dmas += [(wsm[:, l, :, 0:16], wv[:, :, IN_AT["glr"]:IN_AT["glr"] + 16]),
                           (wsm[:, l, :, 16:24], wv[:, :, IN_AT["ff"]:IN_AT["ff"] + 8]),
                           (wa1[0:16, l, :], A["w_alpha_up"][l]), (wa1[16:17, l, :], A["b_alpha"][l:l + 1, :]),
                           (bfo[:, l:l + 1], A["b_forget"][l:l + 1, :].rearrange("l h -> h l"))]
        small_dmas += [(wr[:, :, 0:4], kp(A["w_router_group_2"][0])), (wr[:, :, 4:36], kp(A["w_router_expert_2"][0])),
                       (rows44[:, 0:4], A["b_router_group_2"]), (rows44[:, 4:36], A["b_router_expert_2"]),
                       (rows44[:, 36:44], A["attn_sinks_2"])]
        SMALL_ALL = 16 * len(small_dmas)


        STATS = []
        for l in range(DEPTH):
            STATS += [(("n1", l), KT, ones_d, T)]
            STATS += [(("g", l, h), 1, ones_v, T) for h in range(4)] + [(("f", l, j), 1, ones_f, T) for j in range(4)]
            STATS += [(("n2", l), KT, ones_d, T)]
        STATS += [(("nf",), KT, ones_d, T2), (("n3",), KT, ones_d, T2)]
        STATS += [(("h", h), 1, ones_v, T2) for h in range(HG_H)]
        STATS += [(("att",), 4, ones_a, T2), (("n4",), KT, ones_d, T2), (("n5",), KT, ones_d, T2), (("n6",), KT, ones_d, T2)]
        STAT_NO = {s[0]: n for n, s in enumerate(STATS)}
        SQ_NO = {k: n for n, k in enumerate((s[0], i) for s in STATS for i in range(s[1]))}
        SQ_KEYS = list(SQ_NO)

        def stat_square(act, key, i, src):
            n = SQ_NO[(key, i)]
            if n >= 4:
                act.wait_ge(s_averaged.sem, s_averaged.after(*SQ_KEYS[n - 4]))
            w = STATS[STAT_NO[key]][3]
            act.activation(sq[:, n % 4, 0:w], src, ACT.Square).then_inc(s_squared.sem, s_squared.event(key, i))

        def stat_average(pe, key, i):
            no = STAT_NO[key]
            _, n, ones, w = STATS[no]
            if i == 0 and no:
                pe.wait_ge(s_logged.sem, s_logged.after(STATS[no - 1][0]))
            pe.wait_ge(s_squared.sem, s_squared.after(key, i))
            pe.matmul(SUM[:, 0:w], ones[:, :], sq[:, SQ_NO[(key, i)] % 4, 0:w],
                                          start=(i == 0), stop=(i == n - 1)).then_inc(s_averaged.sem, s_averaged.event(key, i))

        def stat_root(act, key):
            no = STAT_NO[key]
            _, n, _, w = STATS[no]
            act.wait_ge(s_averaged.sem, s_averaged.after(key, n - 1))
            if no >= 2:
                root_read(act, STATS[no - 2][0])
            r = rs[:, no % 2, 0:w]
            act.activation(r, SUM[:, 0:w], ACT.Ln, bias=epst[:, 0:1]).then_inc(s_logged.sem, s_logged.event(key))
            act.wait_ge(s_logged.sem, s_logged.after(key))
            act.activation(r, r, ACT.Exp, scale=-0.5).then_inc(s_rooted.sem, s_rooted.event(key))

        def RS(key):
            no = STAT_NO[key]
            return rs[:, no % 2, 0:STATS[no][3]]

        hi_at, lo_at = [0], [0]

        def split_hi(act, upto):
            while hi_at[0] <= min(upto, len(CHUNKS) - 1):
                n = hi_at[0]
                act.wait_ge(s_raw[n % RAW], landed_at[n])
                if n >= SPLIT:
                    act.wait_ge(s_w_used.sem, s_w_used.after(CHUNKS[n - SPLIT]))
                nk = k_tiles(n)
                act.activation(whi[n % SPLIT][:, 0:nk, :], raw[n % RAW][:, 0:nk, :], ACT.Copy).then_inc(s_w_hi.sem, s_w_hi.event(CHUNKS[n]))
                hi_at[0] += 1

        def split_lo(dve, upto):
            while lo_at[0] <= min(upto, len(CHUNKS) - 1):
                n = lo_at[0]
                dve.wait_ge(s_w_hi.sem, s_w_hi.after(CHUNKS[n]))
                nk = k_tiles(n)
                dve.tensor_tensor(wlo[n % SPLIT][:, 0:nk, :], raw[n % RAW][:, 0:nk, :],
                                                  whi[n % SPLIT][:, 0:nk, :].bitcast(F32), ALU.subtract).then_inc(s_w_lo.sem, s_w_lo.event(CHUNKS[n]))
                lo_at[0] += 1

        def x_hi(act, key, k, src, w):
            act.activation(xhi[:, k, 0:w], src, ACT.Copy).then_inc(s_x_hi.sem, s_x_hi.event(key, k))

        def x_lo(dve, key, k, src, w):
            dve.wait_ge(s_x_hi.sem, s_x_hi.after(key, k))
            dve.tensor_tensor(xlo[:, k, 0:w], src, xhi[:, k, 0:w].bitcast(F32), ALU.subtract).then_inc(s_x_lo.sem, s_x_lo.event(key, k))

        def product(pe, dst, ah, al, bh, bl, first, last, **kw):
            pe.matmul(dst, ah, bh, start=first, stop=False, **kw)
            pe.matmul(dst, ah, bl, start=False, stop=False, **kw)
            return pe.matmul(dst, al, bh, start=False, stop=last, **kw)

        def gemm(pe, g, xkey, w, tokens=False):
            no = GROUPS.index(g)
            if no >= 3:
                pg = GROUPS[no - 3]
                drained(pe, pg)
            b = pair(g)
            js = range(3 if g[0] == "down" else 1)
            k = 0
            for j in js:
                n = CHUNK_NO[(g, j)]
                pe.wait_ge(s_w_lo.sem, s_w_lo.after(CHUNKS[n]))
                h, lo = whi[n % SPLIT], wlo[n % SPLIT]
                nk = k_tiles(n)
                k0 = DOWN_K[j][0] if g[0] == "down" else 0
                if xkey is not None and g[2] == 0:
                    pe.wait_ge(s_x_lo.sem, s_x_lo.after(xkey, KT - 1))
                if g[0] == "down" and g[2] == 0:
                    pe.wait_ge(s_h_lo.sem, s_h_lo.after(g[1], k0 + nk - 1))
                xa, xb = (hhi, hlo) if g[0] == "down" else (xhi, xlo)
                if tokens:
                    tiles = [(ps[b + 1][:, 0:CW], 0), (ps[b][:, 0:CW], META), (ps[b][:, CW:2 * CW], META + P)] \
                        if w == T else [(ps[b][:, 0:CW], 0), (ps[b][:, CW:2 * CW], P)]
                    for dst, t0 in tiles:
                        for k in range(8):
                            a = slice(t0, t0 + P)
                            mm = product(pe, dst, xa[:, k, a], xb[:, k, a], h[:, k, :], lo[:, k, :], k == 0, k == 7)
                else:
                    for k in range(nk):
                        for mt in range(2):
                            c = slice(mt * P, mt * P + P)
                            mm = product(pe, ps[b + mt][:, 0:w], h[:, k, c], lo[:, k, c], xa[:, k0 + k, 0:w],
                                         xb[:, k0 + k, 0:w], k == 0 and j == js[0], k == nk - 1 and j == js[-1])
                mm.then_inc(s_w_used.sem, s_w_used.event(CHUNKS[n]))

        def product_done(eng, g):
            eng.wait_ge(s_w_used.sem, s_w_used.after(g, 2 if g[0] == "down" else 0))

        ADA_IN, ADA_UP = (2, 5, 8, 11), (0, 3, 6, 9, 12, 15, 18, 21)

        def ada_no(l, part, i):
            return 12 * l + (ADA_IN.index(i) if part == "in" else 4 + ADA_UP.index(i))

        def mod_columns(pe, a):
            pe.wait_ge(s_ada_sum.sem, s_ada_sum.after(a))
            for j in range(2):
                mm = pe.matmul(ps[7][:, 2 * a + j:2 * a + j + 1], adr[:, a % 2, j * P:j * P + P], ones_1[:, 0:1],
                               start=True, stop=True)
            mm.then_inc(s_ada_used.sem, s_ada_used.event(a))

        block = ctx.enter_context(nc.Block())

        @block.sync
        def _(sp):
            def load_chunk(n):
                if n >= RAW:
                    sp.wait_ge(s_w_lo.sem, s_w_lo.after(CHUNKS[n - RAW]))
                for dst, src in pieces(n):
                    sp.dma_start(dst, src).then_inc(s_raw[n % RAW], 16)

            for t, (a, w) in enumerate(TOK):
                src = A["meta_tokens"] if t == 0 else A["x"][0, a - META:a - META + w, :]
                sp.dma_start(xs[0:w, t, :], src).then_inc(s_x, 16)
            for dst, src in row_dmas:
                sp.dma_start(dst, src).then_inc(s_prm, 16)
            for n in range(RAW):
                load_chunk(n)
            for dst, src in small_dmas:
                sp.dma_start(dst, src).then_inc(s_small, 16)
            for n in range(RAW, len(CHUNKS)):
                load_chunk(n)
            for t in range(2):
                for half_ in range(2):
                    sp.wait_ge(s_turned_back.sem, s_turned_back.after(t, half_))
                    sp.dma_start(out[0, t * P:(t + 1) * P, 512 * half_:512 * half_ + 512],
                                 OB[:, t, 512 * half_:512 * half_ + 512]).then_inc(s_out, 16)
            sp.wait_ge(s_out, 64)

        @block.gpsimd
        def _(pool):
            n_const = [0]

            def fill(t, v):
                pool.memset(t, v).then_inc(s_filled.sem, s_filled.event(n_const[0]))
                pool.wait_ge(s_filled.sem, s_filled.after(n_const[0]))
                n_const[0] += 1

            def keep(t, pattern, op, fill_, base, cm):
                pool.affine_select(out=t, in_=t, pattern=pattern, compare_op=op, fill=fill_,
                                                     base=base, channel_multiplier=cm).then_inc(s_filled.sem, s_filled.event(n_const[0]))
                pool.wait_ge(s_filled.sem, s_filled.after(n_const[0]))
                n_const[0] += 1

            fill(ident[:, :], 0.0)
            keep(ident[:, :], [[-1, P]], ALU.not_equal, 1.0, 0, 1)
            pool.memset(ones_d[:, :], 1.0 / D).then_inc(s_consts.sem, s_consts.event("ident"))
            fill(ones_1[:, :], 1.0)
            fill(ones_v[:, :], 1.0 / P)
            fill(ones_a[:, :], 1.0 / 512)
            fill(onesrow[:, :], 1.0)
            fill(glr1[:, :], 1.0)
            fill(epst[:, :], EPS)
            fill(ones_f[:, :], 0.0)
            for b in range(2):
                pool_block = ones_f[64 * b:64 * b + 64, 64 * b:64 * b + 64]
                fill(pool_block, 1.0 / 64)
            fill(identb[:, :], 0.0)
            keep(identb[:, :], [[-1, P]], ALU.not_equal, 1.0, 0, 1)
            fill(causal[:, :], 0.0)
            keep(causal[:, :], [[-1, P]], ALU.is_ge, -BIG, 0, 1)
            fill(half[:, :], 0.0)
            for b in range(2):
                fill(half[64 * b:64 * b + 64, b:b + 1], 1.0)
            fill(after[:, :], 0.0)
            for b in range(2):
                blk = after[64 * b:64 * b + 64, 64 * b:64 * b + 64]
                fill(blk, 1.0)
                keep(blk, [[-1, 64]], ALU.is_gt, 0.0, 0, 1)
            pool.memset(restart[:, :], 1.0).then_inc(s_consts.sem, s_consts.event("first"))
            pool.wait_ge(s_consts.sem, s_consts.after("first"))
            wv = kp(A["w_ada_2"][0])

            def load_ada(a):
                if a < 24:
                    if a >= 2:
                        pool.wait_ge(s_ada_sum.sem, s_ada_sum.after(a - 2))
                    pool.dma_start(ada[a % 2][:, :, :], wv[:, :, CW * a:CW * (a + 1)]).then_inc(s_ada[a % 2], 16)

            def ada_piece(a):
                load_ada(a + 1)
                pool.wait_ge(s_ada[a % 2], 16 * (a // 2 + 1))
                t = ada[a % 2]
                pool.tensor_tensor(t[:, :, :], t[:, :, :],
                                                      cact[:, :].unsqueeze(2).broadcast_to([P, KT, CW]), ALU.mult).then_inc(s_ada_mul.sem, s_ada_mul.event(a))
                pool.wait_ge(s_ada_mul.sem, s_ada_mul.after(a))
                pool.tensor_tensor(t[:, 0:4, :], t[:, 0:4, :], t[:, 4:8, :], ALU.add).then_inc(s_ada_four.sem, s_ada_four.event(a))
                pool.wait_ge(s_ada_four.sem, s_ada_four.after(a))
                pool.tensor_tensor(t[:, 0:2, :], t[:, 0:2, :], t[:, 2:4, :], ALU.add).then_inc(s_ada_two.sem, s_ada_two.event(a))
                pool.wait_ge(s_ada_two.sem, s_ada_two.after(a))
                if a >= 2:
                    pool.wait_ge(s_ada_used.sem, s_ada_used.after(a - 2))
                pool.tensor_tensor(adr[:, a % 2, :], t[:, 0, :], t[:, 1, :], ALU.add).then_inc(s_ada_sum.sem, s_ada_sum.event(a))

            pool.wait_ge(s_cact.sem, s_cact.after())
            load_ada(0)
            for l in range(DEPTH):
                for i in ADA_IN:
                    ada_piece(ada_no(l, "in", i))
                for i in range(FT):
                    if i in ADA_UP:
                        ada_piece(ada_no(l, "up", i))
                    pool.wait_ge(s_gated.sem, s_gated.after(l, i))
                    n = l * FT + i
                    if i >= 2:
                        pool.wait_ge(s_h_lo.sem, s_h_lo.after(l, i - 2))
                    s = i % 2
                    pool.tensor_tensor(hf[:, s, :], cv[:, s, 0, :], cv[:, s, 1, :], ALU.mult).then_inc(s_hidden.sem, s_hidden.event(l, i))
            fill(same_c[:, :], 0.0)
            for b in range(4):
                fill(same_c[32 * b:32 * b + 32, 32 * b:32 * b + 32], 1.0)
            keep(same_c[:, :], [[1, P]], ALU.is_ge, 0.0, 0, -1)
            fill(restart[:, :].rearrange("p (c t) -> p c t", t=HG_C)[:, :, 0:1], 0.0)
            fill(slope_i[:, :, :], 0.0)
            for h in range(ATT_H):
                keep(slope_i[:, h, :], [[-1, P]], ALU.not_equal, -(2.0 ** -(h + 1)), 0, 1)
            pool.iota(dist[:, :], pattern=[[-1, 2 * P]], base=P, channel_multiplier=1,
                                        allow_small_or_imprecise_dtypes=True).then_inc(s_filled.sem, s_filled.event(n_const[0]))
            pool.wait_ge(s_filled.sem, s_filled.after(n_const[0]))
            n_const[0] += 1
            keep(dist[:, :], [[-1, 2 * P]], ALU.is_ge, 2.0 ** 100, P, 1)
            keep(dist[:, :], [[1, 2 * P]], ALU.is_ge, 2.0 ** 100, -1, -1)
            pool.iota(iota8[:, :], pattern=[[1, 8]], base=0, channel_multiplier=0,
                                        allow_small_or_imprecise_dtypes=True).then_inc(s_filled.sem, s_filled.event(n_const[0]))
            pool.wait_ge(s_filled.sem, s_filled.after(n_const[0]))
            n_const[0] += 1
            product_done(pool, ("down", DEPTH - 1, 3))
            fill(At[:, :, :, :], 0.0)
            pool.memset(lbt[:, 4, :], 0.0).then_inc(s_consts.sem, s_consts.event("second"))

        @block.scalar
        def _(act):
            def drain(g, dst, src, func=ACT.Copy, last=True, **k):
                i = act.activation(dst, src, func, **k)
                if last:
                    i.then_inc(s_drained_act.sem, s_drained_act.event(g))

            act.wait_ge(s_params.sem, s_params.after())
            act.activation(cact[:, :], col("c", 0, 8), ACT.Silu).then_inc(s_cact.sem, s_cact.event())
            split_hi(act, 1)
            for l in range(DEPTH):
                src = ("x0",) if l == 0 else ("d", 0)
                key = ("n1", l)
                if l == 0:
                    for k in range(KT):
                        act.wait_ge(s_xt.sem, s_xt.after(src, k))
                        stat_square(act, key, k, XT[:, k, :])
                stat_root(act, key)
                for k in range(KT):
                    act.wait_ge(s_normed.sem, s_normed.after(key, k))
                    x_hi(act, key, k, XN[:, k, :], T)
                act.wait_ge(s_fz.sem, s_fz.after(l))
                act.activation(fl[:, :], fz[:, :], ACT.Abs).then_inc(s_fl1.sem, s_fl1.event(l))
                act.wait_ge(s_fl1.sem, s_fl1.after(l))
                act.activation(fl[:, :], fl[:, :], ACT.Exp, scale=-1.0).then_inc(s_fl2.sem, s_fl2.event(l))
                act.wait_ge(s_fl2.sem, s_fl2.after(l))
                act.activation(fl[:, :], fl[:, :], ACT.Ln, bias=1.0).then_inc(s_fl3.sem, s_fl3.event(l))
                for i, (name, h) in enumerate(IN_ORDER):
                    g = ("in", l, i)
                    split_hi(act, CHUNK_NO[(g, 0)] + 1)
                    if name not in ACT_DRAINS:
                        continue
                    product_done(act, g)
                    b = pair(g)
                    if name in ("gv", "fv"):
                        t = gvt if name == "gv" else fvt
                        cs = slice(CW * h, CW * h + CW)
                        drain(g, t[:, 1:3, cs], ps[b][:, :].rearrange("p (t n) -> p t n", t=2), last=False)
                        drain(g, t[0:META, 0, cs], ps[b + 1][0:META, 0:CW])
                    elif name == "gr":
                        for t in range(2):
                            drain(g, grT[:, 2 * h + t, :], ps[b + t][:, 0:T], ACT.Silu, last=(t == 1))
                    else:
                        for t in range(2):
                            drain(g, fqT[:, 2 * h + t, :], ps[b + t][:, 0:T], ACT.Copy, last=(t == 1), scale=0.125)
                split_hi(act, CHUNK_NO[(("in", l, 11), 0)] + 2)
                act.wait_ge(s_z.sem, s_z.after(l))
                full, mt = la[:, 1:3, :].rearrange("p t n -> p (t n)"), la[0:META, 0, :]
                act.activation(full, ps[0][:, :], ACT.Abs)
                act.activation(mt, ps[1][0:META, 0:256], ACT.Abs).then_inc(s_za.sem, s_za.event(l))
                act.wait_ge(s_za.sem, s_za.after(l))
                act.activation(full, full, ACT.Exp, scale=-1.0)
                act.activation(mt, mt, ACT.Exp, scale=-1.0).then_inc(s_zb.sem, s_zb.event(l))
                act.wait_ge(s_zb.sem, s_zb.after(l))
                act.activation(full, full, ACT.Ln, bias=1.0)
                act.activation(mt, mt, ACT.Ln, bias=1.0).then_inc(s_zc.sem, s_zc.event(l))
                act.wait_ge(s_gla_d.sem, s_gla_d.after(l))
                act.activation(kd[:, 1:3, :].rearrange("p t n -> p (t n)"), ps[2][:, :], ACT.Exp, scale=1 / 16.0)
                act.activation(kd[0:META, 0, :], ps[3][0:META, 0:256], ACT.Exp, scale=1 / 16.0)
                act.activation(dec[:, :], ps[6][:, 0:8], ACT.Exp, scale=1 / 16.0).then_inc(s_gla_e.sem, s_gla_e.event(l))
                for h in range(4):
                    act.wait_ge(s_gla_o.sem, s_gla_o.after(l, h))
                    stat_square(act, ("g", l, h), 0, ps[GLA_BANK[h]][:, 0:T])
                for h in range(4):
                    stat_root(act, ("g", l, h))
                for h in range(4):
                    act.wait_ge(s_mixed.sem, s_mixed.after(l, h))
                    x_hi(act, ("mix", l), h, XN[:, h, :], T)
                for s in range(FOX_H + 4):
                    if s >= 3 and (s - 3) % 2 == 1:
                        stat_root(act, ("f", l, (s - 4) // 2))
                    if s < FOX_H:
                        for q, (q0, qn) in enumerate(TOK):
                            act.wait_ge(s_nmax.sem, s_nmax.after(l, s, q))
                            if s >= 2:
                                act.wait_ge(s_turned.sem, s_turned.after(l, s - 2))
                            c = s * 3 + q
                            act.activation(Pq[0:qn, s % 2, q, 0:q0 + qn], ps[FOX_BANK[q]][0:qn, 0:q0 + qn], ACT.Exp, bias=nmx[0:qn, c:c + 1], accum_out=psm[0:qn, c:c + 1]).then_inc(s_pexp.sem, s_pexp.event(l, s, q))
                    if 1 <= s <= FOX_H:
                        h = s - 1
                        act.wait_ge(s_turned.sem, s_turned.after(l, h))
                        if h >= 2:
                            act.wait_ge(s_pv.sem, s_pv.after(l, h - 2))
                        act.activation(PTs[:, h % 2, :], ps[2 + h % 2][:, 0:384], ACT.Copy).then_inc(s_pt_copied.sem, s_pt_copied.event(l, h))
                    if s >= 3 and (s - 3) % 2 == 0 and (s - 3) // 2 < 4:
                        j = (s - 3) // 2
                        act.wait_ge(s_fox_o.sem, s_fox_o.after(l, j))
                        stat_square(act, ("f", l, j), 0, XN[:, 4 + j, :])
                    if s >= 5 and (s - 5) % 2 == 0 and (s - 5) // 2 < 4:
                        j = (s - 5) // 2
                        act.wait_ge(s_mixed.sem, s_mixed.after(l, 4 + j))
                        x_hi(act, ("mix", l), 4 + j, XN[:, 4 + j, :], T)
                key = ("n2", l)
                for i in range(4):
                    g = ("out", l, i)
                    split_hi(act, CHUNK_NO[(g, 0)] + 1)
                    for t in range(2):
                        act.wait_ge(s_xt.sem, s_xt.after(("o", l), 2 * i + t))
                        stat_square(act, key, 2 * i + t, XT[:, 2 * i + t, :])
                split_hi(act, CHUNK_NO[(("out", l, 3), 0)] + 2)
                stat_root(act, key)
                for k in range(KT):
                    act.wait_ge(s_normed.sem, s_normed.after(key, k))
                    x_hi(act, key, k, XN[:, k, :], T)
                for i in range(FT + 2):
                    if i < FT:
                        g = ("up", l, i)
                        split_hi(act, CHUNK_NO[(g, 0)] + 1)
                        product_done(act, g)
                        if i >= 2:
                            act.wait_ge(s_hidden.sem, s_hidden.after(l, i - 2))
                        for t in range(2):
                            f = i + FT * t
                            o = act.activation(cv[:, i % 2, t, :], ps[pair(g) + t][:, 0:T], ACT.Identity,
                                               bias=col("conv_b", l * 2 * FT + f),
                                               scale=col("conv_w", (l * 3 + 2) * 2 * FT + f))
                        o.then_inc(s_tap2.sem, s_tap2.event(l, i))
                    if 1 <= i <= FT:
                        act.wait_ge(s_convolved.sem, s_convolved.after(l, i - 1))
                        s = (i - 1) % 2
                        act.activation(cv[:, s, 1, :], cv[:, s, 1, :], ACT.Silu).then_inc(s_gated.sem, s_gated.event(l, i - 1))
                    if i >= 2:
                        act.wait_ge(s_hidden.sem, s_hidden.after(l, i - 2))
                        act.activation(hhi[:, i - 2, :], hf[:, i % 2, :], ACT.Copy).then_inc(s_h_hi.sem, s_h_hi.event(l, i - 2))
                key = ("n1", l + 1) if l + 1 < DEPTH else ("nf",)
                for i in range(4):
                    g = ("down", l, i)
                    split_hi(act, CHUNK_NO[(g, 2)] + 1)
                    for t in range(2):
                        act.wait_ge(s_xt.sem, s_xt.after(("d", l), 2 * i + t))
                        m_ = 2 * i + t
                        stat_square(act, key, m_, XT[:, m_, :] if l + 1 < DEPTH else XT[:, m_, META:T])
                split_hi(act, CHUNK_NO[(("down", l, 3), 2)] + 2)
            stat_root(act, ("nf",))
            for k in range(KT):
                act.wait_ge(s_xt.sem, s_xt.after(("f",), k))
                stat_square(act, ("n3",), k, XT[:, k, META:T])
            stat_root(act, ("n3",))
            for k in range(KT):
                act.wait_ge(s_normed.sem, s_normed.after(("n3",), k))
                x_hi(act, ("n3",), k, XN[:, k, 0:T2], T2)
            act.wait_ge(s_lb_sub.sem, s_lb_sub.after())
            act.activation(lbt[:, 1, 0:8], lbt[:, 1, 0:8], ACT.Exp).then_inc(s_lb_exp.sem, s_lb_exp.event())
            for i, (name, h) in enumerate(IN2_ORDER):
                g = ("in2", 0, i)
                split_hi(act, CHUNK_NO[(g, 0)] + 1)
                if name not in ACT_DRAINS:
                    continue
                product_done(act, g)
                for t in range(2):
                    src = ps[pair(g) + t][:, 0:T2]
                    if name == "ka":
                        drain(g, (kaT if t == 0 else vaT)[:, :], src, last=(t == 1))
                    else:
                        dst = {"fh": fh, "qh": qh, "gh": gh}[name]
                        drain(g, dst[:, 2 * h + t, :], src, ACT.Sigmoid if name == "fh" else ACT.Silu, last=(t == 1))
            split_hi(act, CHUNK_NO[(("in2", 0, 10), 0)] + 2)
            fl2 = lambda t: t[:, :, :].rearrange("p h t -> p (h t)")
            act.wait_ge(s_forget.sem, s_forget.after())
            act.activation(fl2(fh), fl2(fh), ACT.Ln).then_inc(s_logf.sem, s_logf.event())
            act.wait_ge(s_cum.sem, s_cum.after(HG_H - 1))
            act.activation(fl2(fh), fl2(bb), ACT.Exp).then_inc(s_exp_b.sem, s_exp_b.event())
            act.activation(fl2(kdT), fl2(bb), ACT.Exp, scale=-1.0).then_inc(s_exp_nb.sem, s_exp_nb.event())
            act.wait_ge(s_end_sub.sem, s_end_sub.after())
            act.activation(fl2(keT), fl2(keT), ACT.Exp).then_inc(s_exp_end.sem, s_exp_end.event())
            for h in range(HG_H):
                act.wait_ge(s_hg_o.sem, s_hg_o.after(h))
                stat_square(act, ("h", h), 0, ps[HG_BANK[h]][:, 0:T2])
            for h in range(HG_H):
                stat_root(act, ("h", h))
            for h in range(HG_H):
                act.wait_ge(s_mixed2.sem, s_mixed2.after(4 + h))
                x_hi(act, ("mix2",), 4 + h, XN[:, 4 + h, 0:T2], T2)
            for s in range(ATT_H + 3):
                if s < ATT_H:
                    h = HEADS[s]
                    for q in range(2):
                        act.wait_ge(s_nmax2.sem, s_nmax2.after(s, q))
                        if s >= 2:
                            act.wait_ge(s_turned2.sem, s_turned2.after(s - 2))
                        c = s * 2 + q
                        dst = P2[:, s % 2, 0:P] if q == 0 else P2[:, s % 2, P:3 * P]
                        act.activation(dst, ps[2 * (s % 2) + q][:, 0:P * (q + 1)], ACT.Exp, bias=nmx[:, c:c + 1],
                                       accum_out=psm[:, c:c + 1])
                        act.activation(pri[:, c:c + 1], bc44[:, 36 + h:37 + h], ACT.Exp, bias=nmx[:, c:c + 1]).then_inc(s_pexp2.sem, s_pexp2.event(s, q))
                if 1 <= s <= ATT_H:
                    act.wait_ge(s_turned2.sem, s_turned2.after(s - 1))
                    if s >= 3:
                        act.wait_ge(s_pv2.sem, s_pv2.after(s - 3))
                    act.activation(PT2[:, (s - 1) % 2, :], ps[4 + (s - 1) % 2][:, 0:384], ACT.Copy).then_inc(s_pt2.sem, s_pt2.event(s - 1))
                if s >= 3 and (s - 3) % 2 == 0 and (s - 3) // 2 < 4:
                    j = (s - 3) // 2
                    act.wait_ge(s_att_o.sem, s_att_o.after(j))
                    stat_square(act, ("att",), j, XN[:, j, 0:T2])
            stat_root(act, ("att",))
            for j in range(4):
                act.wait_ge(s_mixed2.sem, s_mixed2.after(j))
                x_hi(act, ("mix2",), j, XN[:, j, 0:T2], T2)
            for i in range(4):
                g = ("out2", 0, i)
                split_hi(act, CHUNK_NO[(g, 0)] + 1)
                for t in range(2):
                    act.wait_ge(s_mixout.sem, s_mixout.after(2 * i + t))
                    stat_square(act, ("n4",), 2 * i + t, XN[:, 2 * i + t, 0:T2])
            split_hi(act, CHUNK_NO[(("out2", 0, 3), 0)] + 2)
            stat_root(act, ("n4",))
            for k in range(KT):
                act.wait_ge(s_xt.sem, s_xt.after(("p",), k))
                stat_square(act, ("n5",), k, XT[:, k, META:T])
            stat_root(act, ("n5",))
            for k in range(KT):
                act.wait_ge(s_normed.sem, s_normed.after(("n5",), k))
                x_hi(act, ("n5",), k, XN[:, k, 0:T2], T2)
            for t in range(2):
                act.wait_ge(s_r_sub.sem, s_r_sub.after(t))
                act.activation(rt[:, t, 96:104], rt[:, t, 96:104], ACT.Exp).then_inc(s_r_exp.sem, s_r_exp.event(t))
            for e in range(NEXP + 1):
                if e < NEXP:
                    n = CHUNK_NO[(("gate", 0, e), 0)]
                    split_hi(act, n + 2)
                    act.wait_ge(s_w_used.sem, s_w_used.after(("gate", 0, e), 0))
                    if e >= 2:
                        act.wait_ge(s_hu.sem, s_hu.after(e - 2))
                    act.activation(sg[:, e % 2, :], ps[4][:, :], ACT.Silu).then_inc(s_e_gate.sem, s_e_gate.event(e))
                    split_hi(act, n + 3)
                    act.wait_ge(s_hu.sem, s_hu.after(e))
                    if e >= 2:
                        act.wait_ge(s_w_used.sem, s_w_used.after(("dn", 0, e - 2), 0))
                    act.activation(huh[:, e % 2, :], hu[:, e % 2, :], ACT.Copy).then_inc(s_hu_hi.sem, s_hu_hi.event(e))
            for k in range(KT):
                act.wait_ge(s_y.sem, s_y.after(k))
                stat_square(act, ("n6",), k, XN[:, k, 0:T2])
            stat_root(act, ("n6",))

        @block.vector
        def _(dve):
            def normalise(key, gain, off=0, w=T, last_reads=True):
                dve.wait_ge(s_rooted.sem, s_rooted.after(key))
                for k in range(KT):
                    dve.scalar_tensor_tensor(XN[:, k, 0:w], XT[:, k, off:off + w], gain(k), RS(key), ALU.mult, ALU.mult).then_inc(s_normed.sem, s_normed.event(key, k))
                    if k == KT - 1:
                        pass

            def low_parts(key, w=T, xkey=None):
                for k in range(KT):
                    x_lo(dve, xkey or key, k, XN[:, k, 0:w], w)


            dve.wait_ge(s_prm_turned.sem, s_prm_turned.after())
            dve.tensor_copy(PC[:, :], ps[0][:, 0:RBLK * P]).then_inc(s_params.sem, s_params.event())
            for k in range(KT):
                dve.wait_ge(s_x_turned.sem, s_x_turned.after(k))
                dve.tensor_copy(XT[:, k, :], ps[1 + k % 4][:, 0:T]).then_inc(s_xt.sem, s_xt.event(("x0",), k))
            dve.wait_ge(s_bc.sem, s_bc.after())
            dve.tensor_copy(bc44[:, :], ps[6][:, 0:44]).then_inc(s_bc44.sem, s_bc44.event())
            split_lo(dve, 1)
            for l in range(DEPTH):
                key = ("n1", l)
                dve.wait_ge(s_rooted.sem, s_rooted.after(key))
                dve.wait_ge(s_params.sem, s_params.after())
                if l:
                    dve.wait_ge(s_xt.sem, s_xt.after(("d", l - 1), KT - 1))
                else:
                    dve.wait_ge(s_xt.sem, s_xt.after(("x0",), KT - 1))
                for k in range(KT):
                    dve.scalar_tensor_tensor(XN[:, k, :], XT[:, k, :], col("attn_norm", 8 * l + k), RS(key), ALU.mult, ALU.mult).then_inc(s_normed.sem, s_normed.event(key, k))
                dve.wait_ge(s_normed.sem, s_normed.after(key, KT - 1))
                for k in range(KT):
                    x_lo(dve, key, k, XN[:, k, :], T)
                dve.wait_ge(s_small_ff.sem, s_small_ff.after(l))
                dve.tensor_scalar(fz[:, :], ps[7][0:8, 64:64 + T], bfo[:, l:l + 1], None, ALU.add).then_inc(s_fz.sem, s_fz.event(l))
                dve.wait_ge(s_small_glr.sem, s_small_glr.after(l))
                dve.tensor_copy(glr1[0:16, :], ps[6][0:16, 0:T]).then_inc(s_glr.sem, s_glr.event(l))
                dve.wait_ge(s_fl3.sem, s_fl3.after(l))
                dve.scalar_tensor_tensor(fl[:, :], fz[:, :], 0.0, fl[:, :], ALU.min, ALU.subtract).then_inc(s_lf.sem, s_lf.event(l))
                dve.wait_ge(s_lf.sem, s_lf.after(l))
                dve.tensor_tensor_scan(negc[:, :], onesrow[:, :], fl[:, :], 0.0, ALU.mult, ALU.subtract).then_inc(s_negc.sem, s_negc.event(l))
                for i, (name, h) in enumerate(IN_ORDER):
                    g = ("in", l, i)
                    split_lo(dve, CHUNK_NO[(g, 0)] + 1)
                    if name in ACT_DRAINS:
                        continue
                    product_done(dve, g)
                    b = pair(g)
                    if name == "gk":
                        dve.tensor_copy(gkt[:, 1:3, :], ps[b][:, :].rearrange("p (t n) -> p t n", t=2))
                        dve.tensor_copy(gkt[0:META, 0, :], ps[b + 1][0:META, 0:CW]).then_inc(s_drained_dve.sem, s_drained_dve.event(g))
                    elif name == "gq":
                        for t in range(2):
                            o = dve.tensor_scalar(gqT[:, t, :], ps[b + t][:, 0:T], 0.125, None, ALU.mult)
                        o.then_inc(s_drained_dve.sem, s_drained_dve.event(g))
                    else:
                        for t in range(2):
                            o = dve.tensor_copy(fkT[:, 2 * h + t, :], ps[b + t][:, 0:T])
                        o.then_inc(s_drained_dve.sem, s_drained_dve.event(g))
                split_lo(dve, CHUNK_NO[(("in", l, 11), 0)] + 2)
                dve.wait_ge(s_zc.sem, s_zc.after(l))
                full, mt = la[:, 1:3, :].rearrange("p t n -> p (t n)"), la[0:META, 0, :]
                dve.scalar_tensor_tensor(full, ps[0][:, :], 0.0, full, ALU.min, ALU.subtract)
                dve.scalar_tensor_tensor(mt, ps[1][0:META, 0:256], 0.0, mt, ALU.min, ALU.subtract).then_inc(s_la.sem, s_la.event(l))
                dve.wait_ge(s_gla_e.sem, s_gla_e.after(l))
                dve.tensor_tensor(kd[:, 1:3, :], kd[:, 1:3, :], gkt[:, 1:3, :], ALU.mult)
                dve.tensor_tensor(kd[0:META, 0, :], kd[0:META, 0, :], gkt[0:META, 0, :], ALU.mult).then_inc(s_kd.sem, s_kd.event(l))
                dve.wait_ge(s_gla_u.sem, s_gla_u.after(l))
                for c in range(5):
                    for p in range(2):
                        u = ps[4][:, p * P:p * P + P] if c == 0 else \
                            ps[(c - 1) % 2][:, ((c - 1) // 2) * 256 + p * P:((c - 1) // 2) * 256 + p * P + P]
                        if c == 0:
                            dve.tensor_copy(ST[:, p, 0, :], u).then_inc(s_state.sem, s_state.event(l, c, p))
                        else:
                            dve.wait_ge(s_state.sem, s_state.after(l, c - 1, p))
                            dve.scalar_tensor_tensor(ST[:, p, c, :], ST[:, p, c - 1, :], dec[:, p * 4 + c - 1:p * 4 + c], u, ALU.mult, ALU.add).then_inc(s_state.sem, s_state.event(l, c, p))
                for h in range(4):
                    k_ = ("g", l, h)
                    dve.wait_ge(s_rooted.sem, s_rooted.after(k_))
                    dve.scalar_tensor_tensor(XN[:, h, :], ps[GLA_BANK[h]][:, 0:T], col("gla_norm", 4 * l + h), RS(k_), ALU.mult, ALU.mult).then_inc(s_scaled.sem, s_scaled.event(l, h))
                    dve.wait_ge(s_scaled.sem, s_scaled.after(l, h))
                    dve.tensor_tensor(XN[:, h, :], XN[:, h, :], grT[:, h, :], ALU.mult).then_inc(s_mixed.sem, s_mixed.event(l, h))
                for h in range(4):
                    x_lo(dve, ("mix", l), h, XN[:, h, :], T)
                for s in range(FOX_H + 4):
                    if s < FOX_H:
                        for q, (q0, qn) in enumerate(TOK):
                            c = s * 3 + q
                            dve.wait_ge(s_scores.sem, s_scores.after(l, s, q))
                            dve.tensor_reduce(nmx[0:qn, c:c + 1], ps[FOX_BANK[q]][0:qn, 0:q0 + qn], AX_X,
                                                              ALU.max, negate=True).then_inc(s_nmax.sem, s_nmax.event(l, s, q))
                    if 1 <= s <= FOX_H:
                        h = s - 1
                        dve.wait_ge(s_turned.sem, s_turned.after(l, h))
                        if h >= 2:
                            dve.wait_ge(s_pv.sem, s_pv.after(l, h - 2))
                        dve.tensor_copy(PTm[:, h % 2, :], ps[5][0:META, 0:T]).then_inc(s_ptm_copied.sem, s_ptm_copied.event(l, h))
                    if s < FOX_H:
                        for q, (q0, qn) in enumerate(TOK):
                            c = s * 3 + q
                            dve.wait_ge(s_pexp.sem, s_pexp.after(l, s, q))
                            dve.reciprocal(pri[0:qn, c:c + 1], psm[0:qn, c:c + 1]).then_inc(s_recip.sem, s_recip.event(l, s, q))
                        for q, (q0, qn) in enumerate(TOK):
                            c = s * 3 + q
                            dve.wait_ge(s_recip.sem, s_recip.after(l, s, q))
                            v = Pq[0:qn, s % 2, q, 0:q0 + qn]
                            dve.tensor_scalar(v, v, pri[0:qn, c:c + 1], None, ALU.mult).then_inc(s_prob.sem, s_prob.event(l, s, q))
                    if s >= 3 and (s - 3) % 2 == 0 and (s - 3) // 2 < 4:
                        j = (s - 3) // 2
                        dve.wait_ge(s_pv.sem, s_pv.after(l, 2 * j + 1))
                        dve.tensor_copy(XN[:, 4 + j, :], ps[6][:, 0:T]).then_inc(s_fox_o.sem, s_fox_o.event(l, j))
                    if s >= 4 and (s - 4) % 2 == 0 and (s - 4) // 2 < 4:
                        j = (s - 4) // 2
                        k_ = ("f", l, j)
                        dve.wait_ge(s_rooted.sem, s_rooted.after(k_))
                        dve.wait_ge(s_fox_o.sem, s_fox_o.after(l, j))
                        dve.scalar_tensor_tensor(XN[:, 4 + j, :], XN[:, 4 + j, :], col("fox_norm", 4 * l + j), RS(k_), ALU.mult, ALU.mult).then_inc(s_mixed.sem, s_mixed.event(l, 4 + j))
                        dve.wait_ge(s_mixed.sem, s_mixed.after(l, 4 + j))
                    if s >= 5 and (s - 5) % 2 == 0 and (s - 5) // 2 < 4:
                        x_lo(dve, ("mix", l), 4 + (s - 5) // 2, XN[:, 4 + (s - 5) // 2, :], T)

                def residual(kind, tag, i, last_chunk):
                    g = (kind, l, i)
                    split_lo(dve, last_chunk + 1)
                    product_done(dve, g)
                    for t in range(2):
                        o = dve.tensor_tensor(XT[:, 2 * i + t, :], ps[pair(g) + t][:, 0:T], XT[:, 2 * i + t, :], ALU.add)
                        o.then_inc(s_xt.sem, s_xt.event(tag, l, 2 * i + t))

                for i in range(4):
                    residual("out", "o", i, CHUNK_NO[(("out", l, i), 0)])
                split_lo(dve, CHUNK_NO[(("out", l, 3), 0)] + 2)
                key = ("n2", l)
                dve.wait_ge(s_xt.sem, s_xt.after(("o", l), KT - 1))
                dve.wait_ge(s_rooted.sem, s_rooted.after(key))
                for k in range(KT):
                    dve.scalar_tensor_tensor(XN[:, k, :], XT[:, k, :], col("ffn_norm", 8 * l + k), RS(key), ALU.mult, ALU.mult).then_inc(s_normed.sem, s_normed.event(key, k))
                dve.wait_ge(s_normed.sem, s_normed.after(key, KT - 1))
                for k in range(KT):
                    x_lo(dve, key, k, XN[:, k, :], T)
                for i in range(FT + 3):
                    if i < FT:
                        g = ("up", l, i)
                        split_lo(dve, CHUNK_NO[(g, 0)] + 1)
                        dve.wait_ge(s_tap2.sem, s_tap2.after(l, i))
                        s = i % 2
                        for t in range(2):
                            dve.scalar_tensor_tensor(cv[:, s, t, 1:T], ps[pair(g) + t][:, 0:T - 1], col("conv_w", (l * 3 + 1) * 2 * FT + i + FT * t), cv[:, s, t, 1:T], ALU.mult, ALU.add).then_inc(s_tap1.sem, s_tap1.event(l, i, t))
                        for t in range(2):
                            dve.wait_ge(s_tap1.sem, s_tap1.after(l, i, t))
                            o = dve.scalar_tensor_tensor(cv[:, s, t, 2:T], ps[pair(g) + t][:, 0:T - 2],
                                                         col("conv_w", l * 3 * 2 * FT + i + FT * t), cv[:, s, t, 2:T],
                                                         ALU.mult, ALU.add)
                        o.then_inc(s_convolved.sem, s_convolved.event(l, i))
                    if i >= 3 or i == FT:
                        pass
                    if i >= 2 and i - 2 < FT:
                        dve.wait_ge(s_h_hi.sem, s_h_hi.after(l, i - 2))
                        dve.tensor_tensor(hlo[:, i - 2, :], hf[:, i % 2, :], hhi[:, i - 2, :].bitcast(F32), ALU.subtract).then_inc(s_h_lo.sem, s_h_lo.event(l, i - 2))
                for i in range(4):
                    residual("down", "d", i, CHUNK_NO[(("down", l, i), 2)])
                split_lo(dve, CHUNK_NO[(("down", l, 3), 2)] + 2)
            dve.wait_ge(s_rooted.sem, s_rooted.after(("nf",)))
            dve.wait_ge(s_ada_used.sem, s_ada_used.after(23))
            dve.tensor_tensor(mod[:, :], ps[7][:, 0:48], col("b_ada", 0, 48), ALU.add).then_inc(s_mod.sem, s_mod.event())
            dve.wait_ge(s_mod.sem, s_mod.after())
            for n_, (ln_, m0) in enumerate((("ln1_pre", 8), ("ln1_post", 16), ("ln2_pre", 32), ("ln2_post", 40))):
                o = dve.scalar_tensor_tensor(gsc[:, n_, :], mod[:, m0:m0 + 8], 1.0 if n_ % 2 == 0 else 0.0, col(ln_, 0, 8),
                                             ALU.add, ALU.mult)
            o.then_inc(s_gsc.sem, s_gsc.event())
            ab = col("hgrn_lb", 0, 8)
            dve.tensor_tensor(lbt[:, 0, 0:4], ab[:, 0:4], ab[:, 4:8], ALU.max).then_inc(s_lb_max.sem, s_lb_max.event())
            dve.wait_ge(s_lb_max.sem, s_lb_max.after())
            dve.tensor_tensor(lbt[:, 1, 0:4], ab[:, 0:4], lbt[:, 0, 0:4], ALU.subtract)
            dve.tensor_tensor(lbt[:, 1, 4:8], ab[:, 4:8], lbt[:, 0, 0:4], ALU.subtract).then_inc(s_lb_sub.sem, s_lb_sub.event())
            dve.wait_ge(s_xt.sem, s_xt.after(("d", DEPTH - 1), KT - 1))
            for k in range(KT):
                dve.scalar_tensor_tensor(XT[:, k, META:T], XT[:, k, META:T], col("final_norm", k), RS(("nf",)), ALU.mult, ALU.mult).then_inc(s_xt.sem, s_xt.event(("f",), k))
            dve.wait_ge(s_xt.sem, s_xt.after(("f",), KT - 1))

            def modulated(key, n_, sh):
                dve.wait_ge(s_gsc.sem, s_gsc.after())
                dve.wait_ge(s_rooted.sem, s_rooted.after(key))
                for k in range(KT):
                    dve.scalar_tensor_tensor(XN[:, k, 0:T2], XT[:, k, META:T], gsc[:, n_, k:k + 1], RS(key), ALU.mult, ALU.mult).then_inc(s_scaled_n.sem, s_scaled_n.event(key, k))
                for k in range(KT):
                    dve.wait_ge(s_scaled_n.sem, s_scaled_n.after(key, k))
                    dve.tensor_scalar(XN[:, k, 0:T2], XN[:, k, 0:T2], mod[:, sh + k:sh + k + 1], None, ALU.add).then_inc(s_normed.sem, s_normed.event(key, k))
                for k in range(KT):
                    x_lo(dve, key, k, XN[:, k, 0:T2], T2)

            modulated(("n3",), 0, 0)
            dve.wait_ge(s_lb_exp.sem, s_lb_exp.after())
            dve.tensor_tensor(lbt[:, 2, 0:4], lbt[:, 1, 0:4], lbt[:, 1, 4:8], ALU.add).then_inc(s_lb_sum.sem, s_lb_sum.event())
            dve.wait_ge(s_lb_sum.sem, s_lb_sum.after())
            dve.reciprocal(lbt[:, 2, 4:8], lbt[:, 2, 0:4]).then_inc(s_lb_rec.sem, s_lb_rec.event())
            dve.wait_ge(s_lb_rec.sem, s_lb_rec.after())
            dve.tensor_tensor(lbt[:, 3, 0:4], lbt[:, 1, 0:4], lbt[:, 2, 4:8], ALU.mult).then_inc(s_lb.sem, s_lb.event())
            dve.wait_ge(s_lb.sem, s_lb.after())
            dve.tensor_scalar(lbt[:, 3, 4:8], lbt[:, 3, 0:4], -1.0, 1.0, ALU.mult, ALU.add).then_inc(s_lb1.sem, s_lb1.event())
            dve.wait_ge(s_lb1.sem, s_lb1.after())
            dve.wait_ge(s_consts.sem, s_consts.after("second"))
            dve.tensor_scalar(lbt[:, 4, 0:4], lbt[:, 3, 4:8], -1.0, None, ALU.mult).then_inc(s_lb2.sem, s_lb2.event())
            dve.wait_ge(s_lb2.sem, s_lb2.after())
            for i, (name, h) in enumerate(IN2_ORDER):
                g = ("in2", 0, i)
                split_lo(dve, CHUNK_NO[(g, 0)] + 1)
                if name == "qh" and h == 0:
                    dve.wait_ge(s_drained_act.sem, s_drained_act.after(("in2", 0, 1)))
                    for t in range(HG_H):
                        dve.tensor_scalar(kh[:, t, :], fh[:, t, :], lbt[:, 4, t:t + 1], lbt[:, 3, 4 + t:5 + t], ALU.mult, ALU.add).then_inc(s_kh.sem, s_kh.event(t))
                    for t in range(HG_H):
                        dve.wait_ge(s_kh.sem, s_kh.after(t))
                        o = dve.tensor_scalar(fh[:, t, :], fh[:, t, :], lbt[:, 3, 4 + t:5 + t], lbt[:, 3, t:t + 1], ALU.mult, ALU.add)
                    o.then_inc(s_forget.sem, s_forget.event())
                if name in ACT_DRAINS:
                    continue
                product_done(dve, g)
                b = pair(g)
                if name == "ih":
                    o = dve.tensor_copy(ih[:, :, CW * h:CW * h + CW], ps[b][:, :].rearrange("p (t n) -> p t n", t=2))
                else:
                    for t in range(2):
                        o = dve.tensor_scalar(qaT[:, 2 * h + t, :], ps[b + t][:, 0:T2], 0.125, None, ALU.mult)
                o.then_inc(s_drained_dve.sem, s_drained_dve.event(g))
            split_lo(dve, CHUNK_NO[(("in2", 0, 10), 0)] + 2)
            fl2 = lambda t: t[:, :, :].rearrange("p h t -> p (h t)")
            by_chunk = lambda t, h: t[:, h, :].rearrange("p (c t) -> p c t", t=HG_C)
            dve.wait_ge(s_logf.sem, s_logf.after())
            for h in range(HG_H):
                dve.tensor_tensor_scan(bb[:, h, :], restart[:, :], fh[:, h, :], 0.0, ALU.mult, ALU.add).then_inc(s_cum.sem, s_cum.event(h))
            dve.wait_ge(s_cum.sem, s_cum.after(HG_H - 1))
            for h in range(HG_H):
                v = by_chunk(bb, h)
                o = dve.tensor_tensor(by_chunk(keT, h), v[:, :, HG_C - 1:HG_C].broadcast_to([P, T2 // HG_C, HG_C]), v, ALU.subtract)
            o.then_inc(s_end_sub.sem, s_end_sub.event())
            dve.wait_ge(s_exp_b.sem, s_exp_b.after())
            dve.tensor_tensor(fl2(qh), fl2(qh), fl2(fh), ALU.mult).then_inc(s_qd.sem, s_qd.event())
            dve.wait_ge(s_exp_nb.sem, s_exp_nb.after())
            dve.tensor_tensor(fl2(kdT), fl2(kdT), fl2(kh), ALU.mult).then_inc(s_kd2.sem, s_kd2.event())
            dve.wait_ge(s_exp_end.sem, s_exp_end.after())
            dve.tensor_tensor(fl2(keT), fl2(keT), fl2(kh), ALU.mult).then_inc(s_ke.sem, s_ke.event())
            for t in range(2):
                dve.wait_ge(s_ke_turned.sem, s_ke_turned.after(t))
                dve.tensor_copy(ke[:, t, :, :].rearrange("p h n -> p (h n)"), ps[t][:, :]).then_inc(s_ke_copied.sem, s_ke_copied.event(t))
                dve.wait_ge(s_intra.sem, s_intra.after(t))
                mask = same_c[:, :].bitcast(I32)
                for h in range(HG_H):
                    o = dve.copy_predicated(At[:, t, h, :], mask, ps[2 + t][:, P * h:P * h + P])
                o.then_inc(s_a_copied.sem, s_a_copied.event(t))
            dve.wait_ge(s_va_turned.sem, s_va_turned.after())
            dve.tensor_copy(va[:, :, :].rearrange("p t n -> p (t n)"), ps[0][:, 0:256]).then_inc(s_va.sem, s_va.event())
            for c in range(7):
                u = ps[4 + c % 4] if c < 4 else ps[c % 4]
                dve.wait_ge(s_hg_u.sem, s_hg_u.after(c // 4))
                if c == 0:
                    dve.tensor_copy(SS[:, 0, :, :].rearrange("p h n -> p (h n)"), u[:, :]).then_inc(s_hg_s.sem, s_hg_s.event(0))
                    continue
                if c == 1:
                    pass
                dve.wait_ge(s_hg_s.sem, s_hg_s.after(c - 1))
                for h in range(HG_H):
                    d = fh[:, h, c * HG_C + HG_C - 1:c * HG_C + HG_C]
                    o = dve.scalar_tensor_tensor(SS[:, c, h, :], SS[:, c - 1, h, :], d, u[:, P * h:P * h + P],
                                                 ALU.mult, ALU.add)
                o.then_inc(s_hg_s.sem, s_hg_s.event(c))
            for h in range(HG_H):
                k_ = ("h", h)
                dve.wait_ge(s_rooted.sem, s_rooted.after(k_))
                dve.scalar_tensor_tensor(XN[:, 4 + h, 0:T2], ps[HG_BANK[h]][:, 0:T2], col("hgrn_out_norm", h), RS(k_), ALU.mult, ALU.mult).then_inc(s_scaled2.sem, s_scaled2.event(h))
                dve.wait_ge(s_scaled2.sem, s_scaled2.after(h))
                dve.tensor_tensor(XN[:, 4 + h, 0:T2], XN[:, 4 + h, 0:T2], gh[:, h, :], ALU.mult).then_inc(s_mixed2.sem, s_mixed2.event(4 + h))
            for h in range(HG_H):
                x_lo(dve, ("mix2",), 4 + h, XN[:, 4 + h, 0:T2], T2)
            dve.wait_ge(s_bc44.sem, s_bc44.after())
            for s in range(ATT_H + 3):
                if s < ATT_H:
                    h = HEADS[s]
                    for q in range(2):
                        c = 2 * s + q
                        dve.wait_ge(s_scores2.sem, s_scores2.after(s, q))
                        dve.tensor_reduce(nmx[:, c:c + 1], ps[2 * (s % 2) + q][:, 0:P * (q + 1)], AX_X, ALU.max,
                                                           negate=True).then_inc(s_nmaxa.sem, s_nmaxa.event(s, q))
                    for q in range(2):
                        c = 2 * s + q
                        dve.wait_ge(s_nmaxa.sem, s_nmaxa.after(s, q))
                        dve.scalar_tensor_tensor(nmx[:, c:c + 1], bc44[:, 36 + h:37 + h], -1.0, nmx[:, c:c + 1], ALU.mult, ALU.min).then_inc(s_nmax2.sem, s_nmax2.event(s, q))
                    for q in range(2):
                        c = 2 * s + q
                        dve.wait_ge(s_pexp2.sem, s_pexp2.after(s, q))
                        dve.tensor_tensor(psm[:, c:c + 1], psm[:, c:c + 1], pri[:, c:c + 1], ALU.add).then_inc(s_den2.sem, s_den2.event(s, q))
                    for q in range(2):
                        c = 2 * s + q
                        dve.wait_ge(s_den2.sem, s_den2.after(s, q))
                        dve.reciprocal(pri[:, c:c + 1], psm[:, c:c + 1]).then_inc(s_rec2.sem, s_rec2.event(s, q))
                    for q in range(2):
                        c = 2 * s + q
                        dve.wait_ge(s_rec2.sem, s_rec2.after(s, q))
                        v = P2[:, s % 2, 0:P] if q == 0 else P2[:, s % 2, P:3 * P]
                        dve.tensor_scalar(v, v, pri[:, c:c + 1], None, ALU.mult).then_inc(s_prob2.sem, s_prob2.event(s, q))
                if s >= 3 and (s - 3) % 2 == 0 and (s - 3) // 2 < 4:
                    j = (s - 3) // 2
                    dve.wait_ge(s_pv2.sem, s_pv2.after(2 * j + 1))
                    dve.tensor_copy(XN[:, j, 0:T2], ps[6][:, 0:T2]).then_inc(s_att_o.sem, s_att_o.event(j))
            dve.wait_ge(s_rooted.sem, s_rooted.after(("att",)))
            dve.wait_ge(s_att_o.sem, s_att_o.after(3))
            for j in range(4):
                dve.scalar_tensor_tensor(XN[:, j, 0:T2], XN[:, j, 0:T2], col("attn_out_norm", j), RS(("att",)), ALU.mult, ALU.mult).then_inc(s_mixed2.sem, s_mixed2.event(j))
            dve.wait_ge(s_mixed2.sem, s_mixed2.after(3))
            for j in range(4):
                x_lo(dve, ("mix2",), j, XN[:, j, 0:T2], T2)
            for i in range(4):
                g = ("out2", 0, i)
                split_lo(dve, CHUNK_NO[(g, 0)] + 1)
                product_done(dve, g)
                for t in range(2):
                    dve.tensor_copy(XN[:, 2 * i + t, 0:T2], ps[pair(g) + t][:, 0:T2]).then_inc(s_mixout.sem, s_mixout.event(2 * i + t))
            split_lo(dve, CHUNK_NO[(("out2", 0, 3), 0)] + 2)

            def post_norm(key, n_, tag):
                dve.wait_ge(s_rooted.sem, s_rooted.after(key))
                for k in range(KT):
                    dve.scalar_tensor_tensor(XN[:, k, 0:T2], XN[:, k, 0:T2], gsc[:, n_, k:k + 1], RS(key), ALU.mult, ALU.mult).then_inc(s_post.sem, s_post.event(key, k))
                for k in range(KT):
                    dve.wait_ge(s_post.sem, s_post.after(key, k))
                    dve.tensor_tensor(XT[:, k, META:T], XT[:, k, META:T], XN[:, k, 0:T2], ALU.add).then_inc(s_xt.sem, s_xt.event((tag,), k))

            dve.wait_ge(s_mixout.sem, s_mixout.after(KT - 1))
            post_norm(("n4",), 1, "p")
            dve.wait_ge(s_xt.sem, s_xt.after(("p",), KT - 1))
            modulated(("n5",), 2, 24)
            dve.wait_ge(s_routed.sem, s_routed.after())
            n_r = [0]

            def r(ins):
                ins.then_inc(s_r.sem, s_r.event(n_r[0]))
                dve.wait_ge(s_r.sem, s_r.after(n_r[0]))
                n_r[0] += 1

            r(dve.memset(rt[:, :, 0:8], -3.0e38))
            for t in range(2):
                lg = ps[0][:, 64 * t:64 * t + 36]
                R = lambda a, b: rt[:, t, a:b]
                r(dve.tensor_copy(R(0, 4), lg[:, 0:4]))
                r(dve.tensor_copy(R(8, 40), lg[:, 4:36]))
                r(dve.max(R(40, 48), R(0, 8)))
                r(dve.max_index(R(48, 56).bitcast(U32), R(40, 48), R(0, 8)))
                r(dve.tensor_copy(R(56, 57), R(48, 49).bitcast(U32)))
                r(dve.tensor_scalar(R(64, 72), iota8[:, :], R(56, 57), None, ALU.is_equal))
                r(dve.tensor_scalar(R(72, 80), R(8, 16), R(64, 65), None, ALU.mult))
                for g_ in range(1, 4):
                    r(dve.scalar_tensor_tensor(R(72, 80), R(8 + 8 * g_, 16 + 8 * g_), R(64 + g_, 65 + g_), R(72, 80),
                                               ALU.mult, ALU.add))
                r(dve.max(R(80, 88), R(72, 80)))
                r(dve.max_index(R(48, 56).bitcast(U32), R(80, 88), R(72, 80)))
                r(dve.tensor_copy(R(56, 58), R(48, 50).bitcast(U32)))
                r(dve.tensor_scalar(R(96, 100), R(0, 4), R(40, 41), None, ALU.subtract))
                r(dve.memset(R(101, 104), 0.0))
                dve.tensor_tensor(R(100, 101), R(81, 82), R(80, 81), ALU.subtract).then_inc(s_r_sub.sem, s_r_sub.event(t))
                dve.wait_ge(s_r_exp.sem, s_r_exp.after(t))
                r(dve.tensor_reduce(R(104, 105), R(96, 100), AX_X, ALU.add))
                r(dve.tensor_scalar(R(105, 106), R(100, 101), 1.0, None, ALU.add))
                r(dve.tensor_tensor(R(106, 107), R(104, 105), R(105, 106), ALU.mult))
                r(dve.reciprocal(R(107, 108), R(106, 107)))
                r(dve.tensor_tensor(R(108, 109), R(107, 108), R(100, 101), ALU.mult))
                r(dve.tensor_scalar(R(112, 120), iota8[:, :], R(56, 57), R(107, 108), ALU.is_equal, ALU.mult))
                r(dve.tensor_scalar(R(120, 128), iota8[:, :], R(57, 58), R(108, 109), ALU.is_equal, ALU.mult))
                r(dve.tensor_tensor(R(112, 120), R(112, 120), R(120, 128), ALU.add))
                for g_ in range(4):
                    o = dve.tensor_scalar(wt[:, t, 8 * g_:8 * g_ + 8], R(112, 120), R(64 + g_, 65 + g_), None, ALU.mult)
                o.then_inc(s_wt.sem, s_wt.event(t))
            dve.wait_ge(s_wt_turned.sem, s_wt_turned.after())
            dve.tensor_copy(WT[:, :], ps[1][0:NEXP, 0:T2]).then_inc(s_WT.sem, s_WT.event())
            for e in range(NEXP):
                n = CHUNK_NO[(("gate", 0, e), 0)]
                split_lo(dve, n + 2)
                dve.wait_ge(s_e_gate.sem, s_e_gate.after(e))
                dve.wait_ge(s_weighed.sem, s_weighed.after(e))
                s = e % 2
                w2 = ps[6][:, 0:T2]
                sgv, huv = sg[:, s, :], hu[:, s, :]
                for j in range(2):
                    o = dve.tensor_tensor(sgv[:, T2 * j:T2 * j + T2], sgv[:, T2 * j:T2 * j + T2], w2, ALU.mult)
                o.then_inc(s_sgw.sem, s_sgw.event(e))
                dve.wait_ge(s_sgw.sem, s_sgw.after(e))
                dve.wait_ge(s_w_used.sem, s_w_used.after(("upx", 0, e), 0))
                if e >= 2:
                    dve.wait_ge(s_hu_lo.sem, s_hu_lo.after(e - 2))
                dve.tensor_tensor(huv, ps[5][:, :], sgv, ALU.mult).then_inc(s_hu.sem, s_hu.event(e))
                split_lo(dve, n + 3)
                dve.wait_ge(s_hu_hi.sem, s_hu_hi.after(e))
                if e >= 2:
                    dve.wait_ge(s_w_used.sem, s_w_used.after(("dn", 0, e - 2), 0))
                dve.tensor_tensor(hul[:, s, :], huv, huh[:, s, :].bitcast(F32), ALU.subtract).then_inc(s_hu_lo.sem, s_hu_lo.event(e))
            dve.wait_ge(s_w_used.sem, s_w_used.after(("dn", 0, NEXP - 1), 0))
            for k in range(KT):
                dve.tensor_copy(XN[:, k, 0:T2], ps[k // 2][:, T2 * (k % 2):T2 * (k % 2) + T2]).then_inc(s_y.sem, s_y.event(k))
            dve.wait_ge(s_y.sem, s_y.after(KT - 1))
            post_norm(("n6",), 3, "q")
            for t in range(2):
                for h in range(2):
                    dve.wait_ge(s_out_turned.sem, s_out_turned.after(t, h))
                    dve.tensor_copy(OB[:, t, 512 * h:512 * h + 512], ps[2 * t + h][:, :]).then_inc(s_turned_back.sem, s_turned_back.event(t, h))

        @block.tensor
        def _(pe):
            pe.wait_ge(s_consts.sem, s_consts.after("ident"))
            pe.wait_ge(s_prm, PRM_ALL)
            for b in range(RBLK):
                k = min(P, NROWS - b * P)
                o = pe.transpose(ps[0][:, b * P:b * P + k], prm[0:k, b, :], ident[0:k, 0:k])
            o.then_inc(s_prm_turned.sem, s_prm_turned.event())
            pe.wait_ge(s_x, 48)
            for k in range(KT):
                if k >= 4:
                    pe.wait_ge(s_xt.sem, s_xt.after(("x0",), k - 4))
                for t, (a, w) in enumerate(TOK):
                    o = pe.transpose(ps[1 + k % 4][:, a:a + w], xs[0:w, t, k * P:k * P + P], ident[0:w, 0:w])
                o.then_inc(s_x_turned.sem, s_x_turned.event(k))
            pe.wait_ge(s_consts.sem, s_consts.after("first"))
            pe.wait_ge(s_small, SMALL_ALL)
            pe.matmul(ps[6][:, 0:44], ones_1[0:1, :], rows44[0:1, :], start=True, stop=True).then_inc(s_bc.sem, s_bc.event())
            for l in range(DEPTH):
                key = ("n1", l)
                for k in range(KT if l == 0 else 0):
                    stat_average(pe, key, k)
                pe.wait_ge(s_logged.sem, s_logged.after(key))
                pe.wait_ge(s_normed.sem, s_normed.after(key, KT - 1))
                pe.wait_ge(s_bc44.sem, s_bc44.after())
                for k in range(KT):
                    o = pe.matmul(ps[7][0:8, 64:64 + T], wsm[:, l, k, 16:24], XN[:, k, :], start=(k == 0), stop=(k == KT - 1))
                o.then_inc(s_small_ff.sem, s_small_ff.event(l))
                for k in range(KT):
                    o = pe.matmul(ps[6][0:16, 0:T], wsm[:, l, k, 0:16], XN[:, k, :], start=(k == 0), stop=(k == KT - 1))
                o.then_inc(s_small_glr.sem, s_small_glr.event(l))
                for i, (name, h) in enumerate(IN_ORDER):
                    gemm(pe, ("in", l, i), key, T, tokens=name in ("gk", "gv", "fv"))
                    if i in ADA_IN:
                        pe.wait_ge(s_fz.sem, s_fz.after(l))
                        mod_columns(pe, ada_no(l, "in", i))
                for i in (9, 10, 11):
                    g = ("in", l, i)
                    drained(pe, g)
                pe.wait_ge(s_glr.sem, s_glr.after(l))
                A_, B_, M_ = slice(META, META + P), slice(META + P, T), slice(0, META)
                pe.matmul(ps[0][:, 0:256], glr1[:, A_], wa1[:, l, :], start=True, stop=True)
                pe.matmul(ps[0][:, 256:512], glr1[:, B_], wa1[:, l, :], start=True, stop=True)
                pe.matmul(ps[1][0:META, 0:256], glr1[:, M_], wa1[:, l, :], start=True, stop=True).then_inc(s_z.sem, s_z.event(l))
                pe.wait_ge(s_la.sem, s_la.after(l))
                pe.matmul(ps[2][:, 0:256], after[:, :], la[:, 1, :], start=True, stop=True)
                pe.matmul(ps[2][:, 256:512], after[:, :], la[:, 2, :], start=True, stop=True)
                pe.matmul(ps[3][0:META, 0:256], after[0:META, 0:META], la[0:META, 0, :], start=True, stop=True)
                for p in range(2):
                    for t in range(2):
                        c = p * 4 + 2 * t
                        o = pe.matmul(ps[6][:, c:c + 2], la[:, 1 + t, p * P:p * P + P], half[:, :], start=True, stop=True)
                o.then_inc(s_gla_d.sem, s_gla_d.event(l))
                pe.wait_ge(s_kd.sem, s_kd.after(l))
                for c, (t, r0_, rn) in enumerate(GLA_CHUNKS):
                    for p in range(2):
                        for hh in range(2):
                            rows = slice(r0_, r0_ + rn)
                            c0 = p * P if c == 0 else ((c - 1) // 2) * 256 + p * P
                            bank = ps[4] if c == 0 else ps[(c - 1) % 2]
                            o = pe.matmul(bank[64 * hh:64 * hh + 64, c0:c0 + P], kd[rows, t, p * P + 64 * hh:p * P + 64 * hh + 64],
                                          gvt[rows, t, (2 * p + hh) * P:(2 * p + hh + 1) * P], start=True, stop=True)
                o.then_inc(s_gla_u.sem, s_gla_u.event(l))
                for h in range(4):
                    p, hb = h // 2, 64 * (h % 2)
                    for c, (t, r0_, rn) in enumerate(GLA_CHUNKS):
                        pe.wait_ge(s_state.sem, s_state.after(l, c, p))
                        q0 = TOK[t][0] + r0_
                        o = pe.matmul(ps[GLA_BANK[h]][:, q0:q0 + rn], ST[hb:hb + 64, p, c, :], gqT[hb:hb + 64, p, q0:q0 + rn],
                                      start=True, stop=True)
                    o.then_inc(s_gla_o.sem, s_gla_o.event(l, h))
                for h in range(4):
                    stat_average(pe, ("g", l, h), 0)
                pe.wait_ge(s_negc.sem, s_negc.after(l))
                for s in range(FOX_H + 4):
                    if s < FOX_H:
                        h, p, hb = s, s // 2, 64 * (s % 2)
                        for q, (q0, qn) in enumerate(TOK):
                            b = ps[FOX_BANK[q]]
                            if s == 0:
                                pe.wait_ge(s_state.sem, s_state.after(l, 4, 1))
                            else:
                                pe.wait_ge(s_pexp.sem, s_pexp.after(l, s - 1, q))
                            end = q0 + qn
                            pe.matmul(b[0:qn, 0:end], fqT[hb:hb + 64, p, q0:end], fkT[hb:hb + 64, p, 0:end], start=True, stop=False)
                            pe.matmul(b[0:qn, 0:end], ident[0:8, h:h + 1].broadcast_to([8, qn]), negc[:, 0:end], start=False, stop=False)
                            o = pe.matmul(b[0:qn, q0:end], identb[0:qn, 0:qn], causal[0:qn, 0:qn], start=False, stop=True)
                            o.then_inc(s_scores.sem, s_scores.event(l, s, q))
                    if 1 <= s <= FOX_H:
                        h = s - 1
                        if h < 2:
                            for j in range(4):
                                pe.wait_ge(s_mixed.sem, s_mixed.after(l, j))
                        else:
                            pe.wait_ge(s_pt_copied.sem, s_pt_copied.after(l, h - 2))
                        if h >= 1:
                            pe.wait_ge(s_ptm_copied.sem, s_ptm_copied.after(l, h - 1))
                        for q in range(3):
                            pe.wait_ge(s_prob.sem, s_prob.after(l, h, q))
                        b, m_ = ps[2 + h % 2], ps[5]
                        pr = Pq[:, h % 2, :, :]
                        pe.transpose(b[:, 0:P], pr[:, 1, META:META + P], ident[:, :])
                        pe.transpose(b[:, P:2 * P], pr[:, 2, META:META + P], ident[:, :])
                        pe.transpose(b[:, 2 * P:3 * P], pr[:, 2, META + P:T], ident[:, :])
                        pe.transpose(m_[0:META, 0:META], pr[0:META, 0, 0:META], ident[0:META, 0:META])
                        pe.transpose(m_[0:META, META:META + P], pr[:, 1, 0:META], ident[:, :])
                        pe.transpose(m_[0:META, META + P:T], pr[:, 2, 0:META], ident[:, :]).then_inc(s_turned.sem, s_turned.event(l, h))
                    if 2 <= s <= FOX_H + 1:
                        h = s - 2
                        j, hb = h // 2, 64 * (h % 2)
                        if h % 2 == 0:
                            if j:
                                pe.wait_ge(s_fox_o.sem, s_fox_o.after(l, j - 1))
                        pe.wait_ge(s_pt_copied.sem, s_pt_copied.after(l, h))
                        pe.wait_ge(s_ptm_copied.sem, s_ptm_copied.after(l, h))
                        d = ps[6][hb:hb + 64, :]
                        cs = slice(64 * h, 64 * h + 64)
                        pe.matmul(d[:, 0:T], fvt[0:META, 0, cs], PTm[:, h % 2, :], start=True, stop=False)
                        pe.matmul(d[:, META:T], fvt[:, 1, cs], PTs[:, h % 2, 0:2 * P], start=False, stop=False)
                        pe.matmul(d[:, META + P:T], fvt[:, 2, cs], PTs[:, h % 2, 2 * P:3 * P], start=False, stop=True).then_inc(s_pv.sem, s_pv.event(l, h))
                    if s >= 4 and (s - 4) % 2 == 0 and (s - 4) // 2 < 4:
                        stat_average(pe, ("f", l, (s - 4) // 2), 0)
                for i in range(4):
                    if i == 0:
                        pe.wait_ge(s_x_lo.sem, s_x_lo.after(("mix", l), 3))
                    gemm(pe, ("out", l, i), ("mix", l), T)
                    if i:
                        for t in range(2):
                            stat_average(pe, ("n2", l), 2 * i - 2 + t)
                for t in range(2):
                    stat_average(pe, ("n2", l), 6 + t)
                for i in range(FT):
                    gemm(pe, ("up", l, i), ("n2", l), T)
                    if i in ADA_UP:
                        mod_columns(pe, ada_no(l, "up", i))
                key = ("n1", l + 1) if l + 1 < DEPTH else ("nf",)
                for i in range(4):
                    gemm(pe, ("down", l, i), None, T)
                    if i:
                        for t in range(2):
                            stat_average(pe, key, 2 * i - 2 + t)
                for t in range(2):
                    stat_average(pe, key, 6 + t)
            for k in range(KT):
                stat_average(pe, ("n3",), k)
            for i, (name, h) in enumerate(IN2_ORDER):
                gemm(pe, ("in2", 0, i), ("n3",), T2, tokens=name == "ih")
            for i in (8, 9, 10):
                g = ("in2", 0, i)
                drained(pe, g)
            pe.wait_ge(s_consts.sem, s_consts.after("second"))
            pe.wait_ge(s_ke.sem, s_ke.after())
            for t in range(2):
                for h in range(HG_H):
                    o = pe.transpose(ps[t][:, P * h:P * h + P], keT[:, h, P * t:P * t + P], ident[:, :])
                o.then_inc(s_ke_turned.sem, s_ke_turned.event(t))
                for h in range(HG_H):
                    tok = slice(P * t, P * t + P)
                    o = pe.matmul(ps[2 + t][:, P * h:P * h + P], kdT[:, h, tok], qh[:, h, tok], start=True, stop=True)
                o.then_inc(s_intra.sem, s_intra.event(t))

            def increments(t, n):
                for r_ in range(n):
                    for h in range(HG_H):
                        rows = slice(32 * r_, 32 * r_ + 32)
                        o = pe.matmul(ps[(4 if t == 0 else 0) + r_][:, P * h:P * h + P], ke[rows, t, h, :],
                                      ih[rows, t, P * h:P * h + P], start=True, stop=True)
                o.then_inc(s_hg_u.sem, s_hg_u.event(t))

            pe.wait_ge(s_ke_copied.sem, s_ke_copied.after(0))
            pe.wait_ge(s_logged.sem, s_logged.after(("n3",)))
            increments(0, 4)
            for t in range(2):
                pe.wait_ge(s_ke_copied.sem, s_ke_copied.after(t))
            for t in range(2):
                o = pe.transpose(ps[0][:, P * t:P * t + P], vaT[:, P * t:P * t + P], ident[:, :])
            o.then_inc(s_va_turned.sem, s_va_turned.event())
            pe.wait_ge(s_va.sem, s_va.after())
            pe.wait_ge(s_a_copied.sem, s_a_copied.after(1))
            increments(1, 3)
            pe.wait_ge(s_hg_s.sem, s_hg_s.after(3))
            for h in range(HG_H):
                b = ps[HG_BANK[h]]
                for t in range(2):
                    a = P * t
                    last = t == 1 and False
                    pe.matmul(b[:, a:a + P], ih[:, t, P * h:P * h + P], At[:, t, h, :], start=True, stop=False,
                              skip_group_check=True)
                    for c in range(4 * t, 4 * t + 4):
                        if c == 0:
                            continue
                        pe.wait_ge(s_hg_s.sem, s_hg_s.after(c - 1))
                        q0 = c * HG_C
                        o = pe.matmul(b[:, q0:q0 + HG_C], SS[:, c - 1, h, :], qh[:, h, q0:q0 + HG_C], start=False,
                                      stop=(c == 4 * t + 3), skip_group_check=True)
                o.then_inc(s_hg_o.sem, s_hg_o.event(h))
            for h in range(HG_H):
                if h == 0:
                    pass
                stat_average(pe, ("h", h), 0)
            pe.wait_ge(s_hg_s.sem, s_hg_s.after(6))
            for s in range(ATT_H + 3):
                if s < ATT_H:
                    h = HEADS[s]
                    j, g_ = h % 4, h // 4
                    hb = 64 * g_
                    for q in range(2):
                        if s >= 2:
                            pe.wait_ge(s_pexp2.sem, s_pexp2.after(s - 2, q))
                        elif s == 1:
                            pe.wait_ge(s_mixed2.sem, s_mixed2.after(7))
                        b = ps[2 * (s % 2) + q][:, 0:P * (q + 1)]
                        pe.matmul(b, qaT[hb:hb + 64, j, P * q:P * q + P], kaT[hb:hb + 64, 0:P * (q + 1)], start=True, stop=False)
                        o = pe.matmul(b, slope_i[:, h, :], dist[:, P * (1 - q):2 * P], start=False, stop=True)
                        o.then_inc(s_scores2.sem, s_scores2.event(s, q))
                if 1 <= s <= ATT_H:
                    n = s - 1
                    if n >= 2:
                        pe.wait_ge(s_pt2.sem, s_pt2.after(n - 2))
                    else:
                        for h in range(HG_H):
                            pe.wait_ge(s_mixed2.sem, s_mixed2.after(4 + h))
                    for q in range(2):
                        pe.wait_ge(s_prob2.sem, s_prob2.after(n, q))
                    b = ps[4 + n % 2]
                    for t in range(3):
                        o = pe.transpose(b[:, P * t:P * t + P], P2[:, n % 2, P * t:P * t + P], ident[:, :])
                    o.then_inc(s_turned2.sem, s_turned2.event(n))
                if 2 <= s <= ATT_H + 1:
                    n = s - 2
                    g_ = HEADS[n] // 4
                    if n % 2 == 0 and n:
                        pe.wait_ge(s_att_o.sem, s_att_o.after(n // 2 - 1))
                    pe.wait_ge(s_pt2.sem, s_pt2.after(n))
                    d = ps[6][64 * g_:64 * g_ + 64, :]
                    pe.matmul(d[:, 0:T2], va[:, 0, 64 * g_:64 * g_ + 64], PT2[:, n % 2, 0:2 * P], start=True, stop=False)
                    pe.matmul(d[:, P:T2], va[:, 1, 64 * g_:64 * g_ + 64], PT2[:, n % 2, 2 * P:3 * P],
                                             start=False, stop=True).then_inc(s_pv2.sem, s_pv2.event(n))
            for j in range(4):
                stat_average(pe, ("att",), j)
            pe.wait_ge(s_x_lo.sem, s_x_lo.after(("mix2",), 3))
            for i in range(4):
                gemm(pe, ("out2", 0, i), ("mix2",), T2)
                if i:
                    for t in range(2):
                        stat_average(pe, ("n4",), 2 * i - 2 + t)
            for t in range(2):
                stat_average(pe, ("n4",), 6 + t)
            for k in range(KT):
                stat_average(pe, ("n5",), k)
            pe.wait_ge(s_normed.sem, s_normed.after(("n5",), KT - 1))
            pe.wait_ge(s_logged.sem, s_logged.after(("n5",)))
            for i in range(4):
                drained(pe, ("out2", 0, i))
            for t in range(2):
                d = ps[0][:, 64 * t:64 * t + 36]
                for k in range(KT):
                    pe.matmul(d, XN[:, k, P * t:P * t + P], wr[:, k, :], start=(k == 0), stop=False)
                o = pe.matmul(d, ones_1[0:1, :], rows44[0:1, 0:36], start=False, stop=True)
            o.then_inc(s_routed.sem, s_routed.event())
            for t in range(2):
                pe.wait_ge(s_wt.sem, s_wt.after(t))
                o = pe.transpose(ps[1][0:NEXP, P * t:P * t + P], wt[:, t, :], ident[:, :])
            o.then_inc(s_wt_turned.sem, s_wt_turned.event())
            pe.wait_ge(s_WT.sem, s_WT.after())
            pe.wait_ge(s_x_lo.sem, s_x_lo.after(("n5",), KT - 1))

            def down(e):
                n = CHUNK_NO[(("dn", 0, e), 0)]
                pe.wait_ge(s_w_lo.sem, s_w_lo.after(CHUNKS[n]))
                pe.wait_ge(s_hu_lo.sem, s_hu_lo.after(e))
                fl = lambda t: t[:, :, :].rearrange("p a b -> p (a b)").rearrange("p (k n) -> p k n", k=2)
                h, lo = fl(whi[n % SPLIT]), fl(wlo[n % SPLIT])
                for mt in range(KT):
                    for k in range(2):
                        d = ps[mt // 2][:, T2 * (mt % 2):T2 * (mt % 2) + T2]
                        c = slice(P * mt, P * mt + P)
                        x = slice(T2 * k, T2 * k + T2)
                        mm = product(pe, d, h[:, k, c], lo[:, k, c], huh[:, e % 2, x], hul[:, e % 2, x],
                                     e == 0 and k == 0 and mt % 2 == 0, e == NEXP - 1 and k == 1, skip_group_check=True)
                mm.then_inc(s_w_used.sem, s_w_used.event(CHUNKS[n]))

            for e in range(NEXP):
                for kind, b in (("gate", ps[4]), ("upx", ps[5])):
                    n = CHUNK_NO[((kind, 0, e), 0)]
                    pe.wait_ge(s_w_lo.sem, s_w_lo.after(CHUNKS[n]))
                    if e:
                        pe.wait_ge(s_hu.sem, s_hu.after(e - 1))
                    if kind == "gate":
                        pe.matmul(ps[6][:, 0:T2], ident[0:NEXP, e:e + 1].broadcast_to([NEXP, P]), WT[:, :],
                                                     start=True, stop=True).then_inc(s_weighed.sem, s_weighed.event(e))
                    h, lo = whi[n % SPLIT], wlo[n % SPLIT]
                    for mt in range(2):
                        for k in range(KT):
                            c = slice(P * mt, P * mt + P)
                            mm = product(pe, b[:, T2 * mt:T2 * mt + T2], h[:, k, c], lo[:, k, c], xhi[:, k, 0:T2], xlo[:, k, 0:T2],
                                         k == 0, k == KT - 1)
                    mm.then_inc(s_w_used.sem, s_w_used.event(CHUNKS[n]))
                down(e)
            for k in range(KT):
                stat_average(pe, ("n6",), k)
            for t in range(2):
                for h in range(2):
                    for j in range(4):
                        k = 4 * h + j
                        pe.wait_ge(s_xt.sem, s_xt.after(("q",), k))
                        o = pe.transpose(ps[2 * t + h][:, P * j:P * j + P], XT[:, k, META + P * t:META + P * t + P], ident[:, :])
                    o.then_inc(s_out_turned.sem, s_out_turned.event(t, h))
    return orders


_INS = ["x", "meta_tokens", "attn_norm", "w_in", "w_alpha_up", "b_alpha", "b_forget", "gla_norm", "fox_norm", "w_out",
        "ffn_norm", "w_up", "conv_w", "conv_b", "w_down", "final_norm", "c_2", "ln1_pre_2", "ln1_post_2", "ln2_pre_2",
        "ln2_post_2", "w_ada_2", "b_ada_2", "w_in_2", "attn_sinks_2", "attn_out_norm_2", "hgrn_lb_2",
        "hgrn_out_norm_2", "w_out_2", "w_router_group_2", "b_router_group_2", "w_router_expert_2", "b_router_expert_2",
        "w_exp_gate_2", "w_exp_up_2", "w_exp_down_2"]


def kernel(**inputs):
    import numpy as _np
    import concourse.bacc as _bacc
    from concourse import mybir as _mybir
    from concourse.bass_utils import run_bass_kernel_spmd as _run

    arrays = {f"in_{n}": _np.ascontiguousarray(inputs[n]) for n in _INS}

    def program(known):
        nc = _bacc.Bacc("TRN2", target_bir_lowering=False, num_devices=1)
        args = {n: nc.dram_tensor(f"in_{n}", arrays[f"in_{n}"].shape, _mybir.dt.from_np(arrays[f"in_{n}"].dtype),
                                  kind="ExternalInput").ap() for n in _INS}
        out = nc.dram_tensor("out_0", (1, T2, D), _mybir.dt.float32, kind="ExternalOutput").ap()
        return nc, build(nc, args, out, known)

    _, order = program(None)
    nc, _ = program(order)
    r = _run(nc, [arrays], core_ids=[0])
    return r.results[0]["out_0"]
```

```python
from contextlib import ExitStack

import concourse.bass as bass
from concourse import mybir

F32 = mybir.dt.float32
F32R = mybir.dt.float32r
BF16 = mybir.dt.bfloat16
I32 = mybir.dt.int32
U32 = mybir.dt.uint32
ALU = mybir.AluOpType
ACT = mybir.ActivationFunctionType
AX_X = mybir.AxisListType.X

P = 128
DEPTH = 2
META = 16
T = 272
T2 = 256
D = 1024
KT = D // P
EPS = 1e-6
DFF = 2816
FT = DFF // P
FOX_H = 8
TOK = [(0, META), (META, P), (META + P, P)]
GLA_CHUNKS = [(0, 0, META), (1, 0, 64), (1, 64, 64), (2, 0, 64), (2, 64, 64)]
ATT_H = 8
HG_H = 4
HG_C = 32
NEXP = 32
GLA_BANK = [2, 3, 5, 6]
FOX_BANK = [0, 1, 4]
HG_BANK = [4, 5, 6, 3]
HEADS = [0, 4, 1, 5, 2, 6, 3, 7]
CW = 256
RAW = 4
SPLIT = 2
BIG = 1.0e30
IN_AT = {"gq": 0, "gk": 256, "gv": 512, "gr": 1024, "glr": 1536, "fq": 1552, "fk": 2064, "fv": 2576, "ff": 3088}
IN_ORDER = [("gk", 0), ("gv", 0), ("gv", 1), ("gq", 0), ("gr", 0), ("gr", 1),
            ("fv", 0), ("fv", 1), ("fk", 0), ("fk", 1), ("fq", 0), ("fq", 1)]
IN2_AT = {"qa": 0, "ka": 512, "qh": 768, "fh": 1280, "ih": 1792, "gh": 2304}
IN2_ORDER = [("fh", 0), ("fh", 1), ("qh", 0), ("qh", 1), ("gh", 0), ("gh", 1), ("ih", 0), ("ih", 1),
             ("ka", 0), ("qa", 0), ("qa", 1)]
UP_FROM = [0] * (DEPTH - 1) + [META - 2]
DOWN_FROM = [0] * (DEPTH - 1) + [META]
DOWN_K = [(0, 8), (8, 7), (15, 7)]

ROWS = {}


def _rows():
    at = 0
    for name, n in (("conv_w", 3 * DEPTH * 2 * FT), ("conv_b", DEPTH * 2 * FT), ("attn_norm", 16), ("ffn_norm", 16),
                    ("gla_norm", 8), ("fox_norm", 8), ("final_norm", 8), ("c", 8), ("ln1_pre", 8), ("ln1_post", 8),
                    ("ln2_pre", 8), ("ln2_post", 8), ("b_ada", 48), ("attn_out_norm", 4), ("hgrn_lb", 8),
                    ("hgrn_out_norm", 4)):
        ROWS[name] = (at, n)
        at += n
    return at


NROWS = _rows()
RBLK = -(-NROWS // P)


def gemm_groups():
    out = []
    for l in range(DEPTH):
        out += [("in", l, i) for i in range(len(IN_ORDER))]
        out += [("out", l, i) for i in range(4)]
        out += [("up", l, i) for i in range(FT)]
        out += [("down", l, i) for i in range(4)]
    out += [("in2", 0, i) for i in range(len(IN2_ORDER))]
    out += [("out2", 0, i) for i in range(4)]
    return out


GROUPS = gemm_groups()


def chunk_list():
    out = []
    for g in GROUPS:
        out += [(g, j) for j in range(3 if g[0] == "down" else 1)]
    out += [(("gate", 0, 0), 0), (("upx", 0, 0), 0)]
    for e in range(1, NEXP):
        out += [(("gate", 0, e), 0), (("dn", 0, e - 1), 0), (("upx", 0, e), 0)]
    out += [(("dn", 0, NEXP - 1), 0)]
    return out


CHUNKS = chunk_list()
CHUNK_NO = {c: n for n, c in enumerate(CHUNKS)}
EXPERTS_AT = CHUNK_NO[(("gate", 0, 0), 0)]
SLOT = [n % SPLIT if n < EXPERTS_AT else (n - EXPERTS_AT + 2) % (SPLIT + 1) for n in range(len(CHUNKS))]
LAST_IN_SLOT = [max([m for m in range(n) if SLOT[m] == SLOT[n]], default=None) for n in range(len(CHUNKS))]


class Signal:

    def __init__(self, sem, order, known):
        self.sem, self.order, self.known = sem, order, known

    @staticmethod
    def flat(key):
        return sum((Signal.flat(k) if isinstance(k, tuple) else (k,) for k in key), ())

    def event(self, *key):
        self.order.append(self.flat(key))
        return 1

    def after(self, *key):
        return 1 if self.known is None else self.known[self.flat(key)] + 1


def build(nc, A, out, known):
    orders = {}
    with ExitStack() as ctx:
        def sem(name):
            return ctx.enter_context(nc.semaphore(name))

        def signal(name):
            orders[name] = []
            numbers = None if known is None else {k: n for n, k in enumerate(known[name])}
            return Signal(sem("s_" + name), orders[name], numbers)

        top = [-(-nc.sbuf_base // 64) * 64]

        def sb(name, shape, dt=F32, at=None):
            n = 2 if dt == BF16 else 4
            for s in shape[1:]:
                n *= s
            if at is None:
                off, top[0] = top[0], top[0] + -(-n // 32) * 32
            else:
                off, at[0] = at[0], at[0] + -(-n // 32) * 32
                assert at[0] <= at[1], name
            return nc.alloc_sbuf_tensor_at(name, list(shape), dt, offset=off)

        raw = [sb(f"raw{i}", [P, 8, CW]) for i in range(RAW)]
        whi = [sb(f"whi{i}", [P, 8, CW], F32R) for i in range(SPLIT)]
        wlo = [sb(f"wlo{i}", [P, 8, CW], F32R) for i in range(SPLIT)]
        ada_at = top[0]
        ada = [sb(f"ada{i}", [P, 8, CW]) for i in range(2)]
        m = [ada_at, ada_at + 2 * 8 * CW * 4]
        whi.append(sb("whi_x", [P, 8, CW], F32R, at=m))
        wlo.append(sb("wlo_x", [P, 8, CW], F32R, at=m))
        XT, XN = sb("XT", [P, KT, T]), sb("XN", [P, KT, T])
        xhi, xlo = sb("xhi", [P, KT, T], F32R), sb("xlo", [P, KT, T], F32R)
        mix_at = top[0]
        hhi, hlo = sb("hhi", [P, FT, T], F32R), sb("hlo", [P, FT, T], F32R)
        mix_end = top[0]
        sq = sb("sq", [P, 4, T])
        rs = sb("rs", [P, 2, T])
        ident, ones_1 = sb("ident", [P, P]), sb("ones_1", [P, P])
        ones_d, ones_v, ones_a, ones_f = (sb(n, [P, P]) for n in ("ones_d", "ones_v", "ones_a", "ones_f"))
        after = sb("after", [P, P])
        half = sb("half", [P, 2])
        identb, causal = sb("identb", [P, P], BF16), sb("causal", [P, P], BF16)
        same_c = sb("same_c", [P, P])
        restart = sb("restart", [P, T2])
        onesrow = sb("onesrow", [8, T])
        slope_i = sb("slope_i", [P, ATT_H, P], BF16)
        dist = sb("dist", [P, 2 * P], BF16)
        iota8 = sb("iota8", [P, 8])
        PC = sb("PC", [P, RBLK * P])
        wsm = sb("wsm", [P, DEPTH, KT, 24])
        wa1 = sb("wa1", [17, DEPTH, 256])
        bfo = sb("bfo", [8, DEPTH])
        wr = sb("wr", [P, KT, 36])
        rows44 = sb("rows44", [1, 44])
        bc44 = sb("bc44", [P, 44])
        epst = sb("epst", [P, 1])
        mod = sb("mod", [P, 48])
        gsc = sb("gsc", [P, 4, KT])
        cact = sb("cact", [P, KT])
        lbt = sb("lbt", [P, 5, 8])
        adr = sb("adr", [P, 2, CW])
        cv = sb("cv", [P, 2, 2, T])
        hf = sb("hf", [P, 2, T])
        glr1 = sb("glr1", [17, T])
        fz, fl, negc = sb("fz", [8, T]), sb("fl", [8, T]), sb("negc", [8, T])
        nmx, psm, pri = sb("nmx", [P, 24]), sb("psm", [P, 24]), sb("pri", [P, 24])
        keT, kdT = sb("keT", [P, HG_H, T2]), sb("kdT", [P, HG_H, T2])
        assert top[0] <= nc.sbuf_usable_end

        m = [mix_at, mix_end]
        gkt, gvt, fvt = sb("gkt", [P, 3, 256], at=m), sb("gvt", [P, 3, 512], at=m), sb("fvt", [P, 3, 512], at=m)
        gqT, grT = sb("gqT", [P, 2, T], at=m), sb("grT", [P, 4, T], at=m)
        fqT, fkT = sb("fqT", [P, 4, T], at=m), sb("fkT", [P, 4, T], at=m)
        rest = m[0]
        Pq, PTs, PTm = sb("Pq", [P, 2, 3, T], at=m), sb("PTs", [P, 2, 384], at=m), sb("PTm", [META, 2, T], at=m)
        m = [rest, mix_end]
        la, kd, ST = sb("la", [P, 3, 256], at=m), sb("kd", [P, 3, 256], at=m), sb("ST", [P, 2, 5, P], at=m)
        dec = sb("dec", [P, 8], at=m)
        m = [mix_at, mix_end]
        xs, prm = sb("xs", [P, 3, D], at=m), sb("prm", [P, RBLK, P], at=m)
        m = [mix_at, mix_end]
        qh, fh, gh, kh = (sb(n, [P, HG_H, T2], at=m) for n in ("qh", "fh", "gh", "kh"))
        bb, ih = sb("bb", [P, HG_H, T2], at=m), sb("ih", [P, 2, 512], at=m)
        qaT, kaT, vaT = sb("qaT", [P, 4, T2], at=m), sb("kaT", [P, T2], at=m), sb("vaT", [P, T2], at=m)
        ke, At, va = sb("ke", [P, 2, HG_H, P], at=m), sb("At", [P, 2, HG_H, P], at=m), sb("va", [P, 2, P], at=m)
        P2, PT2 = sb("P2", [P, 2, 384], at=m), sb("PT2", [P, 2, 384], at=m)
        m = [ada_at, ada_at + 2 * 8 * CW * 4]
        SS = sb("SS", [P, 7, HG_H, P], at=m)
        m = [mix_at, mix_end]
        rt = sb("rt", [P, 2, 160], at=m)
        wt = sb("wt", [P, 2, NEXP], at=m)
        WT = sb("WT", [NEXP, T2], at=m)
        sg, hu = sb("sg", [P, 2, 512], at=m), sb("hu", [P, 2, 512], at=m)
        huh, hul = sb("huh", [P, 2, 512], F32R, at=m), sb("hul", [P, 2, 512], F32R, at=m)
        OB = sb("OB", [P, 2, D], at=m)
        WTh, WTl = sb("WTh", [NEXP, T2], F32R, at=m), sb("WTl", [NEXP, T2], F32R, at=m)
        identr = sb("identr", [NEXP, NEXP], F32R, at=m)

        ps = [ctx.enter_context(nc.psum_tensor(f"ps{i}", [P, 512], F32)) for i in range(8)]
        SUM = ps[7][:, 64:64 + T]

        s_raw = [sem(f"s_raw{i}") for i in range(RAW)]
        s_ada = [sem(f"s_ada{i}") for i in range(2)]
        s_x = sem("s_x")
        s_prm = sem("s_prm")
        s_small = sem("s_small")
        s_out = sem("s_out")

        s_xt = signal("xt")
        s_convolved = signal("convolved")
        s_mixout = signal("mixout")
        s_normed = signal("normed")
        s_scaled = signal("scaled")
        s_mixed = signal("mixed")
        s_scaled_n = signal("scaled_n")
        s_scaled2 = signal("scaled2")
        s_mixed2 = signal("mixed2")
        s_post = signal("post")
        s_averaged = signal("averaged")
        s_logged = signal("logged")
        s_squared = signal("squared")
        s_w_used = signal("w_used")
        s_w_hi = signal("w_hi")
        s_x_hi = signal("x_hi")
        s_w_lo = signal("w_lo")
        s_x_lo = signal("x_lo")
        s_h_lo = signal("h_lo")
        s_ada_sum = signal("ada_sum")
        s_turned_back = signal("turned_back")
        s_filled = signal("filled")
        s_consts = signal("consts")
        s_ada_mul = signal("ada_mul")
        s_ada_four = signal("ada_four")
        s_ada_two = signal("ada_two")
        s_ada_used = signal("ada_used")
        s_cact = signal("cact")
        s_gated = signal("gated")
        s_params = signal("params")
        s_fz = signal("fz")
        s_fl1 = signal("fl1")
        s_fl2 = signal("fl2")
        s_z = signal("z")
        s_gla_d = signal("gla_d")
        s_gla_o = signal("gla_o")
        s_nmax = signal("nmax")
        s_turned = signal("turned")
        s_pv = signal("pv")
        s_fox_o = signal("fox_o")
        s_hidden = signal("hidden")
        s_lb_sub = signal("lb_sub")
        s_forget = signal("forget")
        s_cum = signal("cum")
        s_end_sub = signal("end_sub")
        s_hg_o = signal("hg_o")
        s_nmax2 = signal("nmax2")
        s_turned2 = signal("turned2")
        s_pv2 = signal("pv2")
        s_att_o = signal("att_o")
        s_r_sub = signal("r_sub")
        s_hu = signal("hu")
        s_y = signal("y")
        s_rooted = signal("rooted")
        s_prm_turned = signal("prm_turned")
        s_x_turned = signal("x_turned")
        s_bc = signal("bc")
        s_small_ff = signal("small_ff")
        s_small_glr = signal("small_glr")
        s_fl3 = signal("fl3")
        s_lf = signal("lf")
        s_zc = signal("zc")
        s_gla_e = signal("gla_e")
        s_gla_u = signal("gla_u")
        s_state = signal("state")
        s_scores = signal("scores")
        s_pexp = signal("pexp")
        s_recip = signal("recip")
        s_tap2 = signal("tap2")
        s_tap1 = signal("tap1")
        s_h_hi = signal("h_hi")
        s_mod = signal("mod")
        s_shifted = signal("shifted")
        s_root_sq = signal("root_sq")
        s_mean3 = signal("mean3")
        s_lb_max = signal("lb_max")
        s_gsc = signal("gsc")
        s_lb_exp = signal("lb_exp")
        s_lb_sum = signal("lb_sum")
        s_lb_rec = signal("lb_rec")
        s_lb = signal("lb")
        s_lb1 = signal("lb1")
        s_lb2 = signal("lb2")
        s_drained_act = signal("drained_act")
        s_kh = signal("kh")
        s_logf = signal("logf")
        s_exp_b = signal("exp_b")
        s_exp_nb = signal("exp_nb")
        s_exp_end = signal("exp_end")
        s_ke_turned = signal("ke_turned")
        s_intra = signal("intra")
        s_va_turned = signal("va_turned")
        s_hg_u = signal("hg_u")
        s_hg_s = signal("hg_s")
        s_bc44 = signal("bc44")
        s_scores2 = signal("scores2")
        s_nmaxa = signal("nmaxa")
        s_pexp2 = signal("pexp2")
        s_den2 = signal("den2")
        s_rec2 = signal("rec2")
        s_routed = signal("routed")
        s_r = signal("r")
        s_r_exp = signal("r_exp")
        s_wt_turned = signal("wt_turned")
        s_e_gate = signal("e_gate")
        s_weighed = signal("weighed")
        s_sgw = signal("sgw")
        s_hu_lo = signal("hu_lo")
        s_hu_hi = signal("hu_hi")
        s_out_turned = signal("out_turned")
        s_glr = signal("glr")
        s_la = signal("la")
        s_kd = signal("kd")
        s_negc = signal("negc")
        s_pt_copied = signal("pt_copied")
        s_ptm_copied = signal("ptm_copied")
        s_prob = signal("prob")
        s_ke = signal("ke")
        s_ke_copied = signal("ke_copied")
        s_va = signal("va")
        s_a_copied = signal("a_copied")
        s_pt2 = signal("pt2")
        s_prob2 = signal("prob2")
        s_wt = signal("wt")
        s_WT = signal("WT")
        s_wt_hi = signal("wt_hi")
        s_wt_lo = signal("wt_lo")
        s_drained_dve = signal("drained_dve")
        s_qd = signal("qd")
        s_kd2 = signal("kd2")
        s_za = signal("za")
        s_zb = signal("zb")

        def col(name, i, n=1):
            a = ROWS[name][0] + i
            return PC[:, a:a + n]

        def pair(g):
            return 2 * (GROUPS.index(g) % 3)

        ACT_DRAINS = {"gv", "gr", "fv", "fq", "fh", "qh", "gh", "ka"}

        def drained(eng, g):
            kind, l, i = g
            if kind in ("out", "down"):
                eng.wait_ge(s_xt.sem, s_xt.after("o" if kind == "out" else "d", l, 2 * i + 1))
            elif kind == "up":
                eng.wait_ge(s_convolved.sem, s_convolved.after(l, i))
            elif kind == "out2":
                eng.wait_ge(s_mixout.sem, s_mixout.after(2 * i + 1))
            else:
                name = (IN_ORDER if kind == "in" else IN2_ORDER)[i][0]
                if name in ACT_DRAINS:
                    eng.wait_ge(s_drained_act.sem, s_drained_act.after(g))
                else:
                    eng.wait_ge(s_drained_dve.sem, s_drained_dve.after(g))

        def root_read(eng, key):
            kind = key[0]
            if kind in ("n1", "n2"):
                eng.wait_ge(s_normed.sem, s_normed.after(key, KT - 1))
            elif kind == "g":
                eng.wait_ge(s_scaled.sem, s_scaled.after(key[1:]))
            elif kind == "f":
                eng.wait_ge(s_mixed.sem, s_mixed.after(key[1], 4 + key[2]))
            elif kind == "nf":
                eng.wait_ge(s_xt.sem, s_xt.after("f", KT - 1))
            elif kind in ("n3", "n5"):
                eng.wait_ge(s_scaled_n.sem, s_scaled_n.after(key, KT - 1))
            elif kind == "h":
                eng.wait_ge(s_scaled2.sem, s_scaled2.after(key[1]))
            elif kind == "att":
                eng.wait_ge(s_mixed2.sem, s_mixed2.after(3))
            else:
                eng.wait_ge(s_post.sem, s_post.after(key, KT - 1))

        def kp(w):
            return w.rearrange("(k p) n -> p k n", p=P)

        def pieces(n):
            (kind, l, i), j = CHUNKS[n]
            dst = raw[n % RAW]
            if kind == "in":
                name, h = IN_ORDER[i]
                c0 = IN_AT[name] + CW * h
                return [(dst[:, :, :], kp(A["w_in"][l])[:, :, c0:c0 + CW])]
            if kind == "out":
                return [(dst[:, :, :], kp(A["w_out"][l])[:, :, CW * i:CW * (i + 1)])]
            if kind == "up":
                w = kp(A["w_up"][l])
                return [(dst[:, :, P * h:P * (h + 1)], w[:, :, DFF * h + P * i:DFF * h + P * (i + 1)]) for h in range(2)]
            if kind == "down":
                k0, nk = DOWN_K[j]
                return [(dst[:, 0:nk, :], kp(A["w_down"][l])[:, k0:k0 + nk, CW * i:CW * (i + 1)])]
            if kind == "in2":
                name, h = IN2_ORDER[i]
                w = A["w_in_2"][0]
                if name == "qa":
                    v = w[:, 0:512].rearrange("(k p) (g t d) -> p k g t d", p=P, g=2, d=64)
                    return [(dst[:, :, P * t + 64 * g:P * t + 64 * g + 64], v[:, :, g, 2 * h + t, :])
                            for t in range(2) for g in range(2)]
                c0 = IN2_AT[name] + CW * h
                return [(dst[:, :, :], kp(w)[:, :, c0:c0 + CW])]
            if kind == "out2":
                cs = slice(CW * i, CW * (i + 1))
                w = A["w_out_2"][0]
                v = w[0:512, cs].rearrange("(g t d) n -> g d t n", g=2, d=64)
                return [(dst[64 * g:64 * g + 64, 0:4, :], v[g]) for g in range(2)] + \
                       [(dst[:, 4:8, :], kp(w)[:, 4:8, cs])]
            if kind == "dn":
                flat = dst[:, :, :].rearrange("p a b -> p (a b)").rearrange("p (k n) -> p k n", k=2)
                return [(flat, kp(A["w_exp_down_2"][0, i]))]
            w = A["w_exp_gate_2" if kind == "gate" else "w_exp_up_2"]
            return [(dst[:, :, :], kp(w[0, i]))]

        landed_at, total = [], [0] * RAW
        for n in range(len(CHUNKS)):
            total[n % RAW] += 16 * len(pieces(n))
            landed_at.append(total[n % RAW])

        def k_tiles(n):
            (kind, _, _), j = CHUNKS[n]
            return DOWN_K[j][1] if kind == "down" else 8


        def v2(name):
            return A[name].rearrange("l (a p) -> (l a) p", p=P)

        row_srcs = [("conv_w", A["conv_w"].rearrange("l j (a p) -> (l j a) p", p=P)), ("conv_b", v2("conv_b")),
                    ("attn_norm", v2("attn_norm")), ("ffn_norm", v2("ffn_norm")), ("gla_norm", v2("gla_norm")),
                    ("fox_norm", v2("fox_norm")), ("final_norm", A["final_norm"].rearrange("(a p) -> a p", p=P)),
                    ("c", v2("c_2"))] + [(nm, v2(nm + "_2")) for nm in
                    ("ln1_pre", "ln1_post", "ln2_pre", "ln2_post", "b_ada", "hgrn_lb", "hgrn_out_norm")]
        row_dmas = []
        for name, src in row_srcs:
            at, cnt = ROWS[name]
            done = 0
            while done < cnt:
                b, r = divmod(at + done, P)
                k = min(cnt - done, P - r)
                row_dmas.append((prm[r:r + k, b, :], src[done:done + k, :]))
                done += k
        b0, r0 = divmod(ROWS["attn_out_norm"][0], P)
        aon = A["attn_out_norm_2"].rearrange("l (g j d) -> (l g) j d", g=2, d=64)
        row_dmas += [(prm[r0:r0 + 4, b0, 64 * g:64 * g + 64], aon[g]) for g in range(2)]
        PRM_ALL = 16 * len(row_dmas)
        small_dmas = []
        for l in range(DEPTH):
            wv = kp(A["w_in"][l])
            small_dmas += [(wsm[:, l, :, 0:16], wv[:, :, IN_AT["glr"]:IN_AT["glr"] + 16]),
                           (wsm[:, l, :, 16:24], wv[:, :, IN_AT["ff"]:IN_AT["ff"] + 8]),
                           (wa1[0:16, l, :], A["w_alpha_up"][l]), (wa1[16:17, l, :], A["b_alpha"][l:l + 1, :]),
                           (bfo[:, l:l + 1], A["b_forget"][l:l + 1, :].rearrange("l h -> h l"))]
        small_dmas += [(wr[:, :, 0:4], kp(A["w_router_group_2"][0])), (wr[:, :, 4:36], kp(A["w_router_expert_2"][0])),
                       (rows44[:, 0:4], A["b_router_group_2"]), (rows44[:, 4:36], A["b_router_expert_2"]),
                       (rows44[:, 36:44], A["attn_sinks_2"])]
        SMALL_ALL = 16 * len(small_dmas)


        STATS = []
        for l in range(DEPTH):
            STATS += [(("n1", l), KT, ones_d, T)]
            STATS += [(("g", l, h), 1, ones_v, T) for h in range(4)] + [(("f", l, j), 1, ones_f, T) for j in range(4)]
            STATS += [(("n2", l), KT, ones_d, T)]
        STATS += [(("nf",), KT, ones_d, T2), (("n3",), KT, ones_d, T2)]
        STATS += [(("h", h), 1, ones_v, T2) for h in range(HG_H)]
        STATS += [(("att",), 4, ones_a, T2), (("n4",), KT, ones_d, T2), (("n5",), KT, ones_d, T2), (("n6",), KT, ones_d, T2)]
        STAT_NO = {s[0]: n for n, s in enumerate(STATS)}
        SQ_ORDER = [(s[0], i) for s in STATS if s[0] not in (("nf",), ("n3",)) for i in range(s[1])]
        first = SQ_ORDER.index((("h", 0), 0))
        SQ_ORDER[first:first] = [(k_, i) for i in range(KT) for k_ in (("nf",), ("n3",))]
        SQ_NO = {k: n for n, k in enumerate(SQ_ORDER)}
        SQ_KEYS = list(SQ_NO)

        def stat_square(act, key, i, src, **k_):
            n = SQ_NO[(key, i)]
            if n >= 4:
                act.wait_ge(s_averaged.sem, s_averaged.after(*SQ_KEYS[n - 4]))
            w = STATS[STAT_NO[key]][3]
            act.activation(sq[:, n % 4, 0:w], src, ACT.Square, **k_).then_inc(s_squared.sem, s_squared.event(key, i))

        def stat_average(pe, key, i):
            no = STAT_NO[key]
            _, n, ones, w = STATS[no]
            if key == ("n3",):
                SUM_ = ps[6]
                if i == 0:
                    pe.wait_ge(s_fox_o.sem, s_fox_o.after(DEPTH - 1, 3))
            else:
                SUM_ = SUM
            if i == 0 and no and key != ("n3",):
                pe.wait_ge(s_logged.sem, s_logged.after(STATS[no - 1][0]))
            pe.wait_ge(s_squared.sem, s_squared.after(key, i))
            pe.matmul(SUM_[:, 0:w], ones[:, :], sq[:, SQ_NO[(key, i)] % 4, 0:w],
                                          start=(i == 0), stop=(i == n - 1)).then_inc(s_averaged.sem, s_averaged.event(key, i))

        def stat_root(act, key):
            no = STAT_NO[key]
            _, n, _, w = STATS[no]
            act.wait_ge(s_averaged.sem, s_averaged.after(key, n - 1))
            if no >= 2:
                root_read(act, STATS[no - 2][0])
            r = rs[:, no % 2, 0:w]
            act.activation(r, SUM[:, 0:w], ACT.Ln, bias=epst[:, 0:1]).then_inc(s_logged.sem, s_logged.event(key))
            act.wait_ge(s_logged.sem, s_logged.after(key))
            act.activation(r, r, ACT.Exp, scale=-0.5).then_inc(s_rooted.sem, s_rooted.event(key))

        def RS(key):
            no = STAT_NO[key]
            return rs[:, no % 2, 0:STATS[no][3]]

        hi_at, lo_at = [0], [0]

        def split_hi(act, upto):
            while hi_at[0] <= min(upto, len(CHUNKS) - 1):
                n = hi_at[0]
                act.wait_ge(s_raw[n % RAW], landed_at[n])
                if LAST_IN_SLOT[n] is not None:
                    act.wait_ge(s_w_used.sem, s_w_used.after(CHUNKS[LAST_IN_SLOT[n]]))
                nk = k_tiles(n)
                act.activation(whi[SLOT[n]][:, 0:nk, :], raw[n % RAW][:, 0:nk, :], ACT.Copy).then_inc(s_w_hi.sem, s_w_hi.event(CHUNKS[n]))
                hi_at[0] += 1

        def split_lo(dve, upto):
            while lo_at[0] <= min(upto, len(CHUNKS) - 1):
                n = lo_at[0]
                dve.wait_ge(s_w_hi.sem, s_w_hi.after(CHUNKS[n]))
                nk = k_tiles(n)
                dve.tensor_tensor(wlo[SLOT[n]][:, 0:nk, :], raw[n % RAW][:, 0:nk, :],
                                                  whi[SLOT[n]][:, 0:nk, :].bitcast(F32), ALU.subtract).then_inc(s_w_lo.sem, s_w_lo.event(CHUNKS[n]))
                lo_at[0] += 1

        def x_hi(act, key, k, src, w):
            act.activation(xhi[:, k, 0:w], src, ACT.Copy).then_inc(s_x_hi.sem, s_x_hi.event(key, k))

        def shifted_hi(act, key, sh):
            for k in range(KT):
                act.wait_ge(s_scaled_n.sem, s_scaled_n.after(key, k))
                act.activation(xhi[:, k, 0:T2], XN[:, k, 0:T2], ACT.Identity, bias=mod[:, sh + k:sh + k + 1]).then_inc(s_x_hi.sem, s_x_hi.event(key, k))

        def x_lo(dve, key, k, src, w):
            dve.wait_ge(s_x_hi.sem, s_x_hi.after(key, k))
            dve.tensor_tensor(xlo[:, k, 0:w], src, xhi[:, k, 0:w].bitcast(F32), ALU.subtract).then_inc(s_x_lo.sem, s_x_lo.event(key, k))

        def product(pe, dst, ah, al, bh, bl, first, last, **kw):
            pe.matmul(dst, ah, bh, start=first, stop=False, **kw)
            pe.matmul(dst, ah, bl, start=False, stop=False, **kw)
            return pe.matmul(dst, al, bh, start=False, stop=last, **kw)

        def gemm(pe, g, xkey, w, tokens=False, c0=0):
            no = GROUPS.index(g)
            if no >= 3:
                pg = GROUPS[no - 3]
                drained(pe, pg)
            b = pair(g)
            js = range(3 if g[0] == "down" else 1)
            k = 0
            for j in js:
                n = CHUNK_NO[(g, j)]
                pe.wait_ge(s_w_lo.sem, s_w_lo.after(CHUNKS[n]))
                h, lo = whi[SLOT[n]], wlo[SLOT[n]]
                nk = k_tiles(n)
                k0 = DOWN_K[j][0] if g[0] == "down" else 0
                fresh = xkey is not None and g[2] == 0
                if g[0] == "down" and g[2] == 0:
                    pe.wait_ge(s_h_lo.sem, s_h_lo.after(g[1], k0 + nk - 1))
                xa, xb = (hhi, hlo) if g[0] == "down" else (xhi, xlo)
                if tokens:
                    tiles = [(ps[b + 1][:, 0:CW], 0), (ps[b][:, 0:CW], META), (ps[b][:, CW:2 * CW], META + P)] \
                        if w == T else [(ps[b][:, 0:CW], 0), (ps[b][:, CW:2 * CW], P)]
                    for no_, (dst, t0) in enumerate(tiles):
                        for k in range(8):
                            if fresh and no_ == 0:
                                pe.wait_ge(s_x_lo.sem, s_x_lo.after(xkey, k))
                            a = slice(t0, t0 + P)
                            mm = product(pe, dst, xa[:, k, a], xb[:, k, a], h[:, k, :], lo[:, k, :], k == 0, k == 7)
                else:
                    for k in range(nk):
                        if fresh:
                            pe.wait_ge(s_x_lo.sem, s_x_lo.after(xkey, k))
                        for mt in range(2):
                            c = slice(mt * P, mt * P + P)
                            mm = product(pe, ps[b + mt][:, c0:w], h[:, k, c], lo[:, k, c], xa[:, k0 + k, c0:w],
                                         xb[:, k0 + k, c0:w], k == 0 and j == js[0], k == nk - 1 and j == js[-1])
                mm.then_inc(s_w_used.sem, s_w_used.event(CHUNKS[n]))

        def product_done(eng, g):
            eng.wait_ge(s_w_used.sem, s_w_used.after(g, 2 if g[0] == "down" else 0))

        ADA_IN, ADA_UP = (4, 6, 8, 11), (0, 3, 6, 9, 12, 15, 18, 21)

        def ada_no(l, part, i):
            return 12 * l + (ADA_IN.index(i) if part == "in" else 4 + ADA_UP.index(i))

        def mod_columns(pe, a):
            pe.wait_ge(s_ada_sum.sem, s_ada_sum.after(a))
            for j in range(2):
                mm = pe.matmul(ps[7][:, 2 * a + j:2 * a + j + 1], adr[:, a % 2, j * P:j * P + P], ones_1[:, 0:1],
                               start=True, stop=True)
            mm.then_inc(s_ada_used.sem, s_ada_used.event(a))

        block = ctx.enter_context(nc.Block())

        @block.sync
        def _(sp):
            def load_chunk(n):
                if n >= RAW:
                    sp.wait_ge(s_w_lo.sem, s_w_lo.after(CHUNKS[n - RAW]))
                for dst, src in pieces(n):
                    sp.dma_start(dst, src).then_inc(s_raw[n % RAW], 16)

            for t, (a, w) in enumerate(TOK):
                src = A["meta_tokens"] if t == 0 else A["x"][0, a - META:a - META + w, :]
                sp.dma_start(xs[0:w, t, :], src).then_inc(s_x, 16)
            load_chunk(0)
            for dst, src in row_dmas[0::2]:
                sp.dma_start(dst, src).then_inc(s_prm, 16)
            for n in range(1, RAW):
                load_chunk(n)
            for n in range(RAW, len(CHUNKS)):
                load_chunk(n)
            for t in range(2):
                for half_ in range(2):
                    sp.wait_ge(s_turned_back.sem, s_turned_back.after(t, half_))
                    sp.dma_start(out[0, t * P:(t + 1) * P, 512 * half_:512 * half_ + 512],
                                 OB[:, t, 512 * half_:512 * half_ + 512]).then_inc(s_out, 16)
            sp.wait_ge(s_out, 64)

        @block.gpsimd
        def _(pool):
            n_const = [0]

            def fill(t, v):
                pool.memset(t, v).then_inc(s_filled.sem, s_filled.event(n_const[0]))
                pool.wait_ge(s_filled.sem, s_filled.after(n_const[0]))
                n_const[0] += 1

            def keep(t, pattern, op, fill_, base, cm):
                pool.affine_select(out=t, in_=t, pattern=pattern, compare_op=op, fill=fill_,
                                                     base=base, channel_multiplier=cm).then_inc(s_filled.sem, s_filled.event(n_const[0]))
                pool.wait_ge(s_filled.sem, s_filled.after(n_const[0]))
                n_const[0] += 1

            fill(epst[:, :], EPS)
            fill(ident[:, :], 0.0)
            keep(ident[:, :], [[-1, P]], ALU.not_equal, 1.0, 0, 1)
            pool.memset(ones_d[:, :], 1.0 / D).then_inc(s_consts.sem, s_consts.event("ident"))
            fill(ones_1[:, :], 1.0)
            fill(ones_v[:, :], 1.0 / P)
            fill(ones_a[:, :], 1.0 / 512)
            fill(onesrow[:, :], 1.0)
            fill(glr1[:, :], 1.0)
            fill(ones_f[:, :], 0.0)
            for b in range(2):
                pool_block = ones_f[64 * b:64 * b + 64, 64 * b:64 * b + 64]
                fill(pool_block, 1.0 / 64)
            fill(identb[:, :], 0.0)
            keep(identb[:, :], [[-1, P]], ALU.not_equal, 1.0, 0, 1)
            fill(causal[:, :], 0.0)
            keep(causal[:, :], [[-1, P]], ALU.is_ge, -BIG, 0, 1)
            fill(half[:, :], 0.0)
            for b in range(2):
                fill(half[64 * b:64 * b + 64, b:b + 1], 1.0)
            fill(after[:, :], 0.0)
            for b in range(2):
                blk = after[64 * b:64 * b + 64, 64 * b:64 * b + 64]
                fill(blk, 1.0)
                keep(blk, [[-1, 64]], ALU.is_gt, 0.0, 0, 1)
            pool.memset(restart[:, :], 1.0).then_inc(s_consts.sem, s_consts.event("first"))
            pool.wait_ge(s_consts.sem, s_consts.after("first"))
            for dst, src in small_dmas:
                pool.dma_start(dst, src).then_inc(s_small, 16)
            wv = kp(A["w_ada_2"][0])

            def load_ada(a):
                if a < 24:
                    if a >= 2:
                        pool.wait_ge(s_ada_sum.sem, s_ada_sum.after(a - 2))
                    pool.dma_start(ada[a % 2][:, :, :], wv[:, :, CW * a:CW * (a + 1)]).then_inc(s_ada[a % 2], 16)

            def ada_piece(a):
                load_ada(a + 1)
                pool.wait_ge(s_ada[a % 2], 16 * (a // 2 + 1))
                t = ada[a % 2]
                pool.tensor_tensor(t[:, :, :], t[:, :, :],
                                                      cact[:, :].unsqueeze(2).broadcast_to([P, KT, CW]), ALU.mult).then_inc(s_ada_mul.sem, s_ada_mul.event(a))
                pool.wait_ge(s_ada_mul.sem, s_ada_mul.after(a))
                pool.tensor_tensor(t[:, 0:4, :], t[:, 0:4, :], t[:, 4:8, :], ALU.add).then_inc(s_ada_four.sem, s_ada_four.event(a))
                pool.wait_ge(s_ada_four.sem, s_ada_four.after(a))
                pool.tensor_tensor(t[:, 0:2, :], t[:, 0:2, :], t[:, 2:4, :], ALU.add).then_inc(s_ada_two.sem, s_ada_two.event(a))
                pool.wait_ge(s_ada_two.sem, s_ada_two.after(a))
                if a >= 2:
                    pool.wait_ge(s_ada_used.sem, s_ada_used.after(a - 2))
                pool.tensor_tensor(adr[:, a % 2, :], t[:, 0, :], t[:, 1, :], ALU.add).then_inc(s_ada_sum.sem, s_ada_sum.event(a))

            pool.wait_ge(s_cact.sem, s_cact.after())
            load_ada(0)
            for l in range(DEPTH):
                for i in ADA_IN:
                    ada_piece(ada_no(l, "in", i))
                for i in ADA_UP:
                    ada_piece(ada_no(l, "up", i))
            fill(same_c[:, :], 0.0)
            for b in range(4):
                fill(same_c[32 * b:32 * b + 32, 32 * b:32 * b + 32], 1.0)
            keep(same_c[:, :], [[1, P]], ALU.is_ge, 0.0, 0, -1)
            fill(restart[:, :].rearrange("p (c t) -> p c t", t=HG_C)[:, :, 0:1], 0.0)
            fill(slope_i[:, :, :], 0.0)
            for h in range(ATT_H):
                keep(slope_i[:, h, :], [[-1, P]], ALU.not_equal, -(2.0 ** -(h + 1)), 0, 1)
            pool.iota(dist[:, :], pattern=[[-1, 2 * P]], base=P, channel_multiplier=1,
                                        allow_small_or_imprecise_dtypes=True).then_inc(s_filled.sem, s_filled.event(n_const[0]))
            pool.wait_ge(s_filled.sem, s_filled.after(n_const[0]))
            n_const[0] += 1
            keep(dist[:, :], [[-1, 2 * P]], ALU.is_ge, 2.0 ** 100, P, 1)
            keep(dist[:, :], [[1, 2 * P]], ALU.is_ge, 2.0 ** 100, -1, -1)
            pool.iota(iota8[:, :], pattern=[[1, 8]], base=0, channel_multiplier=0,
                                        allow_small_or_imprecise_dtypes=True).then_inc(s_filled.sem, s_filled.event(n_const[0]))
            pool.wait_ge(s_filled.sem, s_filled.after(n_const[0]))
            n_const[0] += 1
            product_done(pool, ("down", DEPTH - 1, 3))
            fill(At[:, :, :, :], 0.0)
            pool.memset(lbt[:, 4, :], 0.0).then_inc(s_consts.sem, s_consts.event("second"))
            for k in range(KT):
                pool.wait_ge(s_x_lo.sem, s_x_lo.after(("n5",), k))
                pool.tensor_scalar(XN[:, k, 0:T2], XN[:, k, 0:T2], mod[:, 24 + k:25 + k], None, ALU.add).then_inc(s_shifted.sem, s_shifted.event(k))

        @block.scalar
        def _(act):
            def drain(g, dst, src, func=ACT.Copy, last=True, **k):
                i = act.activation(dst, src, func, **k)
                if last:
                    i.then_inc(s_drained_act.sem, s_drained_act.event(g))

            for dst, src in row_dmas[1::2]:
                act.dma_start(dst, src).then_inc(s_prm, 16)
            for l in range(DEPTH):
                src = ("x0",) if l == 0 else ("d", 0)
                key = ("n1", l)
                if l == 0:
                    for k in range(KT):
                        act.wait_ge(s_xt.sem, s_xt.after(src, k))
                        stat_square(act, key, k, XT[:, k, :])
                        if k == 5:
                            split_hi(act, 0)
                    act.preload_act_table_set("natural_log_exp_and_others")
                stat_root(act, key)
                for k in range(KT):
                    act.wait_ge(s_normed.sem, s_normed.after(key, k))
                    x_hi(act, key, k, XN[:, k, :], T)
                if l == 0:
                    act.wait_ge(s_params.sem, s_params.after())
                    act.activation(cact[:, :], col("c", 0, 8), ACT.Silu).then_inc(s_cact.sem, s_cact.event())
                    act.preload_act_table_set("natural_log_exp_and_others")
                for i, (name, h) in enumerate(IN_ORDER):
                    g = ("in", l, i)
                    split_hi(act, CHUNK_NO[(g, 0)] + 1)
                    full, mt = la[:, 1:3, :].rearrange("p t n -> p (t n)"), la[0:META, 0, :]
                    if i == 2:
                        act.wait_ge(s_z.sem, s_z.after(l))
                        act.activation(full, ps[6][:, :], ACT.Abs)
                        act.activation(mt, ps[7][0:META, 64:320], ACT.Abs).then_inc(s_za.sem, s_za.event(l))
                        act.wait_ge(s_za.sem, s_za.after(l))
                        act.activation(full, full, ACT.Exp, scale=-1.0)
                        act.activation(mt, mt, ACT.Exp, scale=-1.0).then_inc(s_zb.sem, s_zb.event(l))
                        act.wait_ge(s_zb.sem, s_zb.after(l))
                        act.activation(full, full, ACT.Ln, bias=1.0)
                        act.activation(mt, mt, ACT.Ln, bias=1.0).then_inc(s_zc.sem, s_zc.event(l))
                    if i == 3:
                        act.wait_ge(s_gla_d.sem, s_gla_d.after(l))
                        act.activation(kd[:, 1:3, :].rearrange("p t n -> p (t n)"), ps[6][:, :], ACT.Exp, scale=1 / 16.0)
                        act.activation(kd[0:META, 0, :], ps[7][0:META, 64:320], ACT.Exp, scale=1 / 16.0)
                        act.activation(dec[:, :], ps[7][:, 340:348], ACT.Exp, scale=1 / 16.0).then_inc(s_gla_e.sem, s_gla_e.event(l))
                    if i == 1:
                        act.wait_ge(s_fz.sem, s_fz.after(l))
                        act.activation(fl[:, :], fz[:, :], ACT.Abs).then_inc(s_fl1.sem, s_fl1.event(l))
                        act.wait_ge(s_fl1.sem, s_fl1.after(l))
                        act.activation(fl[:, :], fl[:, :], ACT.Exp, scale=-1.0).then_inc(s_fl2.sem, s_fl2.event(l))
                        act.wait_ge(s_fl2.sem, s_fl2.after(l))
                        act.activation(fl[:, :], fl[:, :], ACT.Ln, bias=1.0).then_inc(s_fl3.sem, s_fl3.event(l))
                    if name not in ACT_DRAINS:
                        continue
                    product_done(act, g)
                    b = pair(g)
                    if name in ("gv", "fv"):
                        t = gvt if name == "gv" else fvt
                        cs = slice(CW * h, CW * h + CW)
                        drain(g, t[:, 1:3, cs], ps[b][:, :].rearrange("p (t n) -> p t n", t=2), last=False)
                        drain(g, t[0:META, 0, cs], ps[b + 1][0:META, 0:CW])
                    elif name == "gr":
                        for t in range(2):
                            drain(g, grT[:, 2 * h + t, :], ps[b + t][:, 0:T], ACT.Silu, last=(t == 1))
                        if h == 1:
                            act.preload_act_table_set("natural_log_exp_and_others")
                    else:
                        for t in range(2):
                            drain(g, fqT[:, 2 * h + t, :], ps[b + t][:, 0:T], ACT.Copy, last=(t == 1), scale=0.125)
                for h in range(4):
                    act.wait_ge(s_gla_o.sem, s_gla_o.after(l, h))
                    stat_square(act, ("g", l, h), 0, ps[GLA_BANK[h]][:, 0:T])
                for h in range(4):
                    stat_root(act, ("g", l, h))
                for h in range(4):
                    act.wait_ge(s_mixed.sem, s_mixed.after(l, h))
                    x_hi(act, ("mix", l), h, XN[:, h, :], T)
                for s in range(FOX_H + 4):
                    if s >= 3 and (s - 3) % 2 == 1:
                        stat_root(act, ("f", l, (s - 4) // 2))
                    if s < FOX_H:
                        for q, (q0, qn) in enumerate(TOK):
                            act.wait_ge(s_nmax.sem, s_nmax.after(l, s, q))
                            if s >= 2:
                                act.wait_ge(s_turned.sem, s_turned.after(l, s - 2))
                            c = s * 3 + q
                            act.activation(Pq[0:qn, s % 2, q, 0:q0 + qn], ps[FOX_BANK[q]][0:qn, 0:q0 + qn], ACT.Exp, bias=nmx[0:qn, c:c + 1], accum_out=psm[0:qn, c:c + 1]).then_inc(s_pexp.sem, s_pexp.event(l, s, q))
                    if 1 <= s <= FOX_H:
                        h = s - 1
                        act.wait_ge(s_turned.sem, s_turned.after(l, h))
                        if h >= 2:
                            act.wait_ge(s_pv.sem, s_pv.after(l, h - 2))
                        act.activation(PTs[:, h % 2, :], ps[2 + h % 2][:, 0:384], ACT.Copy).then_inc(s_pt_copied.sem, s_pt_copied.event(l, h))
                    if s >= 3 and (s - 3) % 2 == 0 and (s - 3) // 2 < 4:
                        j = (s - 3) // 2
                        act.wait_ge(s_fox_o.sem, s_fox_o.after(l, j))
                        stat_square(act, ("f", l, j), 0, XN[:, 4 + j, :])
                    if s >= 5 and (s - 5) % 2 == 0 and (s - 5) // 2 < 4:
                        j = (s - 5) // 2
                        act.wait_ge(s_mixed.sem, s_mixed.after(l, 4 + j))
                        x_hi(act, ("mix", l), 4 + j, XN[:, 4 + j, :], T)
                key = ("n2", l)
                for i in range(4):
                    g = ("out", l, i)
                    split_hi(act, CHUNK_NO[(g, 0)] + 1)
                    for t in range(2):
                        act.wait_ge(s_xt.sem, s_xt.after(("o", l), 2 * i + t))
                        stat_square(act, key, 2 * i + t, XT[:, 2 * i + t, :])
                stat_root(act, key)
                for k in range(KT):
                    act.wait_ge(s_normed.sem, s_normed.after(key, k))
                    x_hi(act, key, k, XN[:, k, :], T)
                c0 = UP_FROM[l]
                for i in range(FT + 2):
                    if i >= FT:
                        split_hi(act, CHUNK_NO[(("up", l, FT - 1), 0)] + 2 + i - FT)
                    if i < FT:
                        g = ("up", l, i)
                        split_hi(act, CHUNK_NO[(g, 0)] + 1)
                        product_done(act, g)
                        if i >= 2:
                            act.wait_ge(s_hidden.sem, s_hidden.after(l, i - 2))
                        for t in range(2):
                            f = i + FT * t
                            o = act.activation(cv[:, i % 2, t, c0:T], ps[pair(g) + t][:, c0:T], ACT.Identity,
                                               bias=col("conv_b", l * 2 * FT + f),
                                               scale=col("conv_w", (l * 3 + 2) * 2 * FT + f))
                        o.then_inc(s_tap2.sem, s_tap2.event(l, i))
                    if 1 <= i <= FT:
                        act.wait_ge(s_convolved.sem, s_convolved.after(l, i - 1))
                        s = (i - 1) % 2
                        act.activation(cv[:, s, 1, c0:T], cv[:, s, 1, c0:T], ACT.Silu).then_inc(s_gated.sem, s_gated.event(l, i - 1))
                    if i >= 2:
                        act.wait_ge(s_hidden.sem, s_hidden.after(l, i - 2))
                        act.activation(hhi[:, i - 2, c0:T], hf[:, i % 2, c0:T], ACT.Copy).then_inc(s_h_hi.sem, s_h_hi.event(l, i - 2))
                act.preload_act_table_set("natural_log_exp_and_others")
                key = ("n1", l + 1) if l + 1 < DEPTH else ("nf",)
                for i in range(4):
                    g = ("down", l, i)
                    split_hi(act, CHUNK_NO[(g, 2)] + 1)
                    for t in range(2):
                        act.wait_ge(s_xt.sem, s_xt.after(("d", l), 2 * i + t))
                        m_ = 2 * i + t
                        if l + 1 < DEPTH:
                            stat_square(act, key, m_, XT[:, m_, :])
                        else:
                            stat_square(act, key, m_, XT[:, m_, META:T])
                            stat_square(act, ("n3",), m_, XT[:, m_, META:T], scale=col("final_norm", m_))
            stat_root(act, ("nf",))
            act.wait_ge(s_mean3.sem, s_mean3.after())
            act.activation(RS(("n3",)), RS(("n3",)), ACT.Ln, bias=epst[:, 0:1]).then_inc(s_logged.sem, s_logged.event(("n3",)))
            act.wait_ge(s_logged.sem, s_logged.after(("n3",)))
            act.activation(RS(("n3",)), RS(("n3",)), ACT.Exp, scale=-0.5).then_inc(s_rooted.sem, s_rooted.event(("n3",)))
            shifted_hi(act, ("n3",), 0)
            act.wait_ge(s_lb_sub.sem, s_lb_sub.after())
            act.activation(lbt[:, 1, 0:8], lbt[:, 1, 0:8], ACT.Exp).then_inc(s_lb_exp.sem, s_lb_exp.event())
            fl2 = lambda t: t[:, :, :].rearrange("p h t -> p (h t)")
            for i, (name, h) in enumerate(IN2_ORDER):
                g = ("in2", 0, i)
                split_hi(act, CHUNK_NO[(g, 0)] + 1)
                if i == 6:
                    act.preload_act_table_set("natural_log_exp_and_others")
                    act.wait_ge(s_forget.sem, s_forget.after())
                    act.activation(fl2(fh), fl2(fh), ACT.Ln).then_inc(s_logf.sem, s_logf.event())
                elif i == 7:
                    act.wait_ge(s_cum.sem, s_cum.after(HG_H - 1))
                    act.activation(fl2(fh), fl2(bb), ACT.Exp).then_inc(s_exp_b.sem, s_exp_b.event())
                    act.activation(fl2(kdT), fl2(bb), ACT.Exp, scale=-1.0).then_inc(s_exp_nb.sem, s_exp_nb.event())
                elif i == 8:
                    act.wait_ge(s_end_sub.sem, s_end_sub.after())
                    act.activation(fl2(keT), fl2(keT), ACT.Exp).then_inc(s_exp_end.sem, s_exp_end.event())
                if name not in ACT_DRAINS:
                    continue
                product_done(act, g)
                for t in range(2):
                    src = ps[pair(g) + t][:, 0:T2]
                    if name == "ka":
                        drain(g, (kaT if t == 0 else vaT)[:, :], src, last=(t == 1))
                    else:
                        dst = {"fh": fh, "qh": qh, "gh": gh}[name]
                        drain(g, dst[:, 2 * h + t, :], src, ACT.Sigmoid if name == "fh" else ACT.Silu, last=(t == 1))
            for h in range(HG_H):
                act.wait_ge(s_hg_o.sem, s_hg_o.after(h))
                stat_square(act, ("h", h), 0, ps[HG_BANK[h]][:, 0:T2])
            for h in range(HG_H):
                stat_root(act, ("h", h))
            for h in range(HG_H):
                act.wait_ge(s_mixed2.sem, s_mixed2.after(4 + h))
                x_hi(act, ("mix2",), 4 + h, XN[:, 4 + h, 0:T2], T2)
            for s in range(ATT_H + 3):
                if s < ATT_H:
                    h = HEADS[s]
                    for q in range(2):
                        act.wait_ge(s_nmax2.sem, s_nmax2.after(s, q))
                        if s >= 2:
                            act.wait_ge(s_turned2.sem, s_turned2.after(s - 2))
                        c = s * 2 + q
                        dst = P2[:, s % 2, 0:P] if q == 0 else P2[:, s % 2, P:3 * P]
                        act.activation(dst, ps[2 * (s % 2) + q][:, 0:P * (q + 1)], ACT.Exp, bias=nmx[:, c:c + 1],
                                       accum_out=psm[:, c:c + 1])
                        act.activation(pri[:, c:c + 1], bc44[:, 36 + h:37 + h], ACT.Exp, bias=nmx[:, c:c + 1]).then_inc(s_pexp2.sem, s_pexp2.event(s, q))
                if 1 <= s <= ATT_H:
                    act.wait_ge(s_turned2.sem, s_turned2.after(s - 1))
                    if s >= 3:
                        act.wait_ge(s_pv2.sem, s_pv2.after(s - 3))
                    act.activation(PT2[:, (s - 1) % 2, :], ps[4 + (s - 1) % 2][:, 0:384], ACT.Copy).then_inc(s_pt2.sem, s_pt2.event(s - 1))
                if s >= 3 and (s - 3) % 2 == 0 and (s - 3) // 2 < 4:
                    j = (s - 3) // 2
                    act.wait_ge(s_att_o.sem, s_att_o.after(j))
                    stat_square(act, ("att",), j, XN[:, j, 0:T2])
            stat_root(act, ("att",))
            for j in range(4):
                act.wait_ge(s_mixed2.sem, s_mixed2.after(j))
                x_hi(act, ("mix2",), j, XN[:, j, 0:T2], T2)
            for i in range(4):
                g = ("out2", 0, i)
                split_hi(act, CHUNK_NO[(g, 0)] + 1)
                for t in range(2):
                    act.wait_ge(s_mixout.sem, s_mixout.after(2 * i + t))
                    stat_square(act, ("n4",), 2 * i + t, XN[:, 2 * i + t, 0:T2])
            stat_root(act, ("n4",))
            for k in range(KT):
                act.wait_ge(s_xt.sem, s_xt.after(("p",), k))
                stat_square(act, ("n5",), k, XT[:, k, META:T])
            stat_root(act, ("n5",))
            shifted_hi(act, ("n5",), 24)
            split_hi(act, EXPERTS_AT + 2)
            for e in range(NEXP):
                act.wait_ge(s_w_used.sem, s_w_used.after(("gate", 0, e), 0))
                if e >= 2:
                    act.wait_ge(s_hu.sem, s_hu.after(e - 2))
                act.activation(sg[:, e % 2, :], ps[4][:, :], ACT.Silu).then_inc(s_e_gate.sem, s_e_gate.event(e))
                if e == 0:
                    split_hi(act, EXPERTS_AT + 3)
                    for t in range(2):
                        act.wait_ge(s_r_sub.sem, s_r_sub.after(t))
                        act.activation(rt[:, t, 96:104], rt[:, t, 96:104], ACT.Exp).then_inc(s_r_exp.sem, s_r_exp.event(t))
                n = CHUNK_NO[(("upx", 0, e), 0)]
                split_hi(act, n + 1)
                split_hi(act, n + 2)
                if e:
                    split_hi(act, n + 3)
                act.wait_ge(s_hu.sem, s_hu.after(e))
                if e >= 2:
                    act.wait_ge(s_w_used.sem, s_w_used.after(("dn", 0, e - 2), 0))
                act.activation(huh[:, e % 2, :], hu[:, e % 2, :], ACT.Copy).then_inc(s_hu_hi.sem, s_hu_hi.event(e))
            act.preload_act_table_set("natural_log_exp_and_others")
            for k in range(KT):
                act.wait_ge(s_y.sem, s_y.after(k))
                stat_square(act, ("n6",), k, XN[:, k, 0:T2])
            stat_root(act, ("n6",))

        @block.vector
        def _(dve):
            for k in range(KT):
                dve.wait_ge(s_x_turned.sem, s_x_turned.after(k))
                dve.tensor_copy(XT[:, k, :], ps[1 + k % 4][:, 0:T]).then_inc(s_xt.sem, s_xt.event(("x0",), k))
            split_lo(dve, 0)
            dve.wait_ge(s_prm_turned.sem, s_prm_turned.after())
            dve.tensor_copy(PC[:, :], ps[0][:, 0:RBLK * P]).then_inc(s_params.sem, s_params.event())
            for l in range(DEPTH):
                key = ("n1", l)
                dve.wait_ge(s_rooted.sem, s_rooted.after(key))
                dve.wait_ge(s_params.sem, s_params.after())
                if l:
                    dve.wait_ge(s_xt.sem, s_xt.after(("d", l - 1), KT - 1))
                else:
                    dve.wait_ge(s_xt.sem, s_xt.after(("x0",), KT - 1))
                for k in range(KT + 2):
                    if k < KT:
                        dve.scalar_tensor_tensor(XN[:, k, :], XT[:, k, :], col("attn_norm", 8 * l + k), RS(key), ALU.mult, ALU.mult).then_inc(s_normed.sem, s_normed.event(key, k))
                    if k >= 2:
                        x_lo(dve, key, k - 2, XN[:, k - 2, :], T)
                for i, (name, h) in enumerate(IN_ORDER):
                    g = ("in", l, i)
                    split_lo(dve, CHUNK_NO[(g, 0)] + 1)
                    if i == 2:
                        dve.wait_ge(s_zc.sem, s_zc.after(l))
                        full, mt = la[:, 1:3, :].rearrange("p t n -> p (t n)"), la[0:META, 0, :]
                        dve.scalar_tensor_tensor(full, ps[6][:, :], 0.0, full, ALU.min, ALU.subtract)
                        dve.scalar_tensor_tensor(mt, ps[7][0:META, 64:320], 0.0, mt, ALU.min, ALU.subtract).then_inc(s_la.sem, s_la.event(l))
                    if i == 4:
                        dve.wait_ge(s_gla_e.sem, s_gla_e.after(l))
                        dve.tensor_tensor(kd[:, 1:3, :], kd[:, 1:3, :], gkt[:, 1:3, :], ALU.mult)
                        dve.tensor_tensor(kd[0:META, 0, :], kd[0:META, 0, :], gkt[0:META, 0, :], ALU.mult).then_inc(s_kd.sem, s_kd.event(l))
                    if name in ACT_DRAINS:
                        continue
                    product_done(dve, g)
                    b = pair(g)
                    if name == "gk":
                        dve.tensor_copy(gkt[:, 1:3, :], ps[b][:, :].rearrange("p (t n) -> p t n", t=2))
                        dve.tensor_copy(gkt[0:META, 0, :], ps[b + 1][0:META, 0:CW]).then_inc(s_drained_dve.sem, s_drained_dve.event(g))
                        dve.wait_ge(s_small_ff.sem, s_small_ff.after(l))
                        dve.tensor_scalar(fz[:, :], ps[7][0:8, 64:64 + T], bfo[:, l:l + 1], None, ALU.add).then_inc(s_fz.sem, s_fz.event(l))
                        dve.wait_ge(s_small_glr.sem, s_small_glr.after(l))
                        dve.tensor_copy(glr1[0:16, :], ps[6][0:16, 0:T]).then_inc(s_glr.sem, s_glr.event(l))
                        if l == 0:
                            dve.wait_ge(s_bc.sem, s_bc.after())
                            dve.tensor_copy(bc44[:, :], ps[6][:, 0:44]).then_inc(s_bc44.sem, s_bc44.event())
                        split_lo(dve, CHUNK_NO[(g, 0)] + 2)
                        dve.wait_ge(s_fl3.sem, s_fl3.after(l))
                        dve.scalar_tensor_tensor(fl[:, :], fz[:, :], 0.0, fl[:, :], ALU.min, ALU.subtract).then_inc(s_lf.sem, s_lf.event(l))
                        dve.wait_ge(s_lf.sem, s_lf.after(l))
                        dve.tensor_tensor_scan(negc[:, :], onesrow[:, :], fl[:, :], 0.0, ALU.mult, ALU.subtract).then_inc(s_negc.sem, s_negc.event(l))
                    elif name == "gq":
                        for t in range(2):
                            o = dve.tensor_scalar(gqT[:, t, :], ps[b + t][:, 0:T], 0.125, None, ALU.mult)
                        o.then_inc(s_drained_dve.sem, s_drained_dve.event(g))
                    else:
                        for t in range(2):
                            o = dve.tensor_copy(fkT[:, 2 * h + t, :], ps[b + t][:, 0:T])
                        o.then_inc(s_drained_dve.sem, s_drained_dve.event(g))
                dve.wait_ge(s_gla_u.sem, s_gla_u.after(l))
                for c in range(5):
                    for p in range(2):
                        u = ps[4][:, p * P:p * P + P] if c == 0 else \
                            ps[(c - 1) % 2][:, ((c - 1) // 2) * 256 + p * P:((c - 1) // 2) * 256 + p * P + P]
                        if c == 0:
                            dve.tensor_copy(ST[:, p, 0, :], u).then_inc(s_state.sem, s_state.event(l, c, p))
                        else:
                            dve.wait_ge(s_state.sem, s_state.after(l, c - 1, p))
                            dve.scalar_tensor_tensor(ST[:, p, c, :], ST[:, p, c - 1, :], dec[:, p * 4 + c - 1:p * 4 + c], u, ALU.mult, ALU.add).then_inc(s_state.sem, s_state.event(l, c, p))
                for h in range(4):
                    k_ = ("g", l, h)
                    dve.wait_ge(s_rooted.sem, s_rooted.after(k_))
                    dve.scalar_tensor_tensor(XN[:, h, :], ps[GLA_BANK[h]][:, 0:T], col("gla_norm", 4 * l + h), RS(k_), ALU.mult, ALU.mult).then_inc(s_scaled.sem, s_scaled.event(l, h))
                    dve.wait_ge(s_scaled.sem, s_scaled.after(l, h))
                    dve.tensor_tensor(XN[:, h, :], XN[:, h, :], grT[:, h, :], ALU.mult).then_inc(s_mixed.sem, s_mixed.event(l, h))
                for h in range(4):
                    x_lo(dve, ("mix", l), h, XN[:, h, :], T)
                for s in range(FOX_H + 4):
                    if s < FOX_H:
                        for q, (q0, qn) in enumerate(TOK):
                            c = s * 3 + q
                            dve.wait_ge(s_scores.sem, s_scores.after(l, s, q))
                            dve.tensor_reduce(nmx[0:qn, c:c + 1], ps[FOX_BANK[q]][0:qn, 0:q0 + qn], AX_X,
                                                              ALU.max, negate=True).then_inc(s_nmax.sem, s_nmax.event(l, s, q))
                    if 1 <= s <= FOX_H:
                        h = s - 1
                        dve.wait_ge(s_turned.sem, s_turned.after(l, h))
                        if h >= 2:
                            dve.wait_ge(s_pv.sem, s_pv.after(l, h - 2))
                        dve.tensor_copy(PTm[:, h % 2, :], ps[5][0:META, 0:T]).then_inc(s_ptm_copied.sem, s_ptm_copied.event(l, h))
                    if s < FOX_H:
                        for q, (q0, qn) in enumerate(TOK):
                            c = s * 3 + q
                            dve.wait_ge(s_pexp.sem, s_pexp.after(l, s, q))
                            dve.reciprocal(pri[0:qn, c:c + 1], psm[0:qn, c:c + 1]).then_inc(s_recip.sem, s_recip.event(l, s, q))
                        for q, (q0, qn) in enumerate(TOK):
                            c = s * 3 + q
                            dve.wait_ge(s_recip.sem, s_recip.after(l, s, q))
                            v = Pq[0:qn, s % 2, q, 0:q0 + qn]
                            dve.tensor_scalar(v, v, pri[0:qn, c:c + 1], None, ALU.mult).then_inc(s_prob.sem, s_prob.event(l, s, q))
                    if s >= 3 and (s - 3) % 2 == 0 and (s - 3) // 2 < 4:
                        j = (s - 3) // 2
                        dve.wait_ge(s_pv.sem, s_pv.after(l, 2 * j + 1))
                        dve.tensor_copy(XN[:, 4 + j, :], ps[6][:, 0:T]).then_inc(s_fox_o.sem, s_fox_o.event(l, j))
                    if s >= 4 and (s - 4) % 2 == 0 and (s - 4) // 2 < 4:
                        j = (s - 4) // 2
                        k_ = ("f", l, j)
                        dve.wait_ge(s_rooted.sem, s_rooted.after(k_))
                        dve.wait_ge(s_fox_o.sem, s_fox_o.after(l, j))
                        dve.scalar_tensor_tensor(XN[:, 4 + j, :], XN[:, 4 + j, :], col("fox_norm", 4 * l + j), RS(k_), ALU.mult, ALU.mult).then_inc(s_mixed.sem, s_mixed.event(l, 4 + j))
                        dve.wait_ge(s_mixed.sem, s_mixed.after(l, 4 + j))
                    if s >= 5 and (s - 5) % 2 == 0 and (s - 5) // 2 < 4:
                        x_lo(dve, ("mix", l), 4 + (s - 5) // 2, XN[:, 4 + (s - 5) // 2, :], T)

                def residual(kind, tag, i, last_chunk):
                    g = (kind, l, i)
                    split_lo(dve, last_chunk + 1)
                    product_done(dve, g)
                    for t in range(2):
                        c0 = DOWN_FROM[l] if kind == "down" else 0
                        o = dve.tensor_tensor(XT[:, 2 * i + t, c0:T], ps[pair(g) + t][:, c0:T], XT[:, 2 * i + t, c0:T], ALU.add)
                        o.then_inc(s_xt.sem, s_xt.event(tag, l, 2 * i + t))

                for i in range(4):
                    residual("out", "o", i, CHUNK_NO[(("out", l, i), 0)])
                key = ("n2", l)
                dve.wait_ge(s_xt.sem, s_xt.after(("o", l), KT - 1))
                dve.wait_ge(s_rooted.sem, s_rooted.after(key))
                for k in range(KT + 2):
                    if k < KT:
                        dve.scalar_tensor_tensor(XN[:, k, :], XT[:, k, :], col("ffn_norm", 8 * l + k), RS(key), ALU.mult, ALU.mult).then_inc(s_normed.sem, s_normed.event(key, k))
                    if k >= 2:
                        x_lo(dve, key, k - 2, XN[:, k - 2, :], T)
                c0 = UP_FROM[l]
                for i in range(FT + 2):
                    if i >= FT:
                        split_lo(dve, CHUNK_NO[(("up", l, FT - 1), 0)] + 2 + i - FT)
                    if i < FT:
                        g = ("up", l, i)
                        split_lo(dve, CHUNK_NO[(g, 0)] + 1)
                        dve.wait_ge(s_tap2.sem, s_tap2.after(l, i))
                        s = i % 2
                        for t in range(2):
                            dve.scalar_tensor_tensor(cv[:, s, t, c0 + 1:T], ps[pair(g) + t][:, c0:T - 1], col("conv_w", (l * 3 + 1) * 2 * FT + i + FT * t), cv[:, s, t, c0 + 1:T], ALU.mult, ALU.add).then_inc(s_tap1.sem, s_tap1.event(l, i, t))
                        for t in range(2):
                            dve.wait_ge(s_tap1.sem, s_tap1.after(l, i, t))
                            o = dve.scalar_tensor_tensor(cv[:, s, t, c0 + 2:T], ps[pair(g) + t][:, c0:T - 2],
                                                         col("conv_w", l * 3 * 2 * FT + i + FT * t), cv[:, s, t, c0 + 2:T],
                                                         ALU.mult, ALU.add)
                        o.then_inc(s_convolved.sem, s_convolved.event(l, i))
                    if 1 <= i <= FT:
                        dve.wait_ge(s_gated.sem, s_gated.after(l, i - 1))
                        s = (i - 1) % 2
                        if i >= 3:
                            dve.wait_ge(s_h_lo.sem, s_h_lo.after(l, i - 3))
                        dve.tensor_tensor(hf[:, s, c0:T], cv[:, s, 0, c0:T], cv[:, s, 1, c0:T], ALU.mult).then_inc(s_hidden.sem, s_hidden.event(l, i - 1))
                    if i >= 2 and i - 2 < FT:
                        dve.wait_ge(s_h_hi.sem, s_h_hi.after(l, i - 2))
                        dve.tensor_tensor(hlo[:, i - 2, c0:T], hf[:, i % 2, c0:T], hhi[:, i - 2, c0:T].bitcast(F32), ALU.subtract).then_inc(s_h_lo.sem, s_h_lo.event(l, i - 2))
                for i in range(4):
                    residual("down", "d", i, CHUNK_NO[(("down", l, i), 2)])
            dve.wait_ge(s_rooted.sem, s_rooted.after(("nf",)))
            dve.tensor_tensor(RS(("n3",)), RS(("nf",)), RS(("nf",)), ALU.mult).then_inc(s_root_sq.sem, s_root_sq.event())
            dve.wait_ge(s_root_sq.sem, s_root_sq.after())
            dve.wait_ge(s_averaged.sem, s_averaged.after(("n3",), KT - 1))
            dve.tensor_tensor(RS(("n3",)), RS(("n3",)), ps[6][:, 0:T2], ALU.mult).then_inc(s_mean3.sem, s_mean3.event())
            dve.wait_ge(s_ada_used.sem, s_ada_used.after(23))
            dve.tensor_tensor(mod[:, :], ps[7][:, 0:48], col("b_ada", 0, 48), ALU.add).then_inc(s_mod.sem, s_mod.event())
            dve.wait_ge(s_mod.sem, s_mod.after())
            for n_, (ln_, m0) in enumerate((("ln1_pre", 8), ("ln1_post", 16), ("ln2_pre", 32), ("ln2_post", 40))):
                o = dve.scalar_tensor_tensor(gsc[:, n_, :], mod[:, m0:m0 + 8], 1.0 if n_ % 2 == 0 else 0.0, col(ln_, 0, 8),
                                             ALU.add, ALU.mult)
            o.then_inc(s_gsc.sem, s_gsc.event())
            ab = col("hgrn_lb", 0, 8)
            dve.tensor_tensor(lbt[:, 0, 0:4], ab[:, 0:4], ab[:, 4:8], ALU.max).then_inc(s_lb_max.sem, s_lb_max.event())
            dve.wait_ge(s_lb_max.sem, s_lb_max.after())
            dve.tensor_tensor(lbt[:, 1, 0:4], ab[:, 0:4], lbt[:, 0, 0:4], ALU.subtract)
            dve.tensor_tensor(lbt[:, 1, 4:8], ab[:, 4:8], lbt[:, 0, 0:4], ALU.subtract).then_inc(s_lb_sub.sem, s_lb_sub.event())
            dve.wait_ge(s_xt.sem, s_xt.after(("d", DEPTH - 1), KT - 1))
            for k in range(KT):
                dve.scalar_tensor_tensor(XT[:, k, META:T], XT[:, k, META:T], col("final_norm", k), RS(("nf",)), ALU.mult, ALU.mult).then_inc(s_xt.sem, s_xt.event(("f",), k))
            dve.wait_ge(s_xt.sem, s_xt.after(("f",), KT - 1))

            def modulated(key, n_, sh):
                dve.wait_ge(s_gsc.sem, s_gsc.after())
                dve.wait_ge(s_rooted.sem, s_rooted.after(key))
                for i in range(KT + 2):
                    if i < KT:
                        dve.scalar_tensor_tensor(XN[:, i, 0:T2], XT[:, i, META:T], gsc[:, n_, i:i + 1], RS(key), ALU.mult, ALU.mult).then_inc(s_scaled_n.sem, s_scaled_n.event(key, i))
                    if 2 <= i < KT + 2:
                        k = i - 2
                        dve.wait_ge(s_x_hi.sem, s_x_hi.after(key, k))
                        dve.scalar_tensor_tensor(xlo[:, k, 0:T2], XN[:, k, 0:T2], mod[:, sh + k:sh + k + 1], xhi[:, k, 0:T2].bitcast(F32), ALU.add, ALU.subtract).then_inc(s_x_lo.sem, s_x_lo.event(key, k))

            modulated(("n3",), 0, 0)
            dve.wait_ge(s_lb_exp.sem, s_lb_exp.after())
            dve.tensor_tensor(lbt[:, 2, 0:4], lbt[:, 1, 0:4], lbt[:, 1, 4:8], ALU.add).then_inc(s_lb_sum.sem, s_lb_sum.event())
            dve.wait_ge(s_lb_sum.sem, s_lb_sum.after())
            dve.reciprocal(lbt[:, 2, 4:8], lbt[:, 2, 0:4]).then_inc(s_lb_rec.sem, s_lb_rec.event())
            dve.wait_ge(s_lb_rec.sem, s_lb_rec.after())
            dve.tensor_tensor(lbt[:, 3, 0:4], lbt[:, 1, 0:4], lbt[:, 2, 4:8], ALU.mult).then_inc(s_lb.sem, s_lb.event())
            dve.wait_ge(s_lb.sem, s_lb.after())
            dve.tensor_scalar(lbt[:, 3, 4:8], lbt[:, 3, 0:4], -1.0, 1.0, ALU.mult, ALU.add).then_inc(s_lb1.sem, s_lb1.event())
            dve.wait_ge(s_lb1.sem, s_lb1.after())
            dve.wait_ge(s_consts.sem, s_consts.after("second"))
            dve.tensor_scalar(lbt[:, 4, 0:4], lbt[:, 3, 4:8], -1.0, None, ALU.mult).then_inc(s_lb2.sem, s_lb2.event())
            dve.wait_ge(s_lb2.sem, s_lb2.after())
            fl2 = lambda t: t[:, :, :].rearrange("p h t -> p (h t)")
            by_chunk = lambda t, h: t[:, h, :].rearrange("p (c t) -> p c t", t=HG_C)
            for i, (name, h) in enumerate(IN2_ORDER):
                g = ("in2", 0, i)
                split_lo(dve, CHUNK_NO[(g, 0)] + 1)
                if i == 7:
                    dve.wait_ge(s_logf.sem, s_logf.after())
                    for h_ in range(HG_H):
                        dve.tensor_tensor_scan(bb[:, h_, :], restart[:, :], fh[:, h_, :], 0.0, ALU.mult, ALU.add).then_inc(s_cum.sem, s_cum.event(h_))
                    dve.wait_ge(s_cum.sem, s_cum.after(HG_H - 1))
                    for h_ in range(HG_H):
                        v = by_chunk(bb, h_)
                        o = dve.tensor_tensor(by_chunk(keT, h_), v[:, :, HG_C - 1:HG_C].broadcast_to([P, T2 // HG_C, HG_C]), v, ALU.subtract)
                    o.then_inc(s_end_sub.sem, s_end_sub.event())
                if i == 9:
                    dve.wait_ge(s_drained_act.sem, s_drained_act.after(("in2", 0, 3)))
                    dve.wait_ge(s_exp_b.sem, s_exp_b.after())
                    dve.tensor_tensor(fl2(qh), fl2(qh), fl2(fh), ALU.mult).then_inc(s_qd.sem, s_qd.event())
                    dve.wait_ge(s_exp_nb.sem, s_exp_nb.after())
                    dve.tensor_tensor(fl2(kdT), fl2(kdT), fl2(kh), ALU.mult).then_inc(s_kd2.sem, s_kd2.event())
                    dve.wait_ge(s_exp_end.sem, s_exp_end.after())
                    dve.tensor_tensor(fl2(keT), fl2(keT), fl2(kh), ALU.mult).then_inc(s_ke.sem, s_ke.event())
                if name == "qh" and h == 0:
                    dve.wait_ge(s_drained_act.sem, s_drained_act.after(("in2", 0, 1)))
                    for t in range(HG_H):
                        dve.tensor_scalar(kh[:, t, :], fh[:, t, :], lbt[:, 4, t:t + 1], lbt[:, 3, 4 + t:5 + t], ALU.mult, ALU.add).then_inc(s_kh.sem, s_kh.event(t))
                    for t in range(HG_H):
                        dve.wait_ge(s_kh.sem, s_kh.after(t))
                        o = dve.tensor_scalar(fh[:, t, :], fh[:, t, :], lbt[:, 3, 4 + t:5 + t], lbt[:, 3, t:t + 1], ALU.mult, ALU.add)
                    o.then_inc(s_forget.sem, s_forget.event())
                if name in ACT_DRAINS:
                    continue
                product_done(dve, g)
                b = pair(g)
                if name == "ih":
                    o = dve.tensor_copy(ih[:, :, CW * h:CW * h + CW], ps[b][:, :].rearrange("p (t n) -> p t n", t=2))
                else:
                    for t in range(2):
                        o = dve.tensor_scalar(qaT[:, 2 * h + t, :], ps[b + t][:, 0:T2], 0.125, None, ALU.mult)
                o.then_inc(s_drained_dve.sem, s_drained_dve.event(g))
            for t in range(2):
                dve.wait_ge(s_ke_turned.sem, s_ke_turned.after(t))
                dve.tensor_copy(ke[:, t, :, :].rearrange("p h n -> p (h n)"), ps[t][:, :]).then_inc(s_ke_copied.sem, s_ke_copied.event(t))
                dve.wait_ge(s_intra.sem, s_intra.after(t))
                mask = same_c[:, :].bitcast(I32)
                for h in range(HG_H):
                    o = dve.copy_predicated(At[:, t, h, :], mask, ps[2 + t][:, P * h:P * h + P])
                o.then_inc(s_a_copied.sem, s_a_copied.event(t))
            dve.wait_ge(s_va_turned.sem, s_va_turned.after())
            dve.tensor_copy(va[:, :, :].rearrange("p t n -> p (t n)"), ps[0][:, 0:256]).then_inc(s_va.sem, s_va.event())
            for c in range(7):
                u = ps[4 + c % 4] if c < 4 else ps[c % 4]
                dve.wait_ge(s_hg_u.sem, s_hg_u.after(c // 4))
                if c == 0:
                    dve.tensor_copy(SS[:, 0, :, :].rearrange("p h n -> p (h n)"), u[:, :]).then_inc(s_hg_s.sem, s_hg_s.event(0))
                    continue
                dve.wait_ge(s_hg_s.sem, s_hg_s.after(c - 1))
                for h in range(HG_H):
                    d = fh[:, h, c * HG_C + HG_C - 1:c * HG_C + HG_C]
                    o = dve.scalar_tensor_tensor(SS[:, c, h, :], SS[:, c - 1, h, :], d, u[:, P * h:P * h + P],
                                                 ALU.mult, ALU.add)
                o.then_inc(s_hg_s.sem, s_hg_s.event(c))
            for h in range(HG_H):
                k_ = ("h", h)
                dve.wait_ge(s_rooted.sem, s_rooted.after(k_))
                dve.scalar_tensor_tensor(XN[:, 4 + h, 0:T2], ps[HG_BANK[h]][:, 0:T2], col("hgrn_out_norm", h), RS(k_), ALU.mult, ALU.mult).then_inc(s_scaled2.sem, s_scaled2.event(h))
                dve.wait_ge(s_scaled2.sem, s_scaled2.after(h))
                dve.tensor_tensor(XN[:, 4 + h, 0:T2], XN[:, 4 + h, 0:T2], gh[:, h, :], ALU.mult).then_inc(s_mixed2.sem, s_mixed2.event(4 + h))
            for h in range(HG_H):
                x_lo(dve, ("mix2",), 4 + h, XN[:, 4 + h, 0:T2], T2)
            dve.wait_ge(s_bc44.sem, s_bc44.after())
            for s in range(ATT_H + 3):
                if s < ATT_H:
                    h = HEADS[s]
                    for q in range(2):
                        c = 2 * s + q
                        dve.wait_ge(s_scores2.sem, s_scores2.after(s, q))
                        dve.tensor_reduce(nmx[:, c:c + 1], ps[2 * (s % 2) + q][:, 0:P * (q + 1)], AX_X, ALU.max,
                                                           negate=True).then_inc(s_nmaxa.sem, s_nmaxa.event(s, q))
                    for q in range(2):
                        c = 2 * s + q
                        dve.wait_ge(s_nmaxa.sem, s_nmaxa.after(s, q))
                        dve.scalar_tensor_tensor(nmx[:, c:c + 1], bc44[:, 36 + h:37 + h], -1.0, nmx[:, c:c + 1], ALU.mult, ALU.min).then_inc(s_nmax2.sem, s_nmax2.event(s, q))
                    for q in range(2):
                        c = 2 * s + q
                        dve.wait_ge(s_pexp2.sem, s_pexp2.after(s, q))
                        dve.tensor_tensor(psm[:, c:c + 1], psm[:, c:c + 1], pri[:, c:c + 1], ALU.add).then_inc(s_den2.sem, s_den2.event(s, q))
                    for q in range(2):
                        c = 2 * s + q
                        dve.wait_ge(s_den2.sem, s_den2.after(s, q))
                        dve.reciprocal(pri[:, c:c + 1], psm[:, c:c + 1]).then_inc(s_rec2.sem, s_rec2.event(s, q))
                    for q in range(2):
                        c = 2 * s + q
                        dve.wait_ge(s_rec2.sem, s_rec2.after(s, q))
                        v = P2[:, s % 2, 0:P] if q == 0 else P2[:, s % 2, P:3 * P]
                        dve.tensor_scalar(v, v, pri[:, c:c + 1], None, ALU.mult).then_inc(s_prob2.sem, s_prob2.event(s, q))
                if s >= 3 and (s - 3) % 2 == 0 and (s - 3) // 2 < 4:
                    j = (s - 3) // 2
                    dve.wait_ge(s_pv2.sem, s_pv2.after(2 * j + 1))
                    dve.tensor_copy(XN[:, j, 0:T2], ps[6][:, 0:T2]).then_inc(s_att_o.sem, s_att_o.event(j))
            dve.wait_ge(s_rooted.sem, s_rooted.after(("att",)))
            dve.wait_ge(s_att_o.sem, s_att_o.after(3))
            for j in range(4):
                dve.scalar_tensor_tensor(XN[:, j, 0:T2], XN[:, j, 0:T2], col("attn_out_norm", j), RS(("att",)), ALU.mult, ALU.mult).then_inc(s_mixed2.sem, s_mixed2.event(j))
            dve.wait_ge(s_mixed2.sem, s_mixed2.after(3))
            for j in range(4):
                x_lo(dve, ("mix2",), j, XN[:, j, 0:T2], T2)
            for i in range(4):
                g = ("out2", 0, i)
                split_lo(dve, CHUNK_NO[(g, 0)] + 1)
                product_done(dve, g)
                for t in range(2):
                    dve.tensor_copy(XN[:, 2 * i + t, 0:T2], ps[pair(g) + t][:, 0:T2]).then_inc(s_mixout.sem, s_mixout.event(2 * i + t))

            def post_norm(key, n_, tag):
                dve.wait_ge(s_rooted.sem, s_rooted.after(key))
                for i in range(KT + 1):
                    if i < KT:
                        dve.scalar_tensor_tensor(XN[:, i, 0:T2], XN[:, i, 0:T2], gsc[:, n_, i:i + 1], RS(key), ALU.mult, ALU.mult).then_inc(s_post.sem, s_post.event(key, i))
                    if i == 0:
                        continue
                    k = i - 1
                    dve.wait_ge(s_post.sem, s_post.after(key, k))
                    dve.tensor_tensor(XT[:, k, META:T], XT[:, k, META:T], XN[:, k, 0:T2], ALU.add).then_inc(s_xt.sem, s_xt.event((tag,), k))

            dve.wait_ge(s_mixout.sem, s_mixout.after(KT - 1))
            post_norm(("n4",), 1, "p")
            dve.wait_ge(s_xt.sem, s_xt.after(("p",), KT - 1))
            modulated(("n5",), 2, 24)
            split_lo(dve, EXPERTS_AT + 2)
            dve.wait_ge(s_routed.sem, s_routed.after())
            n_r = [0]

            def r(ins):
                ins.then_inc(s_r.sem, s_r.event(n_r[0]))
                dve.wait_ge(s_r.sem, s_r.after(n_r[0]))
                n_r[0] += 1

            r(dve.memset(rt[:, :, 0:8], -3.0e38))
            LG = lambda t, a, b: ps[0][:, 64 * t + a:64 * t + b]
            R = lambda t, a, b: rt[:, t, a:b]
            for t in range(2):
                dve.tensor_copy(R(t, 0, 4), LG(t, 0, 4))
            for t in range(2):
                o = dve.tensor_copy(R(t, 8, 40), LG(t, 4, 36))
            r(o)
            for t in range(2):
                o = dve.max(R(t, 40, 48), R(t, 0, 8))
            r(o)
            for t in range(2):
                o = dve.max_index(R(t, 48, 56).bitcast(U32), R(t, 40, 48), R(t, 0, 8))
            r(o)
            for t in range(2):
                o = dve.tensor_copy(R(t, 56, 57), R(t, 48, 49).bitcast(U32))
            r(o)
            for t in range(2):
                o = dve.tensor_scalar(R(t, 64, 72), iota8[:, :], R(t, 56, 57), None, ALU.is_equal)
            r(o)
            for t in range(2):
                o = dve.tensor_scalar(R(t, 72, 80), R(t, 8, 16), R(t, 64, 65), None, ALU.mult)
            r(o)
            for g_ in range(1, 4):
                for t in range(2):
                    o = dve.scalar_tensor_tensor(R(t, 72, 80), R(t, 8 + 8 * g_, 16 + 8 * g_), R(t, 64 + g_, 65 + g_), R(t, 72, 80), ALU.mult, ALU.add)
                r(o)
            for t in range(2):
                o = dve.max(R(t, 80, 88), R(t, 72, 80))
            r(o)
            for t in range(2):
                o = dve.max_index(R(t, 48, 56).bitcast(U32), R(t, 80, 88), R(t, 72, 80))
            r(o)
            for t in range(2):
                o = dve.tensor_copy(R(t, 56, 58), R(t, 48, 50).bitcast(U32))
            r(o)
            for t in range(2):
                o = dve.tensor_scalar(R(t, 96, 100), R(t, 0, 4), R(t, 40, 41), None, ALU.subtract)
            for t in range(2):
                o = dve.memset(R(t, 101, 104), 0.0)
            r(o)
            for t in range(2):
                dve.tensor_tensor(R(t, 100, 101), R(t, 81, 82), R(t, 80, 81), ALU.subtract).then_inc(s_r_sub.sem, s_r_sub.event(t))
            split_lo(dve, EXPERTS_AT + 3)
            for t in range(2):
                dve.wait_ge(s_r_exp.sem, s_r_exp.after(t))
            for t in range(2):
                o = dve.tensor_reduce(R(t, 104, 105), R(t, 96, 100), AX_X, ALU.add)
            for t in range(2):
                o = dve.tensor_scalar(R(t, 105, 106), R(t, 100, 101), 1.0, None, ALU.add)
            r(o)
            for t in range(2):
                o = dve.tensor_tensor(R(t, 106, 107), R(t, 104, 105), R(t, 105, 106), ALU.mult)
            r(o)
            for t in range(2):
                o = dve.reciprocal(R(t, 107, 108), R(t, 106, 107))
            r(o)
            for t in range(2):
                o = dve.tensor_tensor(R(t, 108, 109), R(t, 107, 108), R(t, 100, 101), ALU.mult)
            r(o)
            for t in range(2):
                o = dve.tensor_scalar(R(t, 112, 120), iota8[:, :], R(t, 56, 57), R(t, 107, 108), ALU.is_equal, ALU.mult)
            r(o)
            for t in range(2):
                o = dve.tensor_scalar(R(t, 120, 128), iota8[:, :], R(t, 57, 58), R(t, 108, 109), ALU.is_equal, ALU.mult)
            r(o)
            for t in range(2):
                o = dve.tensor_tensor(R(t, 112, 120), R(t, 112, 120), R(t, 120, 128), ALU.add)
            r(o)
            for t in range(2):
                for g_ in range(4):
                    o = dve.tensor_scalar(wt[:, t, 8 * g_:8 * g_ + 8], R(t, 112, 120), R(t, 64 + g_, 65 + g_), None, ALU.mult)
                o.then_inc(s_wt.sem, s_wt.event(t))
            dve.wait_ge(s_wt_turned.sem, s_wt_turned.after())
            dve.tensor_copy(WT[:, :], ps[1][0:NEXP, 0:T2]).then_inc(s_WT.sem, s_WT.event())
            dve.tensor_copy(identr[:, :], ident[0:NEXP, 0:NEXP])
            dve.wait_ge(s_WT.sem, s_WT.after())
            dve.tensor_copy(WTh[:, :], WT[:, :]).then_inc(s_wt_hi.sem, s_wt_hi.event())
            dve.wait_ge(s_wt_hi.sem, s_wt_hi.after())
            dve.tensor_tensor(WTl[:, :], WT[:, :], WTh[:, :].bitcast(F32), ALU.subtract).then_inc(s_wt_lo.sem, s_wt_lo.event())
            split_lo(dve, EXPERTS_AT + 2)
            for e in range(NEXP):
                dve.wait_ge(s_e_gate.sem, s_e_gate.after(e))
                dve.wait_ge(s_weighed.sem, s_weighed.after(e))
                s = e % 2
                w2 = ps[6 + s][:, 0:T2]
                sgv, huv = sg[:, s, :], hu[:, s, :]
                for j in range(2):
                    o = dve.tensor_tensor(sgv[:, T2 * j:T2 * j + T2], sgv[:, T2 * j:T2 * j + T2], w2, ALU.mult)
                o.then_inc(s_sgw.sem, s_sgw.event(e))
                n = CHUNK_NO[(("upx", 0, e), 0)]
                split_lo(dve, n + 1)
                split_lo(dve, n + 2)
                dve.wait_ge(s_sgw.sem, s_sgw.after(e))
                dve.wait_ge(s_w_used.sem, s_w_used.after(("upx", 0, e), 0))
                if e >= 2:
                    dve.wait_ge(s_hu_lo.sem, s_hu_lo.after(e - 2))
                dve.tensor_tensor(huv, ps[5][:, :], sgv, ALU.mult).then_inc(s_hu.sem, s_hu.event(e))
                if e:
                    split_lo(dve, n + 3)
                dve.wait_ge(s_hu_hi.sem, s_hu_hi.after(e))
                if e >= 2:
                    dve.wait_ge(s_w_used.sem, s_w_used.after(("dn", 0, e - 2), 0))
                dve.tensor_tensor(hul[:, s, :], huv, huh[:, s, :].bitcast(F32), ALU.subtract).then_inc(s_hu_lo.sem, s_hu_lo.event(e))
            dve.wait_ge(s_w_used.sem, s_w_used.after(("dn", 0, NEXP - 1), 0))
            for k in range(KT):
                dve.tensor_copy(XN[:, k, 0:T2], ps[k // 2][:, T2 * (k % 2):T2 * (k % 2) + T2]).then_inc(s_y.sem, s_y.event(k))
            dve.wait_ge(s_y.sem, s_y.after(KT - 1))
            post_norm(("n6",), 3, "q")
            for t in range(2):
                for h in range(2):
                    dve.wait_ge(s_out_turned.sem, s_out_turned.after(t, h))
                    dve.tensor_copy(OB[:, t, 512 * h:512 * h + 512], ps[2 * t + h][:, :]).then_inc(s_turned_back.sem, s_turned_back.event(t, h))

        @block.tensor
        def _(pe):
            pe.wait_ge(s_consts.sem, s_consts.after("ident"))
            pe.wait_ge(s_x, 48)
            for k in range(KT):
                if k >= 4:
                    pe.wait_ge(s_xt.sem, s_xt.after(("x0",), k - 4))
                for t, (a, w) in enumerate(TOK):
                    o = pe.transpose(ps[1 + k % 4][:, a:a + w], xs[0:w, t, k * P:k * P + P], ident[0:w, 0:w])
                o.then_inc(s_x_turned.sem, s_x_turned.event(k))
                if k:
                    stat_average(pe, ("n1", 0), k - 1)
            stat_average(pe, ("n1", 0), KT - 1)
            pe.wait_ge(s_prm, PRM_ALL)
            for b in range(RBLK):
                k = min(P, NROWS - b * P)
                o = pe.transpose(ps[0][:, b * P:b * P + k], prm[0:k, b, :], ident[0:k, 0:k])
            o.then_inc(s_prm_turned.sem, s_prm_turned.event())
            pe.wait_ge(s_consts.sem, s_consts.after("first"))
            for l in range(DEPTH):
                key = ("n1", l)
                for i, (name, h) in enumerate(IN_ORDER):
                    gemm(pe, ("in", l, i), key, T, tokens=name in ("gk", "gv", "fv"))
                    if i == 0:
                        if l == 0:
                            pe.wait_ge(s_small, SMALL_ALL)
                        pe.wait_ge(s_logged.sem, s_logged.after(key))
                        for k in range(KT):
                            o = pe.matmul(ps[7][0:8, 64:64 + T], wsm[:, l, k, 16:24], XN[:, k, :], start=(k == 0), stop=(k == KT - 1))
                        o.then_inc(s_small_ff.sem, s_small_ff.event(l))
                        for k in range(KT):
                            o = pe.matmul(ps[6][0:16, 0:T], wsm[:, l, k, 0:16], XN[:, k, :], start=(k == 0), stop=(k == KT - 1))
                        o.then_inc(s_small_glr.sem, s_small_glr.event(l))
                        if l == 0:
                            pe.wait_ge(s_glr.sem, s_glr.after(l))
                            pe.matmul(ps[6][:, 0:44], ones_1[0:1, :], rows44[0:1, :], start=True, stop=True).then_inc(s_bc.sem, s_bc.event())
                    if i == 1:
                        pe.wait_ge(s_glr.sem, s_glr.after(l))
                        pe.wait_ge(s_fz.sem, s_fz.after(l))
                        if l == 0:
                            pe.wait_ge(s_bc44.sem, s_bc44.after())
                        A_, B_, M_ = slice(META, META + P), slice(META + P, T), slice(0, META)
                        pe.matmul(ps[6][:, 0:256], glr1[:, A_], wa1[:, l, :], start=True, stop=True)
                        pe.matmul(ps[6][:, 256:512], glr1[:, B_], wa1[:, l, :], start=True, stop=True)
                        pe.matmul(ps[7][0:META, 64:320], glr1[:, M_], wa1[:, l, :], start=True, stop=True).then_inc(s_z.sem, s_z.event(l))
                    if i == 2:
                        pe.wait_ge(s_la.sem, s_la.after(l))
                        pe.matmul(ps[6][:, 0:256], after[:, :], la[:, 1, :], start=True, stop=True)
                        pe.matmul(ps[6][:, 256:512], after[:, :], la[:, 2, :], start=True, stop=True)
                        pe.matmul(ps[7][0:META, 64:320], after[0:META, 0:META], la[0:META, 0, :], start=True, stop=True)
                        for p in range(2):
                            for t in range(2):
                                c = 340 + p * 4 + 2 * t
                                o = pe.matmul(ps[7][:, c:c + 2], la[:, 1 + t, p * P:p * P + P], half[:, :], start=True, stop=True)
                        o.then_inc(s_gla_d.sem, s_gla_d.event(l))
                    if i in ADA_IN:
                        pe.wait_ge(s_gla_e.sem, s_gla_e.after(l))
                        mod_columns(pe, ada_no(l, "in", i))
                for i in (9, 10, 11):
                    g = ("in", l, i)
                    drained(pe, g)
                pe.wait_ge(s_kd.sem, s_kd.after(l))
                for c, (t, r0_, rn) in enumerate(GLA_CHUNKS):
                    for p in range(2):
                        for hh in range(2):
                            rows = slice(r0_, r0_ + rn)
                            c0 = p * P if c == 0 else ((c - 1) // 2) * 256 + p * P
                            bank = ps[4] if c == 0 else ps[(c - 1) % 2]
                            o = pe.matmul(bank[64 * hh:64 * hh + 64, c0:c0 + P], kd[rows, t, p * P + 64 * hh:p * P + 64 * hh + 64],
                                          gvt[rows, t, (2 * p + hh) * P:(2 * p + hh + 1) * P], start=True, stop=True)
                o.then_inc(s_gla_u.sem, s_gla_u.event(l))
                for h in range(4):
                    p, hb = h // 2, 64 * (h % 2)
                    for c, (t, r0_, rn) in enumerate(GLA_CHUNKS):
                        pe.wait_ge(s_state.sem, s_state.after(l, c, p))
                        q0 = TOK[t][0] + r0_
                        o = pe.matmul(ps[GLA_BANK[h]][:, q0:q0 + rn], ST[hb:hb + 64, p, c, :], gqT[hb:hb + 64, p, q0:q0 + rn],
                                      start=True, stop=True)
                    o.then_inc(s_gla_o.sem, s_gla_o.event(l, h))
                for h in range(4):
                    stat_average(pe, ("g", l, h), 0)
                pe.wait_ge(s_negc.sem, s_negc.after(l))
                for s in range(FOX_H + 4):
                    if s < FOX_H:
                        h, p, hb = s, s // 2, 64 * (s % 2)
                        for q, (q0, qn) in enumerate(TOK):
                            b = ps[FOX_BANK[q]]
                            if s == 0:
                                pe.wait_ge(s_state.sem, s_state.after(l, 4, 1))
                            else:
                                pe.wait_ge(s_pexp.sem, s_pexp.after(l, s - 1, q))
                            end = q0 + qn
                            pe.matmul(b[0:qn, 0:end], fqT[hb:hb + 64, p, q0:end], fkT[hb:hb + 64, p, 0:end], start=True, stop=False)
                            pe.matmul(b[0:qn, 0:end], ident[0:8, h:h + 1].broadcast_to([8, qn]), negc[:, 0:end], start=False, stop=False)
                            o = pe.matmul(b[0:qn, q0:end], identb[0:qn, 0:qn], causal[0:qn, 0:qn], start=False, stop=True)
                            o.then_inc(s_scores.sem, s_scores.event(l, s, q))
                    if 1 <= s <= FOX_H:
                        h = s - 1
                        if h < 2:
                            for j in range(4):
                                pe.wait_ge(s_mixed.sem, s_mixed.after(l, j))
                        else:
                            pe.wait_ge(s_pt_copied.sem, s_pt_copied.after(l, h - 2))
                        if h >= 1:
                            pe.wait_ge(s_ptm_copied.sem, s_ptm_copied.after(l, h - 1))
                        for q in range(3):
                            pe.wait_ge(s_prob.sem, s_prob.after(l, h, q))
                        b, m_ = ps[2 + h % 2], ps[5]
                        pr = Pq[:, h % 2, :, :]
                        pe.transpose(b[:, 0:P], pr[:, 1, META:META + P], ident[:, :])
                        pe.transpose(b[:, P:2 * P], pr[:, 2, META:META + P], ident[:, :])
                        pe.transpose(b[:, 2 * P:3 * P], pr[:, 2, META + P:T], ident[:, :])
                        pe.transpose(m_[0:META, 0:META], pr[0:META, 0, 0:META], ident[0:META, 0:META])
                        pe.transpose(m_[0:META, META:META + P], pr[:, 1, 0:META], ident[:, :])
                        pe.transpose(m_[0:META, META + P:T], pr[:, 2, 0:META], ident[:, :]).then_inc(s_turned.sem, s_turned.event(l, h))
                    if 2 <= s <= FOX_H + 1:
                        h = s - 2
                        j, hb = h // 2, 64 * (h % 2)
                        if h % 2 == 0:
                            if j:
                                pe.wait_ge(s_fox_o.sem, s_fox_o.after(l, j - 1))
                        pe.wait_ge(s_pt_copied.sem, s_pt_copied.after(l, h))
                        pe.wait_ge(s_ptm_copied.sem, s_ptm_copied.after(l, h))
                        d = ps[6][hb:hb + 64, :]
                        cs = slice(64 * h, 64 * h + 64)
                        pe.matmul(d[:, 0:T], fvt[0:META, 0, cs], PTm[:, h % 2, :], start=True, stop=False)
                        pe.matmul(d[:, META:T], fvt[:, 1, cs], PTs[:, h % 2, 0:2 * P], start=False, stop=False)
                        pe.matmul(d[:, META + P:T], fvt[:, 2, cs], PTs[:, h % 2, 2 * P:3 * P], start=False, stop=True).then_inc(s_pv.sem, s_pv.event(l, h))
                    if s >= 4 and (s - 4) % 2 == 0 and (s - 4) // 2 < 4:
                        stat_average(pe, ("f", l, (s - 4) // 2), 0)
                for i in range(4):
                    if i == 0:
                        pe.wait_ge(s_x_lo.sem, s_x_lo.after(("mix", l), 3))
                    gemm(pe, ("out", l, i), ("mix", l), T)
                    if i:
                        for t in range(2):
                            stat_average(pe, ("n2", l), 2 * i - 2 + t)
                for t in range(2):
                    stat_average(pe, ("n2", l), 6 + t)
                for i in range(FT):
                    gemm(pe, ("up", l, i), ("n2", l), T, c0=UP_FROM[l])
                    if i in ADA_UP:
                        mod_columns(pe, ada_no(l, "up", i))
                key = ("n1", l + 1) if l + 1 < DEPTH else ("nf",)
                for i in range(4):
                    gemm(pe, ("down", l, i), None, T, c0=DOWN_FROM[l])
                    if i:
                        for t in range(2):
                            stat_average(pe, key, 2 * i - 2 + t)
                            if l == DEPTH - 1:
                                stat_average(pe, ("n3",), 2 * i - 2 + t)
                for t in range(2):
                    stat_average(pe, key, 6 + t)
                    if l == DEPTH - 1:
                        stat_average(pe, ("n3",), 6 + t)
            for i, (name, h) in enumerate(IN2_ORDER):
                gemm(pe, ("in2", 0, i), ("n3",), T2, tokens=name == "ih")
            for i in (8, 9, 10):
                g = ("in2", 0, i)
                drained(pe, g)
            pe.wait_ge(s_consts.sem, s_consts.after("second"))
            pe.wait_ge(s_ke.sem, s_ke.after())
            for t in range(2):
                for h in range(HG_H):
                    o = pe.transpose(ps[t][:, P * h:P * h + P], keT[:, h, P * t:P * t + P], ident[:, :])
                o.then_inc(s_ke_turned.sem, s_ke_turned.event(t))
                for h in range(HG_H):
                    tok = slice(P * t, P * t + P)
                    o = pe.matmul(ps[2 + t][:, P * h:P * h + P], kdT[:, h, tok], qh[:, h, tok], start=True, stop=True)
                o.then_inc(s_intra.sem, s_intra.event(t))

            def increments(t, n):
                for r_ in range(n):
                    for h in range(HG_H):
                        rows = slice(32 * r_, 32 * r_ + 32)
                        o = pe.matmul(ps[(4 if t == 0 else 0) + r_][:, P * h:P * h + P], ke[rows, t, h, :],
                                      ih[rows, t, P * h:P * h + P], start=True, stop=True)
                o.then_inc(s_hg_u.sem, s_hg_u.event(t))

            pe.wait_ge(s_ke_copied.sem, s_ke_copied.after(0))
            pe.wait_ge(s_logged.sem, s_logged.after(("n3",)))
            increments(0, 4)
            for t in range(2):
                pe.wait_ge(s_ke_copied.sem, s_ke_copied.after(t))
            for t in range(2):
                o = pe.transpose(ps[0][:, P * t:P * t + P], vaT[:, P * t:P * t + P], ident[:, :])
            o.then_inc(s_va_turned.sem, s_va_turned.event())
            pe.wait_ge(s_va.sem, s_va.after())
            pe.wait_ge(s_a_copied.sem, s_a_copied.after(1))
            increments(1, 3)
            pe.wait_ge(s_hg_s.sem, s_hg_s.after(3))
            for h in range(HG_H):
                b = ps[HG_BANK[h]]
                for t in range(2):
                    a = P * t
                    pe.matmul(b[:, a:a + P], ih[:, t, P * h:P * h + P], At[:, t, h, :], start=True, stop=False,
                              skip_group_check=True)
                    for c in range(4 * t, 4 * t + 4):
                        if c == 0:
                            continue
                        pe.wait_ge(s_hg_s.sem, s_hg_s.after(c - 1))
                        q0 = c * HG_C
                        o = pe.matmul(b[:, q0:q0 + HG_C], SS[:, c - 1, h, :], qh[:, h, q0:q0 + HG_C], start=False,
                                      stop=(c == 4 * t + 3), skip_group_check=True)
                o.then_inc(s_hg_o.sem, s_hg_o.event(h))
            for h in range(HG_H):
                stat_average(pe, ("h", h), 0)
            pe.wait_ge(s_hg_s.sem, s_hg_s.after(6))
            for s in range(ATT_H + 3):
                if s < ATT_H:
                    h = HEADS[s]
                    j, g_ = h % 4, h // 4
                    hb = 64 * g_
                    for q in range(2):
                        if s >= 2:
                            pe.wait_ge(s_pexp2.sem, s_pexp2.after(s - 2, q))
                        elif s == 1:
                            pe.wait_ge(s_mixed2.sem, s_mixed2.after(7))
                        b = ps[2 * (s % 2) + q][:, 0:P * (q + 1)]
                        pe.matmul(b, qaT[hb:hb + 64, j, P * q:P * q + P], kaT[hb:hb + 64, 0:P * (q + 1)], start=True, stop=False)
                        o = pe.matmul(b, slope_i[:, h, :], dist[:, P * (1 - q):2 * P], start=False, stop=True)
                        o.then_inc(s_scores2.sem, s_scores2.event(s, q))
                if 1 <= s <= ATT_H:
                    n = s - 1
                    if n >= 2:
                        pe.wait_ge(s_pt2.sem, s_pt2.after(n - 2))
                    else:
                        for h in range(HG_H):
                            pe.wait_ge(s_mixed2.sem, s_mixed2.after(4 + h))
                    for q in range(2):
                        pe.wait_ge(s_prob2.sem, s_prob2.after(n, q))
                    b = ps[4 + n % 2]
                    for t in range(3):
                        o = pe.transpose(b[:, P * t:P * t + P], P2[:, n % 2, P * t:P * t + P], ident[:, :])
                    o.then_inc(s_turned2.sem, s_turned2.event(n))
                if 2 <= s <= ATT_H + 1:
                    n = s - 2
                    g_ = HEADS[n] // 4
                    if n % 2 == 0 and n:
                        pe.wait_ge(s_att_o.sem, s_att_o.after(n // 2 - 1))
                    pe.wait_ge(s_pt2.sem, s_pt2.after(n))
                    d = ps[6][64 * g_:64 * g_ + 64, :]
                    pe.matmul(d[:, 0:T2], va[:, 0, 64 * g_:64 * g_ + 64], PT2[:, n % 2, 0:2 * P], start=True, stop=False)
                    pe.matmul(d[:, P:T2], va[:, 1, 64 * g_:64 * g_ + 64], PT2[:, n % 2, 2 * P:3 * P],
                                             start=False, stop=True).then_inc(s_pv2.sem, s_pv2.event(n))
            for j in range(4):
                stat_average(pe, ("att",), j)
            pe.wait_ge(s_x_lo.sem, s_x_lo.after(("mix2",), 3))
            for i in range(4):
                gemm(pe, ("out2", 0, i), ("mix2",), T2)
                if i:
                    for t in range(2):
                        stat_average(pe, ("n4",), 2 * i - 2 + t)
            for t in range(2):
                stat_average(pe, ("n4",), 6 + t)
            for k in range(KT):
                stat_average(pe, ("n5",), k)
            def down(e):
                n = CHUNK_NO[(("dn", 0, e), 0)]
                pe.wait_ge(s_w_lo.sem, s_w_lo.after(CHUNKS[n]))
                pe.wait_ge(s_hu_lo.sem, s_hu_lo.after(e))
                fl = lambda t: t[:, :, :].rearrange("p a b -> p (a b)").rearrange("p (k n) -> p k n", k=2)
                h, lo = fl(whi[SLOT[n]]), fl(wlo[SLOT[n]])
                for mt in range(KT):
                    for k in range(2):
                        d = ps[mt // 2][:, T2 * (mt % 2):T2 * (mt % 2) + T2]
                        c = slice(P * mt, P * mt + P)
                        x = slice(T2 * k, T2 * k + T2)
                        mm = product(pe, d, h[:, k, c], lo[:, k, c], huh[:, e % 2, x], hul[:, e % 2, x],
                                     e == 0 and k == 0 and mt % 2 == 0, e == NEXP - 1 and k == 1, skip_group_check=True)
                mm.then_inc(s_w_used.sem, s_w_used.event(CHUNKS[n]))

            def widen(kind, e, b):
                n = CHUNK_NO[((kind, 0, e), 0)]
                pe.wait_ge(s_w_lo.sem, s_w_lo.after(CHUNKS[n]))
                h, lo = whi[SLOT[n]], wlo[SLOT[n]]
                for mt in range(2):
                    for k in range(KT):
                        if kind == "gate" and e == 0 and mt == 0:
                            pe.wait_ge(s_x_lo.sem, s_x_lo.after(("n5",), k))
                        c = slice(P * mt, P * mt + P)
                        mm = product(pe, b[:, T2 * mt:T2 * mt + T2], h[:, k, c], lo[:, k, c], xhi[:, k, 0:T2], xlo[:, k, 0:T2],
                                     k == 0, k == KT - 1)
                mm.then_inc(s_w_used.sem, s_w_used.event(CHUNKS[n]))

            def route():
                pe.wait_ge(s_shifted.sem, s_shifted.after(KT - 1))
                for t in range(2):
                    d = ps[0][:, 64 * t:64 * t + 36]
                    for k in range(KT):
                        pe.matmul(d, XN[:, k, P * t:P * t + P], wr[:, k, :], start=(k == 0), stop=False)
                    o = pe.matmul(d, ones_1[0:1, :], rows44[0:1, 0:36], start=False, stop=True)
                o.then_inc(s_routed.sem, s_routed.event())

            pe.wait_ge(s_logged.sem, s_logged.after(("n5",)))
            for i in range(4):
                drained(pe, ("out2", 0, i))

            def weigh(e):
                if e >= 2:
                    pe.wait_ge(s_sgw.sem, s_sgw.after(e - 2))
                one = identr[:, e:e + 1].broadcast_to([NEXP, P])
                pe.matmul(ps[6 + e % 2][:, 0:T2], one, WTh[:, :], start=True, stop=False)
                pe.matmul(ps[6 + e % 2][:, 0:T2], one, WTl[:, :], start=False, stop=True).then_inc(s_weighed.sem, s_weighed.event(e))

            for e in range(NEXP + 1):
                if e == 0:
                    widen("gate", e, ps[4])
                    route()
                    widen("upx", e, ps[5])
                elif e < NEXP:
                    if e > 1:
                        weigh(e)
                    pe.wait_ge(s_e_gate.sem, s_e_gate.after(e - 1))
                    widen("gate", e, ps[4])
                if e == 1:
                    for t in range(2):
                        pe.wait_ge(s_wt.sem, s_wt.after(t))
                        o = pe.transpose(ps[1][0:NEXP, P * t:P * t + P], wt[:, t, :], ident[:, :])
                    o.then_inc(s_wt_turned.sem, s_wt_turned.event())
                    pe.wait_ge(s_wt_lo.sem, s_wt_lo.after())
                    weigh(0)
                    weigh(1)
                if e:
                    down(e - 1)
                if 0 < e < NEXP:
                    pe.wait_ge(s_hu.sem, s_hu.after(e - 1))
                    widen("upx", e, ps[5])
            for k in range(KT):
                stat_average(pe, ("n6",), k)
            for t in range(2):
                for h in range(2):
                    for j in range(4):
                        k = 4 * h + j
                        pe.wait_ge(s_xt.sem, s_xt.after(("q",), k))
                        o = pe.transpose(ps[2 * t + h][:, P * j:P * j + P], XT[:, k, META + P * t:META + P * t + P], ident[:, :])
                    o.then_inc(s_out_turned.sem, s_out_turned.event(t, h))
    return orders


_INS = ["x", "meta_tokens", "attn_norm", "w_in", "w_alpha_up", "b_alpha", "b_forget", "gla_norm", "fox_norm", "w_out",
        "ffn_norm", "w_up", "conv_w", "conv_b", "w_down", "final_norm", "c_2", "ln1_pre_2", "ln1_post_2", "ln2_pre_2",
        "ln2_post_2", "w_ada_2", "b_ada_2", "w_in_2", "attn_sinks_2", "attn_out_norm_2", "hgrn_lb_2",
        "hgrn_out_norm_2", "w_out_2", "w_router_group_2", "b_router_group_2", "w_router_expert_2", "b_router_expert_2",
        "w_exp_gate_2", "w_exp_up_2", "w_exp_down_2"]


def kernel(**inputs):
    import numpy as _np
    import concourse.bacc as _bacc
    from concourse import mybir as _mybir
    from concourse.bass_utils import run_bass_kernel_spmd as _run

    arrays = {f"in_{n}": _np.ascontiguousarray(inputs[n]) for n in _INS}

    def program(known):
        nc = _bacc.Bacc("TRN2", target_bir_lowering=False, num_devices=1)
        args = {n: nc.dram_tensor(f"in_{n}", arrays[f"in_{n}"].shape, _mybir.dt.from_np(arrays[f"in_{n}"].dtype),
                                  kind="ExternalInput").ap() for n in _INS}
        out = nc.dram_tensor("out_0", (1, T2, D), _mybir.dt.float32, kind="ExternalOutput").ap()
        return nc, build(nc, args, out, known)

    _, order = program(None)
    nc, _ = program(order)
    r = _run(nc, [arrays], core_ids=[0])
    return r.results[0]["out_0"]
```
